# Optimizing a Trainium2 kernel written in Bass

```python
import jax, jax.numpy as jnp
from jax import lax
import numpy as np

D_MODEL = 1024
BATCH = 1
SEQ = 1024
DEPTH = 1
DEC_BATCH = 1
DEC_SEQ = 2048
PAST_LEN = 128

N_META = 16
GRID_W = 64
Q_BLOCK = 128
ROPE_THETA = 10000.0
NORM_EPS = 1e-6

GQA_HEADS = 8
GQA_KV_HEADS = 2
GQA_HEAD_DIM = 64
GQA_WIDTH = GQA_HEADS * GQA_HEAD_DIM

MLA_HEADS = 8
MLA_Q_RANK = 256
MLA_KV_RANK = 128
MLA_NOPE_DIM = 64
MLA_ROPE_DIM = 32
MLA_V_DIM = 64
MLA_QK_DIM = MLA_NOPE_DIM + MLA_ROPE_DIM
MLA_WIDTH = MLA_HEADS * MLA_V_DIM

D_MIX = GQA_WIDTH + MLA_WIDTH

IN_SPLITS = (GQA_HEADS * GQA_HEAD_DIM,
             GQA_KV_HEADS * GQA_HEAD_DIM,
             GQA_KV_HEADS * GQA_HEAD_DIM,
             MLA_Q_RANK,
             MLA_KV_RANK,
             MLA_ROPE_DIM)
D_IN = 512 + 128 + 128 + 256 + 128 + 32
IN_SPLIT_POINTS = (512, 640, 768, 1024, 1152)

N_GROUPS = 4
EXPERTS_PER_GROUP = 8
N_EXPERTS = N_GROUPS * EXPERTS_PER_GROUP
TOP_K = 2
D_EXPERT = 256
MOE_BLOCK = 128

kernel_name = "hymba_gqa_mla_hier_moe_encoder"

def rms_norm(x, g):
    xf = x.astype(jnp.float32)
    y = xf * lax.rsqrt(jnp.mean(xf * xf, axis=-1, keepdims=True) + NORM_EPS)
    return (y * g.astype(jnp.float32)).astype(x.dtype)

def axial_angles(rows, cols, rot_dim):
    half = rot_dim // 2
    inv = ROPE_THETA ** (-jnp.arange(0, half, 2, dtype=jnp.float32) / half)
    ang = jnp.concatenate([rows.astype(jnp.float32)[:, None] * inv,
                           cols.astype(jnp.float32)[:, None] * inv], axis=-1)
    return jnp.cos(ang), jnp.sin(ang)

def apply_rope(x, cos, sin):
    xf = x.astype(jnp.float32).reshape(x.shape[:-1] + (x.shape[-1] // 2, 2))
    x0, x1 = xf[..., 0], xf[..., 1]
    c, s = cos[None, :, None, :], sin[None, :, None, :]
    out = jnp.stack([x0 * c - x1 * s, x0 * s + x1 * c], axis=-1)
    return out.reshape(x.shape).astype(x.dtype)

def _attend_queries(q, k, v, scale):
    s = jnp.einsum('bqhgd,bkhd->bhgqk', q, k, preferred_element_type=jnp.float32) * scale
    p = jax.nn.softmax(s, axis=-1).astype(v.dtype)
    return jnp.einsum('bhgqk,bkhe->bqhge', p, v)

def bidirectional_attention(q, k, v, scale):
    B, L, H, Dk = q.shape
    Hkv = k.shape[2]
    G = H // Hkv
    qg = q.reshape(B, L, Hkv, G, Dk)
    o_meta = _attend_queries(qg[:, :N_META], k, v, scale)
    n_blk = (L - N_META) // Q_BLOCK
    q_blk = qg[:, N_META:].reshape(B, n_blk, Q_BLOCK, Hkv, G, Dk).transpose(1, 0, 2, 3, 4, 5)
    o_blk = lax.map(lambda qb: _attend_queries(qb, k, v, scale), q_blk)
    o_real = o_blk.transpose(1, 0, 2, 3, 4, 5).reshape(B, L - N_META, Hkv, G, -1)
    return jnp.concatenate([o_meta, o_real], axis=1).reshape(B, L, H, -1)

def parallel_mixer(h, cos_g, sin_g, cos_m, sin_m, norm_mix_g, w_in, gqa_q_norm_g, gqa_k_norm_g,
                   mla_q_norm_g, mla_kv_norm_g, w_mla_q_up, w_mla_kv_up,
                   gqa_out_norm_g, mla_out_norm_g, w_out):
    B, L, _ = h.shape
    u = rms_norm(h, norm_mix_g)
    z = u @ w_in
    q_a, k_a, v_a, c_q, c_kv, k_r = jnp.split(z, list(IN_SPLIT_POINTS), axis=-1)

    q_a = apply_rope(rms_norm(q_a.reshape(B, L, GQA_HEADS, GQA_HEAD_DIM), gqa_q_norm_g), cos_g, sin_g)
    k_a = apply_rope(rms_norm(k_a.reshape(B, L, GQA_KV_HEADS, GQA_HEAD_DIM), gqa_k_norm_g), cos_g, sin_g)
    v_a = v_a.reshape(B, L, GQA_KV_HEADS, GQA_HEAD_DIM)
    o_a = bidirectional_attention(q_a, k_a, v_a, GQA_HEAD_DIM ** -0.5).reshape(B, L, GQA_WIDTH)

    q_b = (rms_norm(c_q, mla_q_norm_g) @ w_mla_q_up).reshape(B, L, MLA_HEADS, MLA_QK_DIM)
    q_nope, q_rope = q_b[..., :MLA_NOPE_DIM], q_b[..., MLA_NOPE_DIM:]
    q_rope = apply_rope(q_rope, cos_m, sin_m)
    kv = (rms_norm(c_kv, mla_kv_norm_g) @ w_mla_kv_up).reshape(B, L, MLA_HEADS, MLA_NOPE_DIM + MLA_V_DIM)
    k_nope, v_b = kv[..., :MLA_NOPE_DIM], kv[..., MLA_NOPE_DIM:]
    k_rope = apply_rope(k_r[:, :, None, :], cos_m, sin_m)
    q_full = jnp.concatenate([q_nope, q_rope], axis=-1)
    k_full = jnp.concatenate([k_nope, jnp.broadcast_to(k_rope, (B, L, MLA_HEADS, MLA_ROPE_DIM))], axis=-1)
    o_b = bidirectional_attention(q_full, k_full, v_b, MLA_QK_DIM ** -0.5).reshape(B, L, MLA_WIDTH)

    o = jnp.concatenate([rms_norm(o_a, gqa_out_norm_g), rms_norm(o_b, mla_out_norm_g)], axis=-1)
    return o @ w_out

def hierarchical_moe(u, w_rg, b_rg, w_re, b_re, w_gate, w_up, w_down):
    B, L, D = u.shape
    x = u.reshape(-1, D)
    T = x.shape[0]
    lg = (x @ w_rg).astype(jnp.float32) + b_rg.astype(jnp.float32)
    pg = jax.nn.softmax(lg, axis=-1)
    p_grp, grp = lax.top_k(pg, 1)
    le = ((x @ w_re).astype(jnp.float32) + b_re.astype(jnp.float32)).reshape(T, N_GROUPS, EXPERTS_PER_GROUP)
    le_sel = jnp.take_along_axis(le, grp[:, :, None], axis=1)[:, 0]
    top_p, top_i = lax.top_k(jax.nn.softmax(le_sel, axis=-1), TOP_K)
    gates = p_grp * (top_p / jnp.sum(top_p, axis=-1, keepdims=True))
    expert_id = grp * EXPERTS_PER_GROUP + top_i

    A = T * TOP_K
    e_flat = expert_id.reshape(-1)
    tok_flat = jnp.repeat(jnp.arange(T, dtype=jnp.int32), TOP_K)
    g_flat = gates.reshape(-1)
    order = jnp.argsort(e_flat)
    e_sorted = e_flat[order]
    counts = jnp.bincount(e_flat, length=N_EXPERTS)
    starts = jnp.cumsum(counts) - counts
    padded = (counts + MOE_BLOCK - 1) // MOE_BLOCK * MOE_BLOCK
    pends = jnp.cumsum(padded)
    pstarts = pends - padded
    slot = pstarts[e_sorted] + jnp.arange(A, dtype=counts.dtype) - starts[e_sorted]
    n_blocks = (A + N_EXPERTS * (MOE_BLOCK - 1) + MOE_BLOCK - 1) // MOE_BLOCK
    P = n_blocks * MOE_BLOCK
    buf_tok = jnp.zeros((P,), jnp.int32).at[slot].set(tok_flat[order])
    buf_gate = jnp.zeros((P,), jnp.float32).at[slot].set(g_flat[order])
    block_expert = jnp.minimum(
        jnp.searchsorted(pends, jnp.arange(n_blocks, dtype=pends.dtype) * MOE_BLOCK, side='right'),
        N_EXPERTS - 1)

    def run_block(args):
        tok, e = args
        xe = x[tok]
        hid = jax.nn.silu(xe @ w_gate[e]) * (xe @ w_up[e])
        return hid @ w_down[e]

    yb = lax.map(run_block, (buf_tok.reshape(n_blocks, MOE_BLOCK), block_expert))
    y = jnp.zeros((T, D), jnp.float32).at[buf_tok].add(yb.reshape(P, D).astype(jnp.float32) * buf_gate[:, None])
    return y.astype(u.dtype).reshape(B, L, D)

def encoder_trunk(x, meta_tokens, norm_mix_g, w_in, gqa_q_norm_g, gqa_k_norm_g, mla_q_norm_g,
                  mla_kv_norm_g, w_mla_q_up, w_mla_kv_up, gqa_out_norm_g, mla_out_norm_g, w_out,
                  norm_ffn_g, w_router_group, b_router_group, w_router_expert, b_router_expert,
                  w_expert_gate, w_expert_up, w_expert_down, norm_final_g):
    B, n, D = x.shape
    rows_count = n // GRID_W
    rows = jnp.concatenate([jnp.full((N_META,), -1, jnp.int32),
                            jnp.repeat(jnp.arange(rows_count, dtype=jnp.int32), GRID_W)])
    cols = jnp.concatenate([jnp.arange(N_META, dtype=jnp.int32),
                            jnp.tile(jnp.arange(GRID_W, dtype=jnp.int32), rows_count)])
    cos_g, sin_g = axial_angles(rows, cols, GQA_HEAD_DIM)
    cos_m, sin_m = axial_angles(rows, cols, MLA_ROPE_DIM)

    h = jnp.concatenate([jnp.broadcast_to(meta_tokens.astype(x.dtype)[None], (B, N_META, D)), x], axis=1)
    for l in range(DEPTH):
        h = h + parallel_mixer(h, cos_g, sin_g, cos_m, sin_m, norm_mix_g[l], w_in[l],
                               gqa_q_norm_g[l], gqa_k_norm_g[l], mla_q_norm_g[l], mla_kv_norm_g[l],
                               w_mla_q_up[l], w_mla_kv_up[l], gqa_out_norm_g[l], mla_out_norm_g[l], w_out[l])
        h = h + hierarchical_moe(rms_norm(h, norm_ffn_g[l]), w_router_group[l], b_router_group[l],
                                 w_router_expert[l], b_router_expert[l],
                                 w_expert_gate[l], w_expert_up[l], w_expert_down[l])
    h = rms_norm(h, norm_final_g)
    return h[:, N_META:]

def setup_inputs(seed: int = 0) -> dict:
    key = jax.random.key(seed)
    ks = jax.random.split(key, 24)
    f32 = jnp.float32

    def nrm(k, shape, scale):
        return jax.random.normal(k, shape, f32) * scale

    def gain(k, shape):
        return 1.0 + 0.02 * jax.random.normal(k, shape, f32)

    return {
        "x_prompt": jax.random.normal(ks[0], (BATCH, SEQ, D_MODEL), f32),
        "x_sample": jax.random.normal(ks[1], (DEC_BATCH, DEC_SEQ, D_MODEL), f32),
        "meta_tokens": nrm(ks[2], (N_META, D_MODEL), 1.0),
        "norm_mix_g": gain(ks[3], (DEPTH, D_MODEL)),
        "w_in": nrm(ks[4], (DEPTH, D_MODEL, D_IN), D_MODEL ** -0.5),
        "gqa_q_norm_g": gain(ks[5], (DEPTH, GQA_HEAD_DIM)),
        "gqa_k_norm_g": gain(ks[6], (DEPTH, GQA_HEAD_DIM)),
        "mla_q_norm_g": gain(ks[7], (DEPTH, MLA_Q_RANK)),
        "mla_kv_norm_g": gain(ks[8], (DEPTH, MLA_KV_RANK)),
        "w_mla_q_up": nrm(ks[9], (DEPTH, MLA_Q_RANK, MLA_HEADS * MLA_QK_DIM), MLA_Q_RANK ** -0.5),
        "w_mla_kv_up": nrm(ks[10], (DEPTH, MLA_KV_RANK, MLA_HEADS * (MLA_NOPE_DIM + MLA_V_DIM)), MLA_KV_RANK ** -0.5),
        "gqa_out_norm_g": gain(ks[11], (DEPTH, GQA_WIDTH)),
        "mla_out_norm_g": gain(ks[12], (DEPTH, MLA_WIDTH)),
        "w_out": nrm(ks[13], (DEPTH, D_MIX, D_MODEL), D_MIX ** -0.5),
        "norm_ffn_g": gain(ks[14], (DEPTH, D_MODEL)),
        "w_router_group": nrm(ks[15], (DEPTH, D_MODEL, N_GROUPS), D_MODEL ** -0.5),
        "b_router_group": nrm(ks[16], (DEPTH, N_GROUPS), 0.01),
        "w_router_expert": nrm(ks[17], (DEPTH, D_MODEL, N_EXPERTS), D_MODEL ** -0.5),
        "b_router_expert": nrm(ks[18], (DEPTH, N_EXPERTS), 0.01),
        "w_expert_gate": nrm(ks[19], (DEPTH, N_EXPERTS, D_MODEL, D_EXPERT), D_MODEL ** -0.5),
        "w_expert_up": nrm(ks[20], (DEPTH, N_EXPERTS, D_MODEL, D_EXPERT), D_MODEL ** -0.5),
        "w_expert_down": nrm(ks[21], (DEPTH, N_EXPERTS, D_EXPERT, D_MODEL), D_EXPERT ** -0.5),
        "norm_final_g": gain(ks[22], (D_MODEL,)),
    }

def reference(x_prompt, x_sample, meta_tokens, norm_mix_g, w_in, gqa_q_norm_g, gqa_k_norm_g,
              mla_q_norm_g, mla_kv_norm_g, w_mla_q_up, w_mla_kv_up, gqa_out_norm_g, mla_out_norm_g,
              w_out, norm_ffn_g, w_router_group, b_router_group, w_router_expert, b_router_expert,
              w_expert_gate, w_expert_up, w_expert_down, norm_final_g):
    y_prompt = encoder_trunk(x_prompt, meta_tokens, norm_mix_g, w_in, gqa_q_norm_g, gqa_k_norm_g,
                             mla_q_norm_g, mla_kv_norm_g, w_mla_q_up, w_mla_kv_up, gqa_out_norm_g,
                             mla_out_norm_g, w_out, norm_ffn_g, w_router_group, b_router_group,
                             w_router_expert, b_router_expert, w_expert_gate, w_expert_up,
                             w_expert_down, norm_final_g)
    y_sample = encoder_trunk(x_sample, meta_tokens, norm_mix_g, w_in, gqa_q_norm_g, gqa_k_norm_g,
                             mla_q_norm_g, mla_kv_norm_g, w_mla_q_up, w_mla_kv_up, gqa_out_norm_g,
                             mla_out_norm_g, w_out, norm_ffn_g, w_router_group, b_router_group,
                             w_router_expert, b_router_expert, w_expert_gate, w_expert_up,
                             w_expert_down, norm_final_g)
    return (y_prompt, y_sample)


_drawn_inputs = setup_inputs


def setup_inputs(seed=0):
    import zlib

    import numpy as np

    out = dict(_drawn_inputs(seed))
    spreads = {}
    factors = {'gqa_k_norm_g': 2.874,
     'mla_q_norm_g': 2.744,
     'gqa_out_norm_g': 11.186,
     'mla_out_norm_g': 11.378,
     'b_router_group': 33.963,
     'b_router_expert': 21.422,
     'norm_final_g': 7.927,
     'norm_ffn_g': 5.801}
    for name, (base, spread) in spreads.items():
        noise = np.random.default_rng([zlib.crc32(name.encode()), seed]).standard_normal(out[name].shape)
        drawn = base * np.exp(spread * noise) if base else spread * noise
        out[name] = __import__('jax').numpy.asarray(drawn.astype(out[name].dtype))
    for name, factor in factors.items():
        out[name] = (out[name] * factor).astype(out[name].dtype)
    return out
```

```python
import numpy as np
import concourse.bass as bass
from concourse import mybir
from contextlib import ExitStack

F32 = mybir.dt.float32
F32R = mybir.dt.float32r
I32 = mybir.dt.int32
U32 = mybir.dt.uint32
ALU = mybir.AluOpType
ACT = mybir.ActivationFunctionType
AX = mybir.AxisListType

P = 128
D = 1024
KC = D // P
SEQ, DEC_SEQ, META = 1024, 2048, 16
TOK = SEQ + DEC_SEQ
KEYS = TOK + META
TILES = TOK // P
SUP = 4
SUPERS = TILES // SUP
W = SUP * P
EPS = 1e-6

GH, GKV, GD = 8, 2, 64
MH, QR, KVR, ND, RD, VD = 8, 256, 128, 64, 32, 64
QKD = ND + RD
D_IN = 1184
ZQ, ZK, ZV, ZCQ, ZCKV, ZKR = 0, 512, 640, 768, 1024, 1152
GSCALE = GD ** -0.5
MSCALE = QKD ** -0.5
PAIRS = GH // 2
NV = PAIRS + MH
VC = VD + 1

G, EPG, E = 4, 8, 32
DE = 256
BLOCKS = 80
assert (2 * TOK + E * (P - 1)) // P < BLOCKS


def stage_project(nc, t):
    with ExitStack() as ctx:
        def sb(name, shape, dt=F32):
            return ctx.enter_context(nc.sbuf_tensor("a_" + name, shape, dt))

        def ps(name, shape):
            return ctx.enter_context(nc.psum_tensor("a_" + name, shape, F32))

        def sem(name):
            return ctx.enter_context(nc.semaphore("a_" + name))

        w_in = sb("w_in", [P, KC, D_IN])
        w_qup = sb("w_qup", [P, 2, MH * P])
        w_kup = sb("w_kup", [P, MH * ND])
        w_vup = sb("w_vup", [P, MH * VD])
        ident = sb("ident", [P, P])
        g_mix = sb("g_mix", [P, KC])
        g_cq = sb("g_cq", [P, 2])
        g_ckv = sb("g_ckv", [P, 1])
        g_rows = sb("g_rows", [P, 4, GD])
        inv_n = sb("inv_n", [P, 12])
        eps = sb("eps", [P, 1])
        x = sb("x", [P, 2, D])
        tab = sb("tab", [P, 2, 192])
        colc = sb("colc", [P, W])
        junk = sb("junk", [P, D_IN])
        ssq = sb("ssq", [P, 2])
        std = sb("std", [P, 2])
        rstd = sb("rstd", [P, 2])
        xT = sb("xT", [P, KC, P])
        z = sb("z", [P, D_IN])
        sq = sb("sq", [P, D_IN])
        hss = sb("hss", [P, 12])
        hsn = sb("hsn", [P, 12])
        hstd = sb("hstd", [P, 12])
        hr = sb("hr", [P, 12])
        tA = sb("tA", [P, 4, GD])
        qn = sb("qn", [P, 640])
        qs = sb("qs", [P, 640])
        kr_tmp = sb("kr_tmp", [P, 2 * RD])
        trin = sb("trin", [P, 2, 1184])
        qk_hi = sb("qk_hi", [P, 5, W], F32R)
        qk_lo = sb("qk_lo", [P, 5, W], F32R)
        kr_hi = sb("kr_hi", [RD + 1, W], F32R)
        kr_lo = sb("kr_lo", [RD, W], F32R)
        ones_row = sb("ones_row", [1, W], F32R)
        cqT = sb("cqT", [P, 2, W])
        ckvT = sb("ckvT", [P, W])
        mq_hi = sb("mq_hi", [QKD, MH, W], F32R)
        mq_lo = sb("mq_lo", [QKD, MH, W], F32R)
        mk_hi = sb("mk_hi", [P, 4, W], F32R)
        mk_lo = sb("mk_lo", [P, 4, W], F32R)
        rope_s = sb("rope_s", [QKD, W])
        rope_c = sb("rope_c", [QKD, W])
        vst = sb("vst", [P, SUP, NV, VC])

        psX = ps("psX", [P, 2, 512])
        psZ = ps("psZ", [P, 3 * 512])
        psR = ps("psR", [P, 3 * 512])

        setup = sem("setup")
        w_loaded = sem("w_loaded")
        consts = sem("consts")
        x_loaded = [sem("x_loaded0"), sem("x_loaded1")]
        col_loaded = sem("col_loaded")
        std_ready = sem("std_ready")
        rstd_ready = sem("rstd_ready")
        xt_psum = sem("xt_psum")
        xt_ready = sem("xt_ready")
        z_psum = sem("z_psum")
        z_ready = sem("z_ready")
        sq_ready = sem("sq_ready")
        hs_ready = sem("hs_ready")
        hstd_ready = sem("hstd_ready")
        rope_ready = sem("rope_ready")
        tr_psum = sem("tr_psum")
        tr_hi = sem("tr_hi")
        tr_free = sem("tr_free")
        mla_psum = sem("mla_psum")
        mla_a = sem("mla_a")
        mla_d = sem("mla_d")
        stored = sem("stored")
        carrier = sem("carrier")

        QU, KU, VU = MH, MH // 2, SUP
        UN = QU + KU + VU
        STORES = 3 * PAIRS + 9
        LAST = TILES

        block = ctx.enter_context(nc.Block())

        def load_n(g, k):
            return 2 * g + (1 + k) // 2, (1 + k) % 2

        @block.sync
        def _(sp):
            def load(T, n, s):
                sp.dma_start(x[:, s, :], t["xall"][bass.ds(T * P, P), :]).then_inc(x_loaded[s], 16)
                sp.dma_start(tab[:, s, :], t["rope_rows"][bass.ds(T * P, P), :]).then_inc(x_loaded[s], 16)

            def load_cols(S):
                sp.dma_start(colc[64:96, :], t["rope_cols"][0, :, bass.ds(S * W, W)]).then_inc(col_loaded, 16)
                sp.dma_start(colc[96:128, :], t["rope_cols"][1, :, bass.ds(S * W, W)]).then_inc(col_loaded, 16)

            def store(S, lo, n, kcol, qcol):
                c = slice(lo, lo + n)
                kc = bass.ds(kcol, n)
                out = []
                for pair in range(PAIRS):
                    r = slice(GD * (pair // 2), GD * (pair // 2) + GD)
                    out += [(t["KGH"][pair * GD:pair * GD + GD, kc], qk_hi[r, 4, c]),
                            (t["KGL"][pair, 0:GD, kc], qk_lo[r, 4, c]),
                            (t["KGL"][pair, GD:GD + 1, kc], ones_row[0:1, 0:n])]
                out += [(t["KRH"][:, kc], kr_hi[:, c]), (t["KRL"][:, kc], kr_lo[:, c]),
                       (t["KMH"].rearrange("(j p) n -> p j n", p=P)[:, :, kc], mk_hi[:, :, c]),
                       (t["KML"].rearrange("(j p) n -> p j n", p=P)[:, :, kc], mk_lo[:, :, c])]
                if n == W:
                    out.append((t["V"][bass.ds(kcol, W), :].rearrange("(j p) c -> p j c", p=P),
                                vst[:, :, :, :].rearrange("p j h c -> p j (h c)")))
                    qc = bass.ds(qcol, n)
                    out += [(t["QGH"].rearrange("(j p) n -> p j n", p=P)[:, :, qc], qk_hi[:, 0:4, :]),
                            (t["QGL"].rearrange("(j p) n -> p j n", p=P)[:, :, qc], qk_lo[:, 0:4, :]),
                            (t["QMH"].rearrange("(j p) n -> p j n", p=QKD)[:, :, qc], mq_hi[:, :, :]),
                            (t["QML"].rearrange("(j p) n -> p j n", p=QKD)[:, :, qc], mq_lo[:, :, :])]
                else:
                    out.append((t["V"][bass.ds(kcol, n), :],
                                vst[0:n, SUP - 1, :, :].rearrange("p h c -> p (h c)")))
                assert len(out) == (STORES if n == W else STORES - 4)
                for o, i in out:
                    sp.dma_start(o, i.bitcast(F32)).then_inc(stored, 16)

            sp.dma_start(x[:, 0, :], t["xall"][0:P, :]).then_inc(x_loaded[0], 16)
            sp.dma_start(tab[:, 0, :], t["rope_rows"][0:P, :]).then_inc(x_loaded[0], 16)
            sp.dma_start(ident[:, :], t["ident"]).then_inc(setup, 16)
            sp.dma_start(g_mix[:, :], t["g_mix"]).then_inc(setup, 16)
            sp.dma_start(g_cq[:, :], t["g_cq"]).then_inc(setup, 16)
            sp.dma_start(g_ckv[:, :], t["g_ckv"]).then_inc(setup, 16)
            sp.dma_start(g_rows[:, :, :], t["g_rows"]).then_inc(setup, 16)
            sp.dma_start(inv_n[:, :], t["inv_n"]).then_inc(setup, 16)
            w_dram = t["w_in"].rearrange("(p c) n -> p c n", c=KC)
            for c in range(0, KC, 4):
                sp.dma_start(w_in[:, c:c + 4, :], w_dram[:, c:c + 4, :]).then_inc(w_loaded, 16)
            load(1, 0, 1)
            sp.dma_start(w_qup[:, :, :], t["w_qup"].rearrange("(c p) n -> p c n", p=P)).then_inc(w_loaded, 16)
            sp.dma_start(w_kup[:, :], t["w_kup"]).then_inc(w_loaded, 16)
            sp.dma_start(w_vup[:, :], t["w_vup"]).then_inc(w_loaded, 16)
            load_cols(0)

            def slot_free(T):
                sp.wait_ge(xt_psum, T + 1)
                sp.wait_ge(std_ready, T + 1)
                sp.wait_ge(rope_ready, T + 1)

            slot_free(0)
            load(2, 1, 0)

            def body(g, last, first=False):
                for k in range(SUP):
                    T = g * SUP + 1 + k
                    slot_free(T)
                    if not (last and k >= SUP - 2):
                        n, s = load_n(g, k)
                        load(T + 2, n + 1, s)
                    if k == 0:
                        sp.wait_ge(mla_a, (g + 1) * UN)
                        sp.sem_inc(carrier, 1)
                        sp.wait_ge(mla_d, (g + 1) * (QU + KU))
                        if first:
                            store(0, W - P, META, 0, None)
                        else:
                            store(g, 0, W, g * W - W + META, g * W - W)
                        load_cols(g + 1)

            body(0, False, first=True)
            with sp.Fori(1, SUPERS - 1) as g:
                body(g, False)
            body(SUPERS - 1, True)
            sp.wait_ge(mla_a, (SUPERS + 1) * UN)
            sp.wait_ge(mla_d, (SUPERS + 1) * (QU + KU))
            sp.wait_ge(tr_free, 2 * (LAST + 1) + 2)
            store(SUPERS, 0, W, TOK - W + META, TOK - W)
            sp.wait_ge(stored, 16 * (STORES - 4 + STORES * SUPERS))

        @block.scalar
        def _(act):
            def x_stats(T, n, s):
                act.drain()
                act.wait_ge(x_loaded[s], 32 * n + 32)
                nc.scalar.activation(junk[:, 0:D], x[:, s, :], ACT.Square, accum_out=ssq[:, s:s + 1])
                act.drain()
                nc.scalar.activation(std[:, s:s + 1], ssq[:, s:s + 1], ACT.Sqrt, scale=1.0 / D,
                                     bias=eps[:, 0:1]).then_inc(std_ready, 1)

            def z_out(T, s, first=False):
                act.wait_ge(z_psum, T + 1)
                act.wait_ge(rstd_ready, T + 1)
                if not first:
                    act.wait_ge(rope_ready, T)
                nc.scalar.activation(z[:, :], psZ[:, 0:D_IN], ACT.Copy, scale=rstd[:, s:s + 1]).then_inc(z_ready, 1)
                act.drain()
                nc.scalar.activation(sq[:, 0:ZKR], z[:, 0:ZKR], ACT.Square).then_inc(sq_ready, 1)

            def head_std(T):
                act.wait_ge(hs_ready, T + 1)
                nc.scalar.activation(hstd[:, :], hsn[:, :], ACT.Sqrt, bias=eps[:, 0:1]).then_inc(hstd_ready, 1)

            def tr_out(U, k):
                act.wait_ge(tr_psum, U + 1)
                cols = slice(k * P, k * P + P)
                nc.scalar.activation(qk_hi[:, :, cols], psR[:, 0:640].rearrange("p (a n) -> p a n", a=5),
                                     ACT.Copy)
                nc.scalar.activation(kr_hi[0:RD, cols], psR[0:RD, 1024:1152], ACT.Copy).then_inc(tr_hi, 1)

            def mla_out(S):
                for u in range(UN):
                    act.wait_ge(mla_psum, S * UN + u + 1)
                    b = psX[:, u % 2, :]
                    if u < QU:
                        nc.scalar.activation(mq_hi[0:ND, u, :], b[0:ND, :], ACT.Copy, scale=MSCALE).then_inc(mla_a, 1)
                    elif u < QU + KU:
                        nc.scalar.activation(mk_hi[:, u - QU, :], b, ACT.Copy).then_inc(mla_a, 1)
                    else:
                        nc.scalar.activation(vst[:, u - QU - KU, PAIRS:, 0:VD],
                                             b.rearrange("p (h c) -> p h c", c=VD), ACT.Copy).then_inc(mla_a, 1)

            act.wait_ge(consts, 1)
            x_stats(0, 0, 0)
            z_out(0, 0, first=True)
            x_stats(1, 0, 1)
            head_std(0)

            def body(g, last, first=False):
                for k in range(SUP):
                    T = g * SUP + 1 + k
                    n, s = load_n(g, k)
                    z_out(T, s)
                    if not (last and k == SUP - 1):
                        n1, s1 = load_n(g, k + 1)
                        x_stats(T + 1, n1, s1)
                    if k == 1:
                        act.wait_ge(stored, 16 * (STORES - 4 + STORES * g))
                    tr_out(T - 1, (k - 1) % SUP)
                    head_std(T)
                    if k == 0:
                        mla_out(g)

            with act.Fori(0, SUPERS - 1) as g:
                body(g, False)
            body(SUPERS - 1, True)
            tr_out(LAST, SUP - 1)
            mla_out(SUPERS)

        @block.vector
        def _(dve):
            def xt_out(T):
                dve.wait_ge(xt_psum, T + 1)
                nc.vector.tensor_tensor(xT[:, :, :], psX[:, :, :].rearrange("p b (c n) -> p (b c) n", n=P),
                                        g_mix[:, :].unsqueeze(2).broadcast_to([P, KC, P]),
                                        ALU.mult).then_inc(xt_ready, 1)

            def x_rstd(T, s):
                dve.wait_ge(std_ready, T + 1)
                nc.vector.reciprocal(rstd[:, s:s + 1], std[:, s:s + 1]).then_inc(rstd_ready, 1)

            def tr_out(U, k, s):
                dve.wait_ge(tr_psum, U + 1)
                dve.wait_ge(tr_hi, U + 1)
                cols = slice(k * P, k * P + P)
                nc.vector.tensor_tensor(cqT[:, :, cols], psR[:, 640:896].rearrange("p (a n) -> p a n", a=2),
                                        g_cq[:, :].unsqueeze(2).broadcast_to([P, 2, P]), ALU.mult)
                nc.vector.tensor_scalar(ckvT[:, cols], psR[:, 896:1024], g_ckv[:, 0:1], None, ALU.mult)
                for copy in range(2):
                    nc.vector.tensor_copy(vst[:, k, copy:PAIRS:2, 0:VD],
                                          trin[:, s, 1056:1184].rearrange("p (h c) -> p h c", c=VD))
                nc.vector.tensor_tensor(kr_lo[:, cols], psR[0:RD, 1024:1152], kr_hi[0:RD, cols].bitcast(F32),
                                        ALU.subtract)
                nc.vector.tensor_tensor(qk_lo[:, :, cols], psR[:, 0:640].rearrange("p (a n) -> p a n", a=5),
                                        qk_hi[:, :, cols].bitcast(F32), ALU.subtract).then_inc(tr_free, 2)

            def reduce(T, s):
                dve.drain()
                dve.wait_ge(sq_ready, T + 1)
                nc.vector.tensor_reduce(hss[:, 0:10], sq[:, 0:640].rearrange("p (h c) -> p h c", c=GD), AX.X, ALU.add)
                nc.vector.tensor_reduce(hss[:, 10:11], sq[:, ZCQ:ZCKV], AX.X, ALU.add)
                nc.vector.tensor_reduce(hss[:, 11:12], sq[:, ZCKV:ZKR], AX.X, ALU.add)
                dve.drain()
                nc.vector.tensor_tensor(hsn[:, :], hss[:, :], inv_n[:, :], ALU.mult).then_inc(hs_ready, 1)
                for j in range(4):
                    nc.vector.scalar_tensor_tensor(tA[:, j, :], tab[:, s, (j % 2) * GD:(j % 2) * GD + GD],
                                                   GSCALE if j < 2 else 1.0, g_rows[:, j, :], ALU.mult, ALU.mult)

            def rope(T, s):
                dve.wait_ge(hstd_ready, T + 1)
                nc.vector.reciprocal(hr[:, :], hstd[:, :])
                dve.drain()
                heads = z[:, 0:640].rearrange("p (h c) -> p h c", c=GD)
                nc.vector.tensor_tensor(qn[:, :].rearrange("p (h c) -> p h c", c=GD), heads,
                                        hr[:, 0:10].unsqueeze(2).broadcast_to([P, 10, GD]), ALU.mult)
                nc.vector.tensor_scalar(trin[:, s, 640:896], z[:, ZCQ:ZCKV], hr[:, 10:11], None, ALU.mult)
                nc.vector.tensor_scalar(trin[:, s, 896:1024], z[:, ZCKV:ZKR], hr[:, 11:12], None, ALU.mult)
                nc.vector.tensor_copy(trin[:, s, 1056:1184], z[:, ZV:ZCQ])
                dve.drain()
                for lo, n, j in ((0, GH, 0), (512, GKV, 2)):
                    q3 = qn[:, lo:lo + n * GD].rearrange("p (h c) -> p h c", c=GD)
                    q4 = qn[:, lo:lo + n * GD].rearrange("p (h i two) -> p h i two", h=n, two=2)
                    s4 = qs[:, lo:lo + n * GD].rearrange("p (h i two) -> p h i two", h=n, two=2)
                    tb = tA[:, j + 1, :].rearrange("p (i two) -> p i two", two=2)
                    for e in range(2):
                        nc.vector.tensor_tensor(s4[:, :, :, e], q4[:, :, :, 1 - e],
                                                tb[:, :, e].unsqueeze(1).broadcast_to([P, n, GD // 2]), ALU.mult)
                    dst = trin[:, s, lo:lo + n * GD].rearrange("p (h c) -> p h c", c=GD)
                    nc.vector.tensor_tensor(dst, q3, tA[:, j, :].unsqueeze(1).broadcast_to([P, n, GD]), ALU.mult)
                kr = z[:, ZKR:D_IN].rearrange("p (i two) -> p i two", two=2)
                ks = kr_tmp[:, 0:RD].rearrange("p (i two) -> p i two", two=2)
                sn = tab[:, s, 160:192].rearrange("p (i two) -> p i two", two=2)
                for e in range(2):
                    nc.vector.tensor_tensor(ks[:, :, e], kr[:, :, 1 - e], sn[:, :, e], ALU.mult)
                nc.vector.tensor_tensor(kr_tmp[:, RD:2 * RD], z[:, ZKR:D_IN], tab[:, s, 128:160], ALU.mult)
                dve.drain()
                nc.vector.tensor_tensor(trin[:, s, 1024:1056], kr_tmp[:, 0:RD], kr_tmp[:, RD:2 * RD], ALU.add)
                nc.vector.tensor_tensor(trin[:, s, 0:640], trin[:, s, 0:640], qs[:, :], ALU.add).then_inc(rope_ready, 1)

            def mla_out(S):
                for u in range(QU + KU):
                    dve.drain()
                    if u == 0:
                        dve.wait_ge(col_loaded, 32 * S + 32)
                    dve.wait_ge(mla_psum, S * UN + u + 1)
                    dve.wait_ge(mla_a, S * UN + u + 1)
                    b = psX[:, u % 2, :]
                    if u < QU:
                        nc.vector.tensor_tensor(rope_s[ND:QKD, :], b[QKD:P, :], colc[QKD:P, :], ALU.mult)
                        nc.vector.tensor_tensor(rope_c[ND:QKD, :], b[ND:QKD, :], colc[ND:QKD, :], ALU.mult)
                        nc.vector.scalar_tensor_tensor(mq_lo[0:ND, u, :], b[0:ND, :], MSCALE,
                                                       mq_hi[0:ND, u, :].bitcast(F32),
                                                       ALU.mult, ALU.subtract)
                        dve.drain()
                        nc.vector.tensor_tensor(rope_s[ND:QKD, :], rope_s[ND:QKD, :], rope_c[ND:QKD, :], ALU.add)
                        dve.drain()
                        nc.vector.tensor_copy(mq_hi[ND:QKD, u, :], rope_s[ND:QKD, :])
                        dve.drain()
                        nc.vector.tensor_tensor(mq_lo[ND:QKD, u, :], rope_s[ND:QKD, :],
                                                mq_hi[ND:QKD, u, :].bitcast(F32), ALU.subtract).then_inc(mla_d, 1)
                    else:
                        nc.vector.tensor_tensor(mk_lo[:, u - QU, :], b, mk_hi[:, u - QU, :].bitcast(F32),
                                                ALU.subtract).then_inc(mla_d, 1)

            nc.vector.memset(eps[:, :], EPS)
            nc.vector.memset(ones_row[:, :].bitcast(F32), 1.0)
            nc.vector.memset(kr_hi[RD:RD + 1, :].bitcast(F32), 1.0)
            nc.vector.memset(vst[:, :, :, :], 1.0)
            nc.vector.memset(cqT[:, :, :], 0.0)
            nc.vector.memset(ckvT[:, :], 0.0).then_inc(consts, 1)
            dve.drain()
            dve.wait_ge(setup, 16 * 6)
            xt_out(0)
            x_rstd(0, 0)
            xt_out(1)
            x_rstd(1, 1)
            reduce(0, 0)
            rope(0, 0)

            def body(g, last):
                for k in range(SUP):
                    T = g * SUP + 1 + k
                    n, s = load_n(g, k)
                    if not (last and k == SUP - 1):
                        xt_out(T + 1)
                        x_rstd(T + 1, 1 - s)
                    if k == 1:
                        dve.wait_ge(stored, 16 * (STORES - 4 + STORES * g))
                    tr_out(T - 1, (k - 1) % SUP, 1 - s)
                    reduce(T, s)
                    if k == 0:
                        mla_out(g)
                    rope(T, s)

            with dve.Fori(0, SUPERS - 1) as g:
                body(g, False)
            body(SUPERS - 1, True)
            tr_out(LAST, SUP - 1, LAST % 2)
            mla_out(SUPERS)

        @block.tensor
        def _(pe):
            def xt(T, n, s, first=False):
                pe.wait_ge(x_loaded[s], 32 * n + 32)
                if not first:
                    pe.wait_ge(xt_ready, T)
                xv = x[:, s, :].rearrange("p (m c) -> p c m", c=KC)
                for c in range(KC):
                    i = nc.tensor.transpose(psX[:, c // 4, (c % 4) * P:(c % 4) * P + P], xv[:, c, :], ident[:, :])
                i.then_inc(xt_psum, 1)

            def zz(T, first=False):
                pe.wait_ge(xt_ready, T + 1)
                if not first:
                    pe.wait_ge(z_ready, T)
                for lo, hi in ((0, 512), (512, 1024), (1024, D_IN)):
                    for c in range(KC):
                        i = nc.tensor.matmul(psZ[:, lo:hi], xT[:, c, :], w_in[:, c, lo:hi],
                                             start=c == 0, stop=c == KC - 1)
                i.then_inc(z_psum, 1)

            def tr(U, s):
                pe.wait_ge(rope_ready, U + 1)
                pe.wait_ge(tr_free, 2 * U + 2)
                for j in range(9):
                    w = P if j < 8 else RD
                    i = nc.tensor.transpose(psR[0:w, j * P:j * P + P], trin[:, s, j * P:j * P + w], ident[:, :])
                i.then_inc(tr_psum, 1)

            def mla(S, T):
                pe.wait_ge(xt_ready, T + 2)
                pe.wait_ge(tr_free, 2 * T + 2)
                for u in range(UN):
                    if u >= 2:
                        pe.wait_ge(mla_a, S * UN + u - 1)
                        if u - 2 < QU + KU:
                            pe.wait_ge(mla_d, S * (QU + KU) + u - 1)
                    b = psX[:, u % 2, :]
                    if u < QU:
                        for c in range(2):
                            i = nc.tensor.matmul(b, w_qup[:, c, u * P:u * P + P], cqT[:, c, :],
                                                 start=c == 0, stop=c == 1)
                    elif u < QU + KU:
                        j = u - QU
                        i = nc.tensor.matmul(b, w_kup[:, j * P:j * P + P], ckvT[:, :], start=True, stop=True)
                    else:
                        j = u - QU - KU
                        i = nc.tensor.matmul(b, ckvT[:, j * P:j * P + P], w_vup[:, :], start=True, stop=True)
                    i.then_inc(mla_psum, 1)

            pe.sem_inc(tr_free, 2)
            pe.wait_ge(setup, 16 * 6)
            xt(0, 0, 0, first=True)
            pe.wait_ge(w_loaded, 16 * 5)
            zz(0, first=True)
            xt(1, 0, 1)

            def body(g, last):
                for k in range(SUP):
                    T = g * SUP + 1 + k
                    n, s = load_n(g, k)
                    zz(T)
                    if k == 1:
                        pe.wait_ge(mla_a, (g + 1) * UN)
                    if not (last and k == SUP - 1):
                        n1, s1 = load_n(g, k + 1)
                        xt(T + 1, n1, s1)
                    tr(T - 1, 1 - s)
                    if k == 0:
                        mla(g, T)

            with pe.Fori(0, SUPERS - 1) as g:
                body(g, False)
            body(SUPERS - 1, True)
            tr(LAST, LAST % 2)
            pe.wait_ge(tr_free, 2 * LAST + 4)
            mla(SUPERS, LAST - 1)


def stage_attend(nc, t):
    with ExitStack() as ctx:
        def sb(name, shape, dt=F32):
            return ctx.enter_context(nc.sbuf_tensor("b_" + name, shape, dt))

        def ps(name, shape):
            return ctx.enter_context(nc.psum_tensor("b_" + name, shape, F32))

        def sem(name):
            return ctx.enter_context(nc.semaphore("b_" + name))

        q0 = [sb(f"q0_{s}", [P, TOK], F32R) for s in range(2)]
        q1 = [sb(f"q1_{s}", [P, TOK], F32R) for s in range(2)]
        k0 = [sb(f"k0_{s}", [P, KEYS], F32R) for s in range(2)]
        k1 = [sb(f"k1_{s}", [P, KEYS], F32R) for s in range(2)]
        v = [sb(f"v_{s}", [P, TILES + 1, VC]) for s in range(2)]
        ident = sb("ident", [P, P])
        NP = 4
        prob = sb("prob", [P, NP, W])
        oT = sb("oT", [VC, 2, W])
        rden = sb("rden", [P, SUP])
        ost = sb("ost", [P, 2, SUP, VD])
        mx_s = sb("mx_s", [P, DEC_SEQ // P, 4])
        mx_p = sb("mx_p", [P, SEQ // P, 2])
        nmx = sb("nmx", [P, TILES])
        nmx_m = sb("nmx_m", [P, TILES])
        nmxT = sb("nmxT", [TILES, P], F32R)

        psS = ps("psS", [P, 2, W])
        psM = ps("psM", [P, 2, 512])
        psK = ps("psK", [P, TILES * META])
        psO = ps("psO", [P, 2, W])
        psT = ps("psT", [P, 512])

        ident_loaded = sem("ident_loaded")
        cleared = sem("cleared")
        ld_s = [sem("sample_loaded0"), sem("sample_loaded1")]
        ld_p = [sem("prompt_loaded0"), sem("prompt_loaded1")]
        s_psum = sem("s_psum")
        p_ready = sem("p_ready")
        pv_done = sem("pv_done")
        ot_ready = sem("ot_ready")
        t_psum = sem("t_psum")
        t_free = sem("t_free")
        o_ready = sem("o_ready")
        o_stored = sem("o_stored")
        ost_free = sem("ost_free")
        m_psum = sem("m_psum")
        m_free = sem("m_free")
        k_psum = sem("k_psum")
        nmx_ready = sem("nmx_ready")
        row_made = sem("row_made")
        row_kept = sem("row_kept")
        row_loaded = sem("row_loaded")
        carrier = sem("carrier")

        ITEMS = []
        BLOCKS_END = []
        for base, n in ((SEQ, DEC_SEQ), (0, SEQ)):
            for qc in range(base, base + n, W):
                ch = [(META + base + c * P, P, (base + c * P) // P) for c in range(n // P)] + [(0, META, TILES)]
                for c, (kc, kn, vc) in enumerate(ch):
                    ITEMS.append((qc, kc, kn, vc, c == 0, c == len(ch) - 1))
                BLOCKS_END.append((len(ITEMS) - 1, qc))
        NI = len(ITEMS)
        NB = len(BLOCKS_END)
        END_OF = {j: b for b, (j, _) in enumerate(BLOCKS_END)}
        SAMPLE_LAST = BLOCKS_END[DEC_SEQ // W - 1][0]
        UNITS = [(SEQ // P + i, META + SEQ + u * 512, u) for i in range(DEC_SEQ // P) for u in range(4)]
        UNITS += [(i, META + u * 512, u) for i in range(SEQ // P) for u in range(2)]
        NU = len(UNITS)
        SPAN = 68
        UNIT_AT = {}
        for u in range(NU):
            UNIT_AT.setdefault(1 + u * SPAN // NU + 1, []).append(u)
        META_AT, ROW_AT = SPAN + 2, SPAN + 6
        NUSE = NB + 1
        ROW_USE = sum(j + 4 <= ROW_AT for j, _ in BLOCKS_END)
        HEADS = GH + MH
        SD, PD = 7 * 16, 8 * 16

        def use(h, b, last):
            return h * NUSE + 1 + b + (1 if b >= ROW_USE and not last else 0)

        block = ctx.enter_context(nc.Block())

        def over_heads(engine, head):
            def pair(i, lasts):
                for s in range(2):
                    gqa, nxt, last = lasts[s]
                    head(2 * i + s, i, s, gqa, nxt, last)
            with engine.Fori(0, GH // 2 - 1) as i:
                pair(i, [(True, True, False)] * 2)
            pair(GH // 2 - 1, [(True, True, False), (True, False, False)])
            with engine.Fori(GH // 2, HEADS // 2 - 1) as i:
                pair(i, [(False, False, False)] * 2)
            pair(HEADS // 2 - 1, [(False, False, False), (False, None, True)])

        @block.sync
        def _(sp):
            def load(h, i, s, gqa, part):
                if part == "s":
                    q, k, sm = slice(SEQ, TOK), slice(META + SEQ, KEYS), ld_s[s]
                else:
                    q, k, sm = slice(0, SEQ), slice(0, META + SEQ), ld_p[s]

                def dma(dst, src):
                    sp.dma_start(dst.bitcast(F32), src).then_inc(sm, 16)

                if gqa:
                    rq, rk = bass.ds(h * GD, GD), bass.ds(i * GD, GD)
                    dma(q0[s][0:GD, q], t["QGH"][rq, q])
                    dma(q0[s][GD:P, q], t["QGL"][rq, q])
                    dma(q1[s][0:GD, q], t["QGH"][rq, q])
                    dma(k0[s][0:GD, k], t["KGH"][rk, k])
                    dma(k0[s][GD:P, k], t["KGH"][rk, k])
                    dma(k1[s][0:GD + 1, k], t["KGL"].rearrange("g r n -> (g r) n")[bass.ds(i * (GD + 1), GD + 1), k])
                    vh = i
                else:
                    m = h - GH
                    rq, rk = bass.ds(m * QKD, QKD), bass.ds(m * ND, ND)
                    dma(q0[s][0:QKD, q], t["QMH"][rq, q])
                    dma(q1[s][0:QKD, q], t["QML"][rq, q])
                    dma(k0[s][0:ND, k], t["KMH"][rk, k])
                    dma(k0[s][ND:QKD + 1, k], t["KRH"][:, k])
                    dma(k1[s][0:ND, k], t["KML"][rk, k])
                    dma(k1[s][ND:QKD, k], t["KRL"][:, k])
                    vh = m + PAIRS
                vcol = bass.ds(vh * VC, VC)
                if part == "s":
                    sp.dma_start(v[s][:, SEQ // P:TILES, :],
                                 t["V"][META + SEQ:KEYS, vcol].rearrange("(c p) d -> p c d", p=P)).then_inc(sm, 16)
                else:
                    sp.dma_start(v[s][:, 0:SEQ // P, :],
                                 t["V"][META:META + SEQ, vcol].rearrange("(c p) d -> p c d", p=P)).then_inc(sm, 16)
                    sp.dma_start(v[s][0:META, TILES, :], t["V"][0:META, vcol]).then_inc(sm, 16)

            def row(n, s, gqa):
                sp.wait_ge(row_made, n + 1)
                sp.dma_start(t["MX"].rearrange("(a b) -> a b", b=P), nmxT[:, :].bitcast(F32)).then_inc(row_kept, 16)
                sp.wait_ge(row_kept, 16 * n + 32)
                dst = q1[s][GD:GD + 1, :] if gqa else q0[s][QKD:QKD + 1, :]
                sp.dma_start(dst.bitcast(F32), t["MX"].rearrange("(a b) -> a b", a=1)).then_inc(row_loaded, 16)
                sp.wait_ge(row_loaded, 16 * n + 16)
                sp.sem_inc(carrier, 1)

            sp.dma_start(ident[:, :], t["ident"]).then_inc(ident_loaded, 16)
            sp.wait_ge(cleared, 1)
            for s in range(2):
                load(s, 0, s, True, "s")
                load(s, 0, s, True, "p")
            row(0, 0, True)

            def head(h, i, s, gqa, nxt, last):
                if last:
                    return
                more = not isinstance(h, int) or h + 2 < HEADS
                kind = gqa if not isinstance(h, int) else h + 2 < GH
                if more:
                    sp.wait_ge(pv_done, h * NI + SAMPLE_LAST + 1 + NP)
                    load(h + 2, i + 1, s, kind, "s")
                row(h + 1, 1 - s, nxt)
                if more:
                    sp.wait_ge(pv_done, h * NI + NI + NP)
                    sp.sem_inc(carrier, 1)
                    load(h + 2, i + 1, s, kind, "p")

            over_heads(sp, head)

        @block.gpsimd
        def _(pool):
            def head(h, i, s, gqa, nxt, last):
                for b, (_, qc) in enumerate(BLOCKS_END):
                    pool.wait_ge(o_ready, h * NB + b + 1)
                    pool.dma_start(t["O"].rearrange("(j p) c -> p j c", p=P)[:, qc // P:qc // P + SUP, bass.ds(h * VD, VD)],
                                   ost[:, b % 2, :, :]).then_inc(o_stored, 16)
                    pool.wait_ge(o_stored, 16 * (h * NB + b + 1))
                    pool.sem_inc(ost_free, 1)
            over_heads(pool, head)

        @block.scalar
        def _(act):
            def exp(h, s, j):
                _, _, kn, _, _, _ = ITEMS[j]
                act.wait_ge(s_psum, h * NI + j + 1)
                act.wait_ge(pv_done, h * NI + j + 1)
                nc.scalar.activation(prob[0:kn, (s * NI + j) % NP, :], psS[0:kn, j % 2, :], ACT.Exp).then_inc(p_ready, 1)

            def o_out(h, b):
                act.wait_ge(pv_done, h * NI + BLOCKS_END[b][0] + 1 + NP)
                nc.scalar.activation(oT[:, b % 2, :], psO[0:VC, b % 2, :], ACT.Copy).then_inc(ot_ready, 1)

            act.sem_inc(pv_done, NP)
            act.wait_ge(cleared, 1)
            exp(0, 0, 0)
            exp(0, 0, 1)

            def head(h, i, s, gqa, nxt, last):
                for j in range(2, NI):
                    exp(h, s, j)
                    if j - 2 in END_OF:
                        o_out(h, END_OF[j - 2])
                if not last:
                    exp(h + 1, 1 - s, 0)
                o_out(h, NB - 1)
                if not last:
                    exp(h + 1, 1 - s, 1)

            over_heads(act, head)

        @block.vector
        def _(dve):
            def unit(n, u):
                q, _, g = UNITS[u]
                dve.wait_ge(m_psum, n * NU + u + 1)
                dst = mx_s[:, q - SEQ // P, g:g + 1] if q >= SEQ // P else mx_p[:, q, g:g + 1]
                nc.vector.tensor_reduce(dst, psM[:, u % 2, :], AX.X, ALU.max).then_inc(m_free, 1)

            def finish(n):
                dve.drain()
                dve.wait_ge(k_psum, n + 1)
                nc.vector.tensor_reduce(nmx_m[:, :], psK[:, :].rearrange("p (a b) -> p a b", b=META), AX.X, ALU.max,
                                        negate=True)
                nc.vector.tensor_reduce(nmx[:, SEQ // P:], mx_s[:, :, :], AX.X, ALU.max, negate=True)
                nc.vector.tensor_reduce(nmx[:, 0:SEQ // P], mx_p[:, :, :], AX.X, ALU.max, negate=True)
                dve.drain()
                nc.vector.tensor_tensor(nmx[:, :], nmx[:, :], nmx_m[:, :], ALU.min).then_inc(nmx_ready, 1)

            def row(n, u):
                dve.wait_ge(t_psum, u + 1)
                dve.wait_ge(row_kept, 16 * n + 16)
                nc.vector.tensor_copy(nmxT[:, :], psT[0:TILES, 260:388])
                dve.drain().then_inc(row_made, 1)
                dve.drain().then_inc(t_free, 1)

            def normalise(h, b, u):
                dve.drain()
                dve.wait_ge(t_psum, u + 1)
                tv = psT[:, 0:SUP * VC].rearrange("p (j c) -> p j c", c=VC)
                nc.vector.reciprocal(rden[:, :].unsqueeze(2), tv[:, :, VD:VC])
                dve.drain()
                dve.wait_ge(ost_free, h * NB + b + 1)
                nc.vector.tensor_tensor(ost[:, b % 2, :, :], tv[:, :, 0:VD],
                                        rden[:, :].unsqueeze(2).broadcast_to([P, SUP, VD]), ALU.mult).then_inc(o_ready, 1)
                dve.drain().then_inc(t_free, 1)

            dve.sem_inc(ost_free, 2)
            dve.sem_inc(row_kept, 16)
            nc.vector.memset(prob[:, :, :], 0.0)
            for s in range(2):
                nc.vector.memset(v[s][:, TILES, :], 0.0)
            dve.drain().then_inc(cleared, 1)
            for u in range(NU):
                unit(0, u)
            finish(0)
            row(0, 0)

            def head(h, i, s, gqa, nxt, last):
                for j in range(2, NI):
                    if not last:
                        for u in UNIT_AT.get(j, ()):
                            unit(h + 1, u)
                        if j == META_AT:
                            finish(h + 1)
                        if j == ROW_AT:
                            row(h + 1, h * NUSE + 1 + ROW_USE)
                    if j - 4 in END_OF:
                        normalise(h, END_OF[j - 4], use(h, END_OF[j - 4], last))
                normalise(h, NB - 1, use(h, NB - 1, last))

            over_heads(dve, head)

        @block.tensor
        def _(pe):
            def qk(h, s, gqa, j):
                qc, kc, kn, _, _, _ = ITEMS[j]
                pe.wait_ge(p_ready, h * NI + j + 1)
                q, k = slice(qc, qc + W), slice(kc, kc + kn)
                passes = ([(k0, q0, P), (k1, q1, GD + 1)] if gqa else
                          [(k0, q0, QKD + 1), (k0, q1, QKD), (k1, q0, QKD)])
                for n, (kk, qq, r) in enumerate(passes):
                    m = nc.tensor.matmul(psS[0:kn, j % 2, :], kk[s][0:r, k], qq[s][0:r, q],
                                         start=n == 0, stop=n == len(passes) - 1)
                m.then_inc(s_psum, 1)

            def pv(h, s, j, b):
                _, _, _, vc, first, last = ITEMS[j]
                pe.wait_ge(p_ready, h * NI + j + 3)
                if first:
                    pe.wait_ge(ot_ready, h * NB + b + 1)
                m = nc.tensor.matmul(psO[0:VC, b % 2, :], v[s][:, vc, :], prob[:, (s * NI + j) % NP, :],
                                     start=first, stop=last)
                m.then_inc(pv_done, 1)

            def unit(n, s, gqa, u):
                q, kc, _ = UNITS[u]
                pe.wait_ge(m_free, n * NU + u + 1)
                r = P if gqa else QKD
                nc.tensor.matmul(psM[:, u % 2, :], q0[s][0:r, q * P:q * P + P], k0[s][0:r, kc:kc + 512],
                                 start=True, stop=True).then_inc(m_psum, 1)

            def meta(n, s, gqa):
                r = P if gqa else QKD
                for q in range(TILES):
                    m = nc.tensor.matmul(psK[:, q * META:q * META + META], q0[s][0:r, q * P:q * P + P],
                                         k0[s][0:r, 0:META], start=True, stop=True)
                m.then_inc(k_psum, 1)

            def row(n, u):
                pe.wait_ge(nmx_ready, n + 1)
                pe.wait_ge(t_free, u + 1)
                nc.tensor.transpose(psT[0:TILES, 260:388], nmx[:, :], ident[:, :]).then_inc(t_psum, 1)

            def o_turn(h, b, u):
                pe.wait_ge(ot_ready, h * NB + b + 3)
                pe.wait_ge(t_free, u + 1)
                for c in range(SUP):
                    m = nc.tensor.transpose(psT[:, c * VC:c * VC + VC], oT[:, b % 2, c * P:c * P + P], ident[0:VC, 0:VC])
                m.then_inc(t_psum, 1)

            pe.sem_inc(p_ready, 2)
            pe.sem_inc(ot_ready, 2)
            pe.sem_inc(m_free, 2)
            pe.sem_inc(t_free, 1)
            pe.wait_ge(ident_loaded, 16)
            pe.wait_ge(ld_s[0], SD)
            pe.wait_ge(ld_p[0], PD)
            for u in range(NU):
                unit(0, 0, True, u)
            meta(0, 0, True)
            row(0, 0)
            pe.wait_ge(row_loaded, 16)
            qk(0, 0, True, 0)
            qk(0, 0, True, 1)

            def head(h, i, s, gqa, nxt, last):
                block_of = [sum(e < j for e, _ in BLOCKS_END) for j in range(NI)]
                i1 = i + s
                for j in range(2, NI):
                    qk(h, s, gqa, j)
                    if not last:
                        for u in UNIT_AT.get(j, ()):
                            if u == 0:
                                pe.wait_ge(ld_s[1 - s], SD * i1 + SD)
                            if UNITS[u][0] == 0 and UNITS[u][2] == 0:
                                pe.wait_ge(ld_p[1 - s], PD * i1 + PD)
                            unit(h + 1, 1 - s, nxt, u)
                        if j == META_AT:
                            meta(h + 1, 1 - s, nxt)
                        if j == ROW_AT:
                            row(h + 1, h * NUSE + 1 + ROW_USE)
                    pv(h, s, j - 2, block_of[j - 2])
                    if j - 4 in END_OF:
                        o_turn(h, END_OF[j - 4], use(h, END_OF[j - 4], last))
                if not last:
                    pe.wait_ge(row_loaded, 16 * h + 32)
                    qk(h + 1, 1 - s, nxt, 0)
                pv(h, s, NI - 2, NB - 1)
                pv(h, s, NI - 1, NB - 1)
                if not last:
                    qk(h + 1, 1 - s, nxt, 1)
                o_turn(h, NB - 1, use(h, NB - 1, last))

            over_heads(pe, head)


def stage_mix_out(nc, t, logits):
    with ExitStack() as ctx:
        def sb(name, shape, dt=F32):
            return ctx.enter_context(nc.sbuf_tensor("c_" + name, shape, dt))

        def ps(name, shape):
            return ctx.enter_context(nc.psum_tensor("c_" + name, shape, F32))

        def sem(name):
            return ctx.enter_context(nc.semaphore("c_" + name))

        NR = G + E
        H = D // 2
        w_raw = sb("w_raw", [P, KC, D])
        w_hi = sb("w_hi", [P, KC, D], F32R)
        w_lo = sb("w_lo", [P, KC, D], F32R)
        w_r = sb("w_r", [P, KC, NR])
        b_r = sb("b_r", [NR, 1])
        g_out = sb("g_out", [P, KC])
        g_ffn = sb("g_ffn", [P, D])
        ident = sb("ident", [P, P])
        eps = sb("eps", [P, 1])
        o = sb("o", [P, 2, D])
        x = sb("x", [P, 2, D])
        junk = sb("junk", [P, D])
        oss = sb("oss", [P, 2, 2])
        ostd = sb("ostd", [P, 2, 2])
        orr = sb("orr", [P, 2, 2])
        os_ = sb("os", [P, 2, D])
        oT = sb("oT", [P, KC, P])
        oT_hi = sb("oT_hi", [P, 2, KC, P], F32R)
        oT_lo = sb("oT_lo", [P, 2, KC, P], F32R)
        h2 = sb("h2", [P, 2, D])
        hss = sb("hss", [P, 2])
        hstd = sb("hstd", [P, 2])
        hr = sb("hr", [P, 2])
        u2 = sb("u2", [P, 2, D])
        uT = sb("uT", [P, KC, P])
        lg = sb("lg", [P, P])

        psA = ps("psA", [P, 2, 512])
        psY = ps("psY", [P, 2, 512])
        psU = ps("psU", [P, 2, 512])
        psR = ps("psR", [NR, 512])
        psL = ps("psL", [P, 512])

        w_loaded, small_loaded = sem("w_loaded"), sem("small_loaded")
        w_hi_ready, w_lo_ready = sem("w_hi_ready"), sem("w_lo_ready")
        eps_ready = sem("eps_ready")
        o_loaded = [sem("o_loaded0"), sem("o_loaded1")]
        x_loaded = [sem("x_loaded0"), sem("x_loaded1")]
        ostd_ready, orr_ready, os_ready = sem("ostd_ready"), sem("orr_ready"), sem("os_ready")
        oT_psum, oT_ready, hi_ready, lo_ready = sem("oT_psum"), sem("oT_ready"), sem("hi_ready"), sem("lo_ready")
        y_psum, h2_ready, hstd_ready = sem("y_psum"), sem("h2_ready"), sem("hstd_ready")
        u2_ready, uT_psum, uT_ready = sem("u2_ready"), sem("uT_psum"), sem("uT_ready")
        r_psum, lg_ready, l_psum, l_ready = sem("r_psum"), sem("lg_ready"), sem("l_psum"), sem("l_ready")
        h_stored = [sem("h_stored0"), sem("h_stored1")]

        N = TILES
        block = ctx.enter_context(nc.Block())

        def over_tiles(engine, body):
            for s in range(2):
                body(s, 0, s)
            with engine.Fori(1, N // 2 - 2) as j:
                for s in range(2):
                    body(2 * j + s, j, s)
            for j in (N // 2 - 2, N // 2 - 1):
                for s in range(2):
                    body(2 * j + s, j, s)

        def at_least(T, n):
            return not isinstance(T, int) or T >= n

        def below(T, n):
            return not isinstance(T, int) or T < n

        @block.sync
        def _(sp):
            def load_o(T, s):
                sp.dma_start(o[:, s, :], t["O"][bass.ds(T * P, P), :]).then_inc(o_loaded[s], 16)

            def load_x(T, s):
                sp.dma_start(x[:, s, :], t["xall"][bass.ds(T * P + P, P), :]).then_inc(x_loaded[s], 16)

            sp.dma_start(ident[:, :], t["ident"]).then_inc(small_loaded, 16)
            sp.dma_start(g_out[:, :], t["g_out"]).then_inc(small_loaded, 16)
            sp.dma_start(w_r[:, :, :], t["w_r"].rearrange("(p c) n -> p c n", c=KC)).then_inc(small_loaded, 16)
            sp.dma_start(b_r[:, :], t["b_r"]).then_inc(small_loaded, 16)
            sp.dma_start(g_ffn[:, :], t["g_ffn"]).then_inc(small_loaded, 16)
            load_o(0, 0)
            load_o(1, 1)
            sp.dma_start(w_raw[:, :, :], t["w_out"].rearrange("(p c) n -> p c n", c=KC)).then_inc(w_loaded, 16)
            load_x(0, 0)
            load_x(1, 1)
            sp.wait_ge(os_ready, 1)
            load_o(2, 0)

            def store(T, j, s):
                sp.wait_ge(u2_ready, T + 1)
                sp.dma_start(t["H2"][bass.ds(T * P, P), :], h2[:, s, :]).then_inc(h_stored[s], 16)
                sp.dma_start(t["U2"][bass.ds(T * P, P), :], u2[:, s, :]).then_inc(h_stored[s], 16)

            def body(T, j, s):
                if at_least(T, 1):
                    if below(T, N - 1):
                        sp.wait_ge(h2_ready, T)
                        load_x(T + 1, 1 - s)
                    store(T - 1, j, 1 - s)
                if below(T, N - 3):
                    sp.wait_ge(os_ready, T + 2)
                    load_o(T + 3, 1 - s)

            over_tiles(sp, body)
            store(N - 1, 0, 1)
            for s in range(2):
                sp.wait_ge(h_stored[s], 32 * (N // 2))

        @block.scalar
        def _(act):
            def o_scaled(T, j, s, again=True):
                act.drain()
                if again:
                    act.wait_ge(oT_psum, T - 1)
                act.wait_ge(o_loaded[s], 16 * j + 16)
                for k in range(2):
                    nc.scalar.activation(junk[:, k * H:k * H + H], o[:, s, k * H:k * H + H], ACT.Square,
                                         accum_out=oss[:, s, k:k + 1])
                act.drain()
                nc.scalar.activation(ostd[:, s, :], oss[:, s, :], ACT.Sqrt, scale=1.0 / H,
                                     bias=eps[:, 0:1]).then_inc(ostd_ready, 1)
                act.wait_ge(orr_ready, T + 1)
                for k in range(2):
                    i = nc.scalar.activation(os_[:, s, k * H:k * H + H], o[:, s, k * H:k * H + H], ACT.Copy,
                                             scale=orr[:, s, k:k + 1])
                i.then_inc(os_ready, 1)

            def oT_rounded(T, s):
                act.wait_ge(oT_ready, T + 1)
                nc.scalar.activation(oT_hi[:, s, :, :], oT[:, :, :], ACT.Copy).then_inc(hi_ready, 1)

            def h_stats(T, s):
                act.drain()
                act.wait_ge(h2_ready, T + 1)
                nc.scalar.activation(junk[:, :], h2[:, s, :], ACT.Square, accum_out=hss[:, s:s + 1])
                act.drain()
                nc.scalar.activation(hstd[:, s:s + 1], hss[:, s:s + 1], ACT.Sqrt, scale=1.0 / D,
                                     bias=eps[:, 0:1]).then_inc(hstd_ready, 1)

            act.wait_ge(eps_ready, 1)
            o_scaled(0, 0, 0, again=False)
            o_scaled(1, 0, 1, again=False)
            act.wait_ge(w_loaded, 16)
            nc.scalar.activation(w_hi[:, :, :], w_raw[:, :, :], ACT.Copy).then_inc(w_hi_ready, 1)
            oT_rounded(0, 0)

            def body(T, j, s):
                if at_least(T, 1):
                    h_stats(T - 1, 1 - s)
                if below(T, N - 1):
                    oT_rounded(T + 1, 1 - s)
                if below(T, N - 2):
                    o_scaled(T + 2, j + 1, s)

            over_tiles(act, body)
            h_stats(N - 1, 1)

        @block.vector
        def _(dve):
            def o_recip(T, s):
                dve.wait_ge(ostd_ready, T + 1)
                nc.vector.reciprocal(orr[:, s, :], ostd[:, s, :]).then_inc(orr_ready, 1)

            def oT_out(T):
                dve.drain()
                dve.wait_ge(oT_psum, T + 1)
                nc.vector.tensor_tensor(oT[:, :, :], psA[:, :, :].rearrange("p b (c n) -> p (b c) n", n=P),
                                        g_out[:, :].unsqueeze(2).broadcast_to([P, KC, P]), ALU.mult).then_inc(oT_ready, 1)

            def oT_rest(T, s):
                dve.wait_ge(hi_ready, T + 1)
                nc.vector.tensor_tensor(oT_lo[:, s, :, :], oT[:, :, :], oT_hi[:, s, :, :].bitcast(F32),
                                        ALU.subtract).then_inc(lo_ready, 1)

            def h_out(T, j, s):
                dve.wait_ge(y_psum, T + 1)
                dve.wait_ge(x_loaded[s], 16 * j + 16)
                if at_least(T, 2):
                    dve.wait_ge(h_stored[s], 32 * j)
                nc.vector.tensor_tensor(h2[:, s, :], psY[:, :, :].rearrange("p b n -> p (b n)"), x[:, s, :],
                                        ALU.add).then_inc(h2_ready, 1)

            def u_out(T, s):
                dve.wait_ge(hstd_ready, T + 1)
                nc.vector.reciprocal(hr[:, s:s + 1], hstd[:, s:s + 1])
                dve.drain()
                nc.vector.scalar_tensor_tensor(u2[:, s, :], h2[:, s, :], hr[:, s:s + 1], g_ffn[:, :],
                                               ALU.mult, ALU.mult).then_inc(u2_ready, 1)

            def uT_out(T):
                dve.wait_ge(uT_psum, T + 1)
                nc.vector.tensor_copy(uT[:, :, :], psU[:, :, :].rearrange("p b (c n) -> p (b c) n", n=P)).then_inc(uT_ready, 1)

            def lg_out(T):
                dve.wait_ge(r_psum, T + 1)
                nc.vector.tensor_scalar(lg[0:NR, :], psR[:, 0:P], b_r[:, 0:1], None, ALU.add).then_inc(lg_ready, 1)

            def l_out(T):
                dve.wait_ge(l_psum, T + 1)
                nc.vector.tensor_copy(logits[:, bass.ds(T * NR, NR)], psL[:, 0:NR]).then_inc(l_ready, 1)

            nc.vector.memset(lg[:, :], 0.0)
            nc.vector.memset(eps[:, :], EPS).then_inc(eps_ready, 1)
            dve.drain()
            dve.wait_ge(small_loaded, 16 * 5)
            o_recip(0, 0)
            o_recip(1, 1)
            dve.wait_ge(w_hi_ready, 1)
            nc.vector.tensor_tensor(w_lo[:, :, :], w_raw[:, :, :], w_hi[:, :, :].bitcast(F32),
                                    ALU.subtract).then_inc(w_lo_ready, 1)
            oT_out(0)
            oT_rest(0, 0)

            def body(T, j, s):
                if at_least(T, 1):
                    h_out(T - 1, j - 1 if s == 0 else j, 1 - s)
                if below(T, N - 1):
                    oT_out(T + 1)
                if at_least(T, 1):
                    u_out(T - 1, 1 - s)
                if below(T, N - 1):
                    oT_rest(T + 1, 1 - s)
                if below(T, N - 2):
                    o_recip(T + 2, s)
                if at_least(T, 2):
                    l_out(T - 2)
                if at_least(T, 1):
                    uT_out(T - 1)
                    lg_out(T - 1)

            over_tiles(dve, body)
            h_out(N - 1, N // 2 - 1, 1)
            u_out(N - 1, 1)
            l_out(N - 2)
            uT_out(N - 1)
            lg_out(N - 1)
            l_out(N - 1)

        @block.tensor
        def _(pe):
            def o_turn(T, s, first=False):
                pe.wait_ge(os_ready, T + 1)
                if not first:
                    pe.wait_ge(oT_ready, T)
                ov = os_[:, s, :].rearrange("p (m c) -> p c m", c=KC)
                for c in range(KC):
                    i = nc.tensor.transpose(psA[:, c // 4, (c % 4) * P:(c % 4) * P + P], ov[:, c, :], ident[:, :])
                i.then_inc(oT_psum, 1)

            def y_of(T, s):
                pe.wait_ge(lo_ready, T + 1)
                if at_least(T, 1):
                    pe.wait_ge(h2_ready, T)
                for b in range(2):
                    n = 0
                    for c in range(KC):
                        for a, w in ((oT_hi, w_hi), (oT_lo, w_hi), (oT_hi, w_lo)):
                            i = nc.tensor.matmul(psY[:, b, :], a[:, s, c, :], w[:, c, b * 512:b * 512 + 512],
                                                 start=n == 0, stop=n == 3 * KC - 1)
                            n += 1
                i.then_inc(y_psum, 1)

            def u_turn(T, s):
                pe.wait_ge(u2_ready, T + 1)
                if at_least(T, 1):
                    pe.wait_ge(uT_ready, T)
                uv = u2[:, s, :].rearrange("p (m c) -> p c m", c=KC)
                for c in range(KC):
                    i = nc.tensor.transpose(psU[:, c // 4, (c % 4) * P:(c % 4) * P + P], uv[:, c, :], ident[:, :])
                i.then_inc(uT_psum, 1)

            def route(T):
                pe.wait_ge(uT_ready, T + 1)
                if at_least(T, 1):
                    pe.wait_ge(lg_ready, T)
                for c in range(KC):
                    i = nc.tensor.matmul(psR[:, 0:P], w_r[:, c, :], uT[:, c, :], start=c == 0, stop=c == KC - 1)
                i.then_inc(r_psum, 1)

            def l_turn(T):
                pe.wait_ge(lg_ready, T + 1)
                if at_least(T, 1):
                    pe.wait_ge(l_ready, T)
                nc.tensor.transpose(psL[:, 0:P], lg[:, :], ident[:, :]).then_inc(l_psum, 1)

            pe.wait_ge(small_loaded, 16 * 5)
            o_turn(0, 0, first=True)
            pe.wait_ge(w_lo_ready, 1)

            def body(T, j, s):
                if below(T, N - 1):
                    o_turn(T + 1, 1 - s)
                if at_least(T, 2):
                    l_turn(T - 2)
                y_of(T, s)
                if at_least(T, 1):
                    u_turn(T - 1, 1 - s)
                    route(T - 1)

            over_tiles(pe, body)
            l_turn(N - 2)
            u_turn(N - 1, 1)
            route(N - 1)
            l_turn(N - 1)


def stage_route(nc, t, logits, picks, eb, idx):
    with ExitStack() as ctx:
        def sb(name, shape, dt=F32):
            return ctx.enter_context(nc.sbuf_tensor("r_" + name, shape, dt))

        def sem(name):
            return ctx.enter_context(nc.semaphore("r_" + name))

        NR = G + E
        N = TILES
        HN = N // 2
        prio = sb("prio", [P, EPG])
        tri = sb("tri", [P, P])
        ones = sb("ones", [P, P])
        tok = sb("tok", [P, N], I32)
        first_slot = sb("first_slot", [1, BLOCKS])
        gm = sb("gm", [P, N])
        gd = sb("gd", [P, N, G])
        ge = sb("ge", [P, N, G])
        gsum = sb("gsum", [P, N])
        pg = sb("pg", [P, N])
        eqg = sb("eqg", [P, N, G])
        top = sb("top", [P, N])
        ohg = sb("ohg", [P, N, G])
        wide = sb("wide", [P, N, G, EPG])
        le = sb("le", [P, N, EPG])
        le2 = sb("le2", [P, N, EPG])
        m1 = sb("m1", [P, N])
        m2 = sb("m2", [P, N])
        eq = sb("eq", [P, N, EPG])
        oh1 = sb("oh1", [P, N, EPG])
        oh2 = sb("oh2", [P, N, EPG])
        md = sb("md", [P, N])
        e2 = sb("e2", [P, N])
        den = sb("den", [P, N])
        pick1 = sb("pick1", [P, N, G, EPG])
        pick2 = sb("pick2", [P, N, G, EPG])
        both = sb("both", [P, N * E])
        total = sb("total", [P, N * E])
        before = sb("before", [P, N + 1, E])
        cnt_i = sb("cnt_i", [P, E], I32)
        padded = sb("padded", [P, E])
        ends = sb("ends", [P, E])
        starts = sb("starts", [P, E])
        base = sb("base", [P, N * E])
        slot_f = sb("slot_f", [P, 2, N])
        slot_i = sb("slot_i", [P, 2, N], I32)
        blk_i = sb("blk_i", [P, 2, N], I32)
        blk_f = sb("blk_f", [P, 2, N])
        addr_f = sb("addr_f", [P, 2, N])
        addr = sb("addr", [P, 2, N], U32)
        cmp = sb("cmp", [1, BLOCKS, E])
        eb_f = sb("eb_f", [1, BLOCKS])
        zeros = sb("zeros", [P, BLOCKS], I32)

        psR = ctx.enter_context(nc.psum_tensor("r_psR", [P, 2, 512], F32))
        psT = ctx.enter_context(nc.psum_tensor("r_psT", [P, 2, 512], F32))

        loaded, zeroed, cleared = sem("loaded"), sem("zeroed"), sem("cleared")
        gd_ready, ge_ready, md_ready, e2_ready = sem("gd_ready"), sem("ge_ready"), sem("md_ready"), sem("e2_ready")
        both_ready, ranks, addr_ready, scattered, idx_loaded = (
            sem("both_ready"), sem("ranks"), sem("addr_ready"), sem("scattered"), sem("idx_loaded"))

        block = ctx.enter_context(nc.Block())

        @block.sync
        def _(sp):
            for dst, src in ((prio, "prio"), (tri, "tri"), (tok, "tok"), (first_slot, "first_slot")):
                sp.dma_start(dst[:, :], t[src]).then_inc(loaded, 16)
            sp.wait_ge(zeroed, 1)
            sp.dma_start(t["TOKD"].rearrange("(p b) o -> p (b o)", b=BLOCKS), zeros[:, :]).then_inc(cleared, 16)
            sp.wait_ge(scattered, 16 * 2 * N)
            sp.dma_start(idx[:, :], t["TOKD"].rearrange("(p b) o -> p (b o)", b=BLOCKS)).then_inc(idx_loaded, 16)
            sp.wait_ge(idx_loaded, 16)

        @block.gpsimd
        def _(pool):
            pool.wait_ge(cleared, 16)
            pool.wait_ge(addr_ready, 1)
            for k in range(2):
                for n in range(N):
                    pool.indirect_dma_start(t["TOKD"], bass.IndirectOffsetOnAxis(addr[:, k, n:n + 1], 0),
                                            tok[:, n:n + 1], None).then_inc(scattered, 16)
            pool.wait_ge(scattered, 16 * 2 * N)

        @block.scalar
        def _(act):
            act.wait_ge(gd_ready, 1)
            nc.scalar.activation(ge[:, :, :], gd[:, :, :], ACT.Exp).then_inc(ge_ready, 1)
            act.wait_ge(md_ready, 1)
            nc.scalar.activation(e2[:, :], md[:, :], ACT.Exp).then_inc(e2_ready, 1)

        @block.tensor
        def _(pe):
            pe.wait_ge(both_ready, 1)
            pe.wait_ge(loaded, 64)
            for h in range(2):
                cols = slice(h * HN * E, (h + 1) * HN * E)
                nc.tensor.matmul(psR[:, h, 0:HN * E], tri[:, :], both[:, cols], start=True, stop=True)
                i = nc.tensor.matmul(psT[:, h, 0:HN * E], ones[:, :], both[:, cols], start=True, stop=True)
            i.then_inc(ranks, 1)

        @block.vector
        def _(dve):
            def over(ap, n):
                return ap.unsqueeze(2).broadcast_to([P, N, n])

            def tt(out, a, b, op):
                i = nc.vector.tensor_tensor(out, a, b, op)
                dve.drain()
                return i

            def red(out, a, op):
                nc.vector.tensor_reduce(out, a, AX.X, op)
                dve.drain()

            L3 = logits[:, :].rearrange("p (n r) -> p n r", r=NR)
            lg = L3[:, :, 0:G]
            nc.vector.memset(ones[:, :], 1.0)
            nc.vector.memset(before[:, 0, :], 0.0)
            nc.vector.memset(zeros[:, :], 0)
            dve.drain().then_inc(zeroed, 1)
            dve.wait_ge(loaded, 64)

            def first_max(onehot, hits, val, m, n):
                tt(hits, val, over(m, n), ALU.is_equal)
                tt(hits, hits, prio[:, EPG - n:EPG].unsqueeze(1).broadcast_to([P, N, n]), ALU.mult)
                red(top[:, :], hits, ALU.max)
                tt(onehot, hits, over(top[:, :], n), ALU.is_equal)

            red(gm[:, :], lg, ALU.max)
            nc.vector.tensor_tensor(gd[:, :, :], lg, over(gm[:, :], G), ALU.subtract).then_inc(gd_ready, 1)
            first_max(ohg[:, :, :], eqg[:, :, :], lg, gm[:, :], G)
            dve.wait_ge(ge_ready, 1)
            red(gsum[:, :], ge[:, :, :], ALU.add)
            nc.vector.reciprocal(pg[:, :], gsum[:, :])

            for g in range(G):
                tt(wide[:, :, g, :], L3[:, :, G + g * EPG:G + (g + 1) * EPG],
                   ohg[:, :, g:g + 1].broadcast_to([P, N, EPG]), ALU.mult)
            tt(le[:, :, :], wide[:, :, 0, :], wide[:, :, 1, :], ALU.add)
            tt(le2[:, :, :], wide[:, :, 2, :], wide[:, :, 3, :], ALU.add)
            tt(le[:, :, :], le[:, :, :], le2[:, :, :], ALU.add)
            red(m1[:, :], le[:, :, :], ALU.max)
            first_max(oh1[:, :, :], eq[:, :, :], le[:, :, :], m1[:, :], EPG)
            nc.vector.scalar_tensor_tensor(le2[:, :, :], oh1[:, :, :], -3.0e38, le[:, :, :], ALU.mult, ALU.add)
            dve.drain()
            red(m2[:, :], le2[:, :, :], ALU.max)
            first_max(oh2[:, :, :], eq[:, :, :], le2[:, :, :], m2[:, :], EPG)

            tt(md[:, :], m2[:, :], m1[:, :], ALU.subtract)
            dve.drain().then_inc(md_ready, 1)
            dve.wait_ge(e2_ready, 1)
            nc.vector.tensor_scalar(den[:, :], e2[:, :], 1.0, None, ALU.add)
            dve.drain()
            nc.vector.reciprocal(den[:, :], den[:, :])
            dve.drain()
            gate = picks[:, :].rearrange("p (n k) -> p n k", k=4)
            tt(gate[:, :, 2], pg[:, :], den[:, :], ALU.mult)
            tt(gate[:, :, 3], gate[:, :, 2], e2[:, :], ALU.mult)

            for g in range(G):
                og = ohg[:, :, g:g + 1].broadcast_to([P, N, EPG])
                nc.vector.tensor_tensor(pick1[:, :, g, :], oh1[:, :, :], og, ALU.mult)
                nc.vector.tensor_tensor(pick2[:, :, g, :], oh2[:, :, :], og, ALU.mult)
            dve.drain()
            flat = "p n g e -> p (n g e)"
            tt(both[:, :], pick1[:, :, :, :].rearrange(flat), pick2[:, :, :, :].rearrange(flat), ALU.add)
            dve.drain().then_inc(both_ready, 1)

            dve.wait_ge(ranks, 1)
            for h in range(2):
                nc.vector.tensor_copy(total[:, h * HN * E:(h + 1) * HN * E], psT[:, h, 0:HN * E])
            dve.drain()
            for n in range(N):
                tt(before[:, n + 1, :], before[:, n, :], total[:, n * E:(n + 1) * E], ALU.add)

            nc.vector.tensor_scalar(cnt_i[:, :], before[:, N, :], float(P - 1), None, ALU.add)
            dve.drain()
            nc.vector.tensor_scalar(cnt_i[:, :], cnt_i[:, :], 7, 7, ALU.arith_shift_right, ALU.logical_shift_left)
            dve.drain()
            nc.vector.tensor_copy(padded[:, :], cnt_i[:, :])
            dve.drain()
            nc.vector.tensor_tensor_scan(ends[:, :], ones[:, 0:E], padded[:, :], 0.0, ALU.mult, ALU.add)
            dve.drain()
            tt(starts[:, :], ends[:, :], padded[:, :], ALU.subtract)

            for h in range(2):
                cols = slice(h * HN * E, (h + 1) * HN * E)
                nc.vector.tensor_tensor(base[:, cols], psR[:, h, 0:HN * E],
                                        before[:, h * HN:(h + 1) * HN, :].rearrange("p n e -> p (n e)"), ALU.add)
            dve.drain()
            b3 = base[:, :].rearrange("p (n e) -> p n e", e=E)
            tt(b3, b3, starts[:, :].unsqueeze(1).broadcast_to([P, N, E]), ALU.add)
            for k, pick in enumerate((pick1, pick2)):
                tt(both[:, :], pick[:, :, :, :].rearrange(flat), base[:, :], ALU.mult)
                red(slot_f[:, k, :], both[:, :].rearrange("p (n e) -> p n e", e=E), ALU.add)
                nc.vector.tensor_copy(gate[:, :, k].bitcast(U32), slot_f[:, k, :])
            nc.vector.tensor_copy(slot_i[:, :, :], slot_f[:, :, :])
            dve.drain()
            nc.vector.tensor_scalar(blk_i[:, :, :], slot_i[:, :, :], 7, None, ALU.arith_shift_right)
            dve.drain()
            nc.vector.tensor_copy(blk_f[:, :, :], blk_i[:, :, :])
            nc.vector.tensor_scalar(addr_f[:, :, :], slot_f[:, :, :], float(BLOCKS), None, ALU.mult)
            dve.drain()
            nc.vector.scalar_tensor_tensor(addr[:, :, :], blk_f[:, :, :], -float(P * BLOCKS - 1), addr_f[:, :, :],
                                           ALU.mult, ALU.add)
            dve.drain().then_inc(addr_ready, 1)

            tt(cmp[:, :, :], ends[0:1, :].unsqueeze(1).broadcast_to([1, BLOCKS, E]),
               first_slot[0:1, :].unsqueeze(2).broadcast_to([1, BLOCKS, E]), ALU.is_le)
            red(eb_f[:, :], cmp[:, :, :], ALU.add)
            nc.vector.tensor_scalar(eb[:, :], eb_f[:, :], float(E - 1), None, ALU.min)
            dve.drain()


def stage_experts(nc, t, eb, idx):
    with ExitStack() as ctx:
        def sb(name, shape, dt=F32):
            return ctx.enter_context(nc.sbuf_tensor("e_" + name, shape, dt))

        def ps(name, shape):
            return ctx.enter_context(nc.psum_tensor("e_" + name, shape, F32))

        def sem(name):
            return ctx.enter_context(nc.semaphore("e_" + name))

        HC = DE // P
        ident = sb("ident", [P, P])
        w_gu = [sb(f"w_gu{s}", [P, KC, 2 * DE]) for s in range(2)]
        w_dn = [sb(f"w_dn{s}", [P, HC, D]) for s in range(2)]
        cur = sb("cur", [P, 2], U32)
        x = [sb(f"x{s}", [P, D]) for s in range(2)]
        xT = sb("xT", [P, 2, KC, P])
        act_g = sb("act_g", [P, DE])
        hid = sb("hid", [P, 2, DE])
        hT = sb("hT", [P, HC, P])
        y = sb("y", [P, 2, D])

        psX = ps("psX", [P, 2, 512])
        psG = ps("psG", [P, 2, 512])
        psH = ps("psH", [P, 512])
        psY = ps("psY", [P, 2, 512])

        ident_loaded = sem("ident_loaded")
        w_loaded = [sem("w_loaded0"), sem("w_loaded1")]
        x_loaded = [sem("x_loaded0"), sem("x_loaded1")]
        cur_ready = sem("cur_ready")
        xT_psum, xT_ready = sem("xT_psum"), sem("xT_ready")
        g_psum, silu_ready, hid_ready = sem("g_psum"), sem("silu_ready"), sem("hid_ready")
        hT_psum, hT_ready = sem("hT_psum"), sem("hT_ready")
        y_psum, y_ready = sem("y_psum"), sem("y_ready")
        y_stored = [sem("y_stored0"), sem("y_stored1")]

        block = ctx.enter_context(nc.Block())

        def over_blocks(engine, body):
            with engine.Fori(0, BLOCKS // 2 - 1) as j:
                for s in range(2):
                    body(2 * j + s, j, s, False)
            for s in range(2):
                body(BLOCKS - 2 + s, BLOCKS // 2 - 1, s, s == 1)

        @block.sync
        def _(sp):
            sp.dma_start(ident[:, :], t["ident"]).then_inc(ident_loaded, 16)
            sp.sem_inc(y_psum, 2)

            def body(b, j, s, last):
                e = sp.value_load(eb[0:1, bass.ds(b, 1)], min_val=0, max_val=E - 1)
                sp.wait_ge(y_psum, b + 1)
                for k, w in enumerate(("w_gate", "w_up")):
                    sp.dma_start(w_gu[s][:, :, k * DE:(k + 1) * DE],
                                 t[w][bass.ds(e * D, D), :].rearrange("(p c) n -> p c n", c=KC)).then_inc(w_loaded[s], 16)
                sp.dma_start(w_dn[s][:, :, :],
                             t["w_down"][bass.ds(e * DE, DE), :].rearrange("(p c) n -> p c n", c=HC)).then_inc(w_loaded[s], 16)

            over_blocks(sp, body)

        @block.gpsimd
        def _(pool):
            pool.sem_inc(xT_psum, 2)

            def body(b, j, s, last):
                pool.wait_ge(xT_psum, b + 1)
                nc.gpsimd.tensor_copy(cur[:, s:s + 1], idx[:, bass.ds(b, 1)]).then_inc(cur_ready, 1)
                pool.wait_ge(ident_loaded, 16)
                pool.wait_ge(cur_ready, b + 1)
                pool.indirect_dma_start(x[s][:, :], None, t["U2"],
                                        bass.IndirectOffsetOnAxis(cur[:, s:s + 1], 0)).then_inc(x_loaded[s], 16)
                pool.wait_ge(x_loaded[s], 16 * j + 16)

            over_blocks(pool, body)

        @block.scalar
        def _(act):
            for s in range(2):
                act.sem_inc(y_stored[s], 16)

            def body(b, j, s, last):
                act.wait_ge(g_psum, b + 1)
                act.wait_ge(hid_ready, b + 1)
                nc.scalar.activation(act_g[:, :], psG[:, s, 0:DE], ACT.Silu).then_inc(silu_ready, 1)
                act.wait_ge(y_psum, b + 3)
                act.wait_ge(y_stored[s], 16 * j + 16)
                nc.scalar.activation(y[:, s, :], psY[:, :, :].rearrange("p b n -> p (b n)"), ACT.Copy).then_inc(y_ready, 1)
                act.wait_ge(y_ready, b + 2)
                act.dma_start(t["Y"][bass.ds(b * P, P), :], y[:, s, :]).then_inc(y_stored[s], 16)

            act.sem_inc(hid_ready, 1)
            over_blocks(act, body)
            for s in range(2):
                act.wait_ge(y_stored[s], 16 * (BLOCKS // 2) + 16)

        @block.vector
        def _(dve):
            def xT_out(b, s):
                dve.wait_ge(xT_psum, b + 3)
                nc.vector.tensor_copy(xT[:, s, :, :], psX[:, :, :].rearrange("p b (c n) -> p (b c) n", n=P)).then_inc(xT_ready, 1)

            def body(b, j, s, last):
                if not last:
                    xT_out(b + 1, 1 - s)
                dve.wait_ge(silu_ready, b + 1)
                nc.vector.tensor_tensor(hid[:, s, :], act_g[:, :], psG[:, s, DE:2 * DE], ALU.mult).then_inc(hid_ready, 1)
                dve.wait_ge(hT_psum, b + 1)
                nc.vector.tensor_copy(hT[:, :, :], psH[:, 0:DE].rearrange("p (c n) -> p c n", n=P)).then_inc(hT_ready, 1)

            xT_out(0, 0)
            over_blocks(dve, body)

        @block.tensor
        def _(pe):
            def x_turn(b, n, s):
                pe.wait_ge(x_loaded[s], 16 * n + 16)
                pe.wait_ge(xT_ready, b + 1)
                xv = x[s][:, :].rearrange("p (m c) -> p c m", c=KC)
                for c in range(KC):
                    i = nc.tensor.transpose(psX[:, c // 4, (c % 4) * P:(c % 4) * P + P], xv[:, c, :], ident[:, :])
                i.then_inc(xT_psum, 1)

            def body(b, j, s, last):
                pe.wait_ge(w_loaded[s], 48 * j + 48)
                pe.wait_ge(xT_ready, b + 2)
                pe.wait_ge(hid_ready, b + 1)
                for c in range(KC):
                    i = nc.tensor.matmul(psG[:, s, :], xT[:, s, c, :], w_gu[s][:, c, :], start=c == 0, stop=c == KC - 1)
                i.then_inc(g_psum, 1)
                if not last:
                    x_turn(b + 1, j + s, 1 - s)
                pe.wait_ge(hid_ready, b + 2)
                hv = hid[:, s, :].rearrange("p (m c) -> p c m", c=HC)
                for c in range(HC):
                    i = nc.tensor.transpose(psH[:, c * P:(c + 1) * P], hv[:, c, :], ident[:, :])
                i.then_inc(hT_psum, 1)
                pe.wait_ge(hT_ready, b + 1)
                pe.wait_ge(y_ready, b + 1)
                for c in range(HC):
                    for h in range(2):
                        i = nc.tensor.matmul(psY[:, h, :], hT[:, c, :], w_dn[s][:, c, h * 512:(h + 1) * 512],
                                             start=c == 0, stop=c == HC - 1)
                i.then_inc(y_psum, 1)

            pe.sem_inc(xT_ready, 1)
            pe.sem_inc(y_ready, 1)
            pe.wait_ge(ident_loaded, 16)
            x_turn(0, 0, 0)
            over_blocks(pe, body)


def stage_combine(nc, t, picks):
    with ExitStack() as ctx:
        def sb(name, shape, dt=F32):
            return ctx.enter_context(nc.sbuf_tensor("f_" + name, shape, dt))

        def sem(name):
            return ctx.enter_context(nc.semaphore("f_" + name))

        N = TILES
        g_fin = sb("g_fin", [P, D])
        eps = sb("eps", [P, 1])
        cur = sb("cur", [P, 2, 4])
        ya = [sb(f"ya{s}", [P, D]) for s in range(2)]
        yb = [sb(f"yb{s}", [P, D]) for s in range(2)]
        h = sb("h", [P, 2, D])
        acc = sb("acc", [P, D])
        junk = sb("junk", [P, D])
        ss, std, rs = sb("ss", [P, 2]), sb("std", [P, 2]), sb("rs", [P, 2])
        res = sb("res", [P, 2, D])

        g_loaded, eps_ready, cur_ready = sem("g_loaded"), sem("eps_ready"), sem("cur_ready")
        y_loaded = [sem("y_loaded0"), sem("y_loaded1")]
        h_loaded = [sem("h_loaded0"), sem("h_loaded1")]
        sum_ready, std_ready, res_ready = sem("sum_ready"), sem("std_ready"), sem("res_ready")
        res_stored = [sem("res_stored0"), sem("res_stored1")]

        block = ctx.enter_context(nc.Block())

        def over_tiles(engine, body):
            with engine.Fori(0, N // 2) as j:
                for s in range(2):
                    body(2 * j + s, j, s)

        @block.sync
        def _(sp):
            sp.dma_start(g_fin[:, :], t["g_fin"]).then_inc(g_loaded, 16)
            sp.sem_inc(res_ready, 2)

            def body(T, j, s):
                sp.wait_ge(res_ready, T + 1)
                sp.dma_start(h[:, s, :], t["H2"][bass.ds(T * P, P), :]).then_inc(h_loaded[s], 16)

            over_tiles(sp, body)

        @block.gpsimd
        def _(pool):
            def body(T, j, s):
                pool.wait_ge(res_ready, T + 1)
                nc.gpsimd.tensor_copy(cur[:, s, :].bitcast(U32),
                                      picks[:, bass.ds(T * 4, 4)].bitcast(U32)).then_inc(cur_ready, 1)
                pool.wait_ge(g_loaded, 16)
                pool.wait_ge(cur_ready, T + 1)
                for k, y in enumerate((ya, yb)):
                    pool.indirect_dma_start(y[s][:, :], None, t["Y"],
                                            bass.IndirectOffsetOnAxis(cur[:, s, k:k + 1].bitcast(U32), 0)).then_inc(y_loaded[s], 16)

            over_tiles(pool, body)

        @block.vector
        def _(dve):
            nc.vector.memset(eps[:, :], EPS).then_inc(eps_ready, 1)
            dve.wait_ge(g_loaded, 16)
            for s in range(2):
                dve.sem_inc(res_stored[s], 16)

            def body(T, j, s):
                dve.drain()
                dve.wait_ge(y_loaded[s], 32 * j + 32)
                dve.wait_ge(h_loaded[s], 16 * j + 16)
                dve.wait_ge(cur_ready, T + 1)
                nc.vector.scalar_tensor_tensor(acc[:, :], ya[s][:, :], cur[:, s, 2:3], h[:, s, :], ALU.mult, ALU.add)
                dve.drain()
                nc.vector.scalar_tensor_tensor(acc[:, :], yb[s][:, :], cur[:, s, 3:4], acc[:, :],
                                               ALU.mult, ALU.add).then_inc(sum_ready, 1)
                dve.wait_ge(std_ready, T + 1)
                nc.vector.reciprocal(rs[:, s:s + 1], std[:, s:s + 1])
                dve.drain()
                dve.wait_ge(res_stored[s], 16 * j + 16)
                nc.vector.scalar_tensor_tensor(res[:, s, :], acc[:, :], rs[:, s:s + 1], g_fin[:, :],
                                               ALU.mult, ALU.mult).then_inc(res_ready, 1)

            over_tiles(dve, body)

        @block.scalar
        def _(act):
            act.wait_ge(eps_ready, 1)

            def body(T, j, s):
                act.drain()
                act.wait_ge(sum_ready, T + 1)
                nc.scalar.activation(junk[:, :], acc[:, :], ACT.Square, accum_out=ss[:, s:s + 1])
                act.drain()
                nc.scalar.activation(std[:, s:s + 1], ss[:, s:s + 1], ACT.Sqrt, scale=1.0 / D,
                                     bias=eps[:, 0:1]).then_inc(std_ready, 1)
                act.wait_ge(res_ready, T + 3)
                act.dma_start(t["out"][bass.ds(T * P, P), :], res[:, s, :]).then_inc(res_stored[s], 16)

            over_tiles(act, body)
            for s in range(2):
                act.wait_ge(res_stored[s], 16 * (N // 2) + 16)


def hymba_trunk(nc, t):
    for name, (shape, dt) in SCRATCH.items():
        t[name] = nc.dram_tensor(name, shape, dt).ap()
    stage_project(nc, t)
    stage_attend(nc, t)
    with ExitStack() as ctx:
        logits = ctx.enter_context(nc.sbuf_tensor("logits", [P, TILES * (G + E)], F32))
        picks = ctx.enter_context(nc.sbuf_tensor("picks", [P, TILES * 4], F32))
        eb = ctx.enter_context(nc.sbuf_tensor("eb", [1, BLOCKS], I32))
        idx = ctx.enter_context(nc.sbuf_tensor("idx", [P, BLOCKS], I32))
        stage_mix_out(nc, t, logits)
        stage_route(nc, t, logits, picks, eb, idx)
        stage_experts(nc, t, eb, idx)
        stage_combine(nc, t, picks)


def layouts(i):
    f = np.float32
    c = np.ascontiguousarray
    sw = np.arange(GD).reshape(-1, 2)[:, ::-1].ravel()
    rows = lambda a: np.broadcast_to(a, (P,) + a.shape)
    meta = np.zeros((P, D), f)
    meta[:META] = i["meta_tokens"]
    xall = np.concatenate([meta, i["x_prompt"][0], i["x_sample"][0]])
    gq, gk = i["gqa_q_norm_g"][0], i["gqa_k_norm_g"][0]
    g_rows = rows(np.stack([gq, gq[sw], gk, gk[sw]]))
    qup = i["w_mla_q_up"][0].reshape(QR, MH, QKD)
    qup = np.concatenate([qup, qup[:, :, ND:][:, :, sw[:RD]]], axis=2).reshape(QR, MH * P)
    kv = i["w_mla_kv_up"][0].reshape(KVR, MH, ND + VD)

    def angles(pr, pc, rot):
        half = rot // 2
        inv = (f(10000.0) ** (-np.arange(0, half, 2, dtype=f) / f(half))).astype(f)
        a = np.concatenate([pr[:, None] * inv, pc[:, None] * inv], axis=-1)
        co, si = np.cos(a).astype(f), np.sin(a).astype(f)
        return np.repeat(co, 2, axis=1), np.stack([-si, si], axis=2).reshape(len(pr), rot)

    n = np.arange(DEC_SEQ)
    pr = np.concatenate([np.full(P, -1), n[:SEQ] // 64, n // 64]).astype(f)
    pc = np.concatenate([np.arange(P), n[:SEQ] % 64, n % 64]).astype(f)
    cg, sg = angles(pr, pc, GD)
    cm, sm = angles(pr, pc, RD)
    rope_rows = np.concatenate([cg, sg, cm, sm], axis=1)
    pad = np.zeros((RD, W - P), f)
    rope_cols = np.stack([np.concatenate([pad, cm.T * f(MSCALE)], axis=1), np.concatenate([pad, sm.T * f(MSCALE)], axis=1)])
    inv_n = np.broadcast_to(np.array([1 / GD] * 10 + [1 / QR, 1 / KVR], f), (P, 12))
    a = {
        "xall": xall, "rope_rows": rope_rows, "rope_cols": rope_cols, "ident": np.eye(P, dtype=f),
        "g_mix": i["norm_mix_g"][0].reshape(P, KC), "g_cq": i["mla_q_norm_g"][0].reshape(2, P).T,
        "g_ckv": i["mla_kv_norm_g"][0].reshape(P, 1), "g_rows": g_rows, "inv_n": inv_n,
        "w_in": i["w_in"][0], "w_qup": qup, "w_kup": kv[:, :, :ND].reshape(KVR, MH * ND),
        "w_vup": kv[:, :, ND:].reshape(KVR, MH * VD),
        "w_out": i["w_out"][0],
        "g_out": np.concatenate([i["gqa_out_norm_g"][0], i["mla_out_norm_g"][0]]).reshape(P, KC),
        "g_ffn": rows(i["norm_ffn_g"][0]),
        "g_fin": rows(i["norm_final_g"]),
        "w_gate": i["w_expert_gate"][0].reshape(E * D, DE), "w_up": i["w_expert_up"][0].reshape(E * D, DE),
        "w_down": i["w_expert_down"][0].reshape(E * DE, D),
        "prio": rows(np.arange(EPG, 0, -1).astype(f)), "tri": np.triu(np.ones((P, P), f), 1),
        "tok": (np.arange(TILES)[None, :] * P + np.arange(P)[:, None]).astype(np.int32),
        "first_slot": (np.arange(BLOCKS) * P).astype(f).reshape(1, BLOCKS),
        "w_r": np.concatenate([i["w_router_group"][0], i["w_router_expert"][0]], axis=1),
        "b_r": np.concatenate([i["b_router_group"][0], i["b_router_expert"][0]]).reshape(G + E, 1),
    }
    return {k: c(np.asarray(v)) for k, v in a.items()}


SCRATCH = {
    "QGH": ([GH * GD, TOK], F32), "QGL": ([GH * GD, TOK], F32),
    "QMH": ([MH * QKD, TOK], F32), "QML": ([MH * QKD, TOK], F32),
    "KGH": ([PAIRS * GD, KEYS], F32), "KGL": ([PAIRS, GD + 1, KEYS], F32),
    "KMH": ([MH * ND, KEYS], F32), "KML": ([MH * ND, KEYS], F32),
    "KRH": ([RD + 1, KEYS], F32), "KRL": ([RD, KEYS], F32),
    "V": ([KEYS, NV * VC], F32),
    "MX": ([TOK], F32), "O": ([TOK, D], F32),
    "H2": ([TOK, D], F32), "U2": ([TOK, D], F32),
    "TOKD": ([P * BLOCKS, 1], I32), "Y": ([P * BLOCKS, D], F32),
}


def kernel(**inputs):
    import concourse.bacc as bacc
    from concourse.bass_utils import run_bass_kernel_spmd

    nc = bacc.Bacc("TRN2", target_bir_lowering=False, num_devices=1)
    arrays = layouts({k: np.asarray(v) for k, v in inputs.items()})
    t = {n: nc.dram_tensor(n, a.shape, mybir.dt.from_np(a.dtype), kind="ExternalInput").ap()
         for n, a in arrays.items()}
    t["out"] = nc.dram_tensor("out", (TOK, D), F32, kind="ExternalOutput").ap()
    hymba_trunk(nc, t)
    out = run_bass_kernel_spmd(nc, [arrays], core_ids=[0]).results[0]["out"]
    return out[None, :SEQ], out[None, SEQ:]
```

```python
import numpy as np
import concourse.bass as bass
from concourse import mybir
from contextlib import ExitStack

F32 = mybir.dt.float32
F32R = mybir.dt.float32r
I32 = mybir.dt.int32
U32 = mybir.dt.uint32
ALU = mybir.AluOpType
ACT = mybir.ActivationFunctionType
AX = mybir.AxisListType

P = 128
D = 1024
KC = D // P
SEQ, DEC_SEQ, META = 1024, 2048, 16
TOK = SEQ + DEC_SEQ
KEYS = TOK + META
TILES = TOK // P
SUP = 4
SUPERS = TILES // SUP
W = SUP * P
EPS = 1e-6

GH, GKV, GD = 8, 2, 64
MH, QR, KVR, ND, RD, VD = 8, 256, 128, 64, 32, 64
QKD = ND + RD
D_IN = 1184
ZQ, ZK, ZV, ZCQ, ZCKV, ZKR = 0, 512, 640, 768, 1024, 1152
GSCALE = GD ** -0.5
MSCALE = QKD ** -0.5
PAIRS = GH // 2
NV = PAIRS + MH
VC = VD + 1

G, EPG, E = 4, 8, 32
DE = 256
BLOCKS = 80
BLOCKS_SURE = 2 * TOK // P
assert (2 * TOK + E * (P - 1)) // P < BLOCKS


def stage_project(nc, t):
    with ExitStack() as ctx:
        def sb(name, shape, dt=F32):
            return ctx.enter_context(nc.sbuf_tensor("a_" + name, shape, dt))

        def ps(name, shape):
            return ctx.enter_context(nc.psum_tensor("a_" + name, shape, F32))

        def sem(name):
            return ctx.enter_context(nc.semaphore("a_" + name))

        w_in = sb("w_in", [P, KC, D_IN])
        w_qup = sb("w_qup", [P, 2, MH * P])
        w_kup = sb("w_kup", [P, MH * ND])
        w_vup = sb("w_vup", [P, MH * VD])
        ident = sb("ident", [P, P])
        g_mix = sb("g_mix", [P, KC])
        g_cq = sb("g_cq", [P, 2])
        g_ckv = sb("g_ckv", [P, 1])
        g_rows = sb("g_rows", [P, 4, GD])
        inv_n = sb("inv_n", [P, 12])
        eps = sb("eps", [P, 1])
        x = sb("x", [P, 2, D])
        tab = sb("tab", [P, 2, 192])
        colc = sb("colc", [P, 2, W])
        junk = sb("junk", [P, D_IN])
        ssq = sb("ssq", [P, 2])
        std = sb("std", [P, 2])
        rstd = sb("rstd", [P, 2])
        xT = sb("xT", [P, KC, P])
        z = sb("z", [P, D_IN])
        sq = sb("sq", [P, D_IN])
        hss = sb("hss", [P, 12])
        hsn = sb("hsn", [P, 12])
        hstd = sb("hstd", [P, 12])
        hr = sb("hr", [P, 12])
        tA = sb("tA", [P, 4, GD])
        qn = sb("qn", [P, 640])
        qs = sb("qs", [P, 640])
        kr_tmp = sb("kr_tmp", [P, 2 * RD])
        trin = sb("trin", [P, 2, 1184])
        qk_hi = sb("qk_hi", [P, 5, W], F32R)
        qk_lo = sb("qk_lo", [P, 5, W], F32R)
        kr_hi = sb("kr_hi", [RD + 1, W], F32R)
        kr_lo = sb("kr_lo", [RD, W], F32R)
        ones_row = sb("ones_row", [1, W], F32R)
        cqT = sb("cqT", [P, 2, W])
        ckvT = sb("ckvT", [P, W])
        qn_hi = sb("qn_hi", [P, 4, W], F32R)
        qn_lo = sb("qn_lo", [P, 4, W], F32R)
        qr_hi = sb("qr_hi", [P, 2, W], F32R)
        qr_lo = sb("qr_lo", [P, 2, W], F32R)
        mk_hi = sb("mk_hi", [P, 4, W], F32R)
        mk_lo = sb("mk_lo", [P, 4, W], F32R)
        rope_s = sb("rope_s", [P, 2, W])
        rope_c = sb("rope_c", [P, 2, W])
        vst = sb("vst", [P, SUP, NV, VC])

        psX = ps("psX", [P, 2, 512])
        psZ = ps("psZ", [P, 3 * 512])
        psR = ps("psR", [P, 3 * 512])

        setup = sem("setup")
        w_loaded, up_loaded = sem("w_loaded"), sem("up_loaded")
        consts = sem("consts")
        x_loaded = [sem("x_loaded0"), sem("x_loaded1")]
        tab_loaded = [sem("tab_loaded0"), sem("tab_loaded1")]
        col_loaded = sem("col_loaded")
        std_ready = sem("std_ready")
        rstd_ready = sem("rstd_ready")
        xt_psum = sem("xt_psum")
        xt_ready = sem("xt_ready")
        z_psum = sem("z_psum")
        z_ready = sem("z_ready")
        sq_ready = sem("sq_ready")
        hs_ready = sem("hs_ready")
        hstd_ready = sem("hstd_ready")
        rope_ready = sem("rope_ready")
        tr_psum = sem("tr_psum")
        tr_hi = sem("tr_hi")
        tr_free = sem("tr_free")
        mla_psum = sem("mla_psum")
        mla_a = sem("mla_a")
        mla_d = sem("mla_d")
        mla_rope = sem("mla_rope")
        stored_t = sem("stored_t")
        stored_m = sem("stored_m")
        carrier = sem("carrier")

        UNITS = [("v", j) for j in range(SUP)] + [("k", j) for j in range(MH // 2)]
        UNITS += [("n", j) for j in range(MH // 2)] + [("r", 0), ("s", 0), ("r", 1), ("s", 1)]
        UN, UV, UA = len(UNITS), SUP, SUP + MH
        UD = UN - UV
        STORES_T, STORES_M = 3 * PAIRS + 5, 6
        META_T, META_M = STORES_T - 2, STORES_M - 4
        LAST = TILES

        block = ctx.enter_context(nc.Block())

        def load_n(g, k):
            return 2 * g + (1 + k) // 2, (1 + k) % 2

        @block.sync
        def _(sp):
            def load_x(T, s):
                sp.dma_start(x[:, s, :], t["xall"][bass.ds(T * P, P), :]).then_inc(x_loaded[s], 16)

            def load_tab(T, s):
                sp.dma_start(tab[:, s, :], t["rope_rows"][bass.ds(T * P, P), :]).then_inc(tab_loaded[s], 16)

            def load_cols(S):
                sp.dma_start(colc[:, :, :], t["rope_cols"].rearrange("k p n -> p k n")[:, :, bass.ds(S * W, W)]).then_inc(col_loaded, 16)

            def store_qk(lo, n, kcol, qcol):
                c = slice(lo, lo + n)
                kc = bass.ds(kcol, n)
                out = []
                for pair in range(PAIRS):
                    r = slice(GD * (pair // 2), GD * (pair // 2) + GD)
                    out += [(t["KGH"][pair * GD:pair * GD + GD, kc], qk_hi[r, 4, c]),
                            (t["KGL"][pair, 0:GD, kc], qk_lo[r, 4, c]),
                            (t["KGL"][pair, GD:GD + 1, kc], ones_row[0:1, 0:n])]
                out += [(t["KRH"][:, kc], kr_hi[:, c]), (t["KRL"][:, kc], kr_lo[:, c])]
                if n == W:
                    qc = bass.ds(qcol, n)
                    out += [(t["QGH"].rearrange("(j p) n -> p j n", p=P)[:, :, qc], qk_hi[:, 0:4, :]),
                            (t["QGL"].rearrange("(j p) n -> p j n", p=P)[:, :, qc], qk_lo[:, 0:4, :])]
                assert len(out) == (STORES_T if n == W else META_T) - 1
                for o, i in out:
                    sp.dma_start(o, i.bitcast(F32)).then_inc(stored_t, 16)

            def store_v(n, kcol):
                if n == W:
                    sp.dma_start(t["V"][bass.ds(kcol, W), :].rearrange("(j p) c -> p j c", p=P),
                                 vst[:, :, :, :].rearrange("p j h c -> p j (h c)")).then_inc(stored_t, 16)
                else:
                    sp.dma_start(t["V"][bass.ds(kcol, n), :],
                                 vst[0:n, SUP - 1, :, :].rearrange("p h c -> p (h c)")).then_inc(stored_t, 16)

            def store_m(lo, n, kcol, qcol):
                c = slice(lo, lo + n)
                out = [(t[name].rearrange("(j p) n -> p j n", p=P)[:, :, bass.ds(kcol, n)], tile[:, :, c])
                       for name, tile in (("KMH", mk_hi), ("KML", mk_lo))]
                if n == W:
                    out += [(t[name].rearrange("(j p) n -> p j n", p=P)[:, :, bass.ds(qcol, n)], tile[:, :, :])
                            for name, tile in (("QNH", qn_hi), ("QNL", qn_lo), ("QRH", qr_hi), ("QRL", qr_lo))]
                assert len(out) == (STORES_M if n == W else META_M)
                for o, i in out:
                    sp.dma_start(o, i.bitcast(F32)).then_inc(stored_m, 16)

            def store(S, last_tile, first=False):
                cols = (W - P, META, 0, None) if first else (0, W, S * W - W + META, S * W - W)
                sp.wait_ge(tr_free, 2 * last_tile + 4)
                sp.sem_inc(carrier, 1)
                store_qk(*cols)
                sp.wait_ge(mla_a, S * UA + UV)
                sp.sem_inc(carrier, 1)
                store_v(cols[1], cols[2])
                sp.wait_ge(mla_rope, S + 1)
                sp.sem_inc(carrier, 1)
                store_m(*cols)

            load_x(0, 0)
            load_tab(0, 0)
            sp.dma_start(ident[:, :], t["ident"]).then_inc(setup, 16)
            sp.dma_start(g_mix[:, :], t["g_mix"]).then_inc(setup, 16)
            sp.dma_start(g_cq[:, :], t["g_cq"]).then_inc(setup, 16)
            sp.dma_start(g_ckv[:, :], t["g_ckv"]).then_inc(setup, 16)
            sp.dma_start(g_rows[:, :, :], t["g_rows"]).then_inc(setup, 16)
            sp.dma_start(inv_n[:, :], t["inv_n"]).then_inc(setup, 16)
            w_dram = t["w_in"].rearrange("(p c) n -> p c n", c=KC)
            for c in range(0, KC, 4):
                sp.dma_start(w_in[:, c:c + 4, :], w_dram[:, c:c + 4, :]).then_inc(w_loaded, 16)
            load_x(1, 1)
            load_tab(1, 1)
            sp.dma_start(w_qup[:, :, :], t["w_qup"].rearrange("(c p) n -> p c n", p=P)).then_inc(up_loaded, 16)
            sp.dma_start(w_kup[:, :], t["w_kup"]).then_inc(up_loaded, 16)
            sp.dma_start(w_vup[:, :], t["w_vup"]).then_inc(up_loaded, 16)
            load_cols(0)

            def loads(T, s):
                sp.wait_ge(xt_psum, T + 1)
                sp.sem_inc(carrier, 1)
                sp.wait_ge(std_ready, T + 1)
                sp.sem_inc(carrier, 1)
                load_x(T + 2, s)

            def rope_loads(T, s):
                sp.wait_ge(rope_ready, T + 1)
                sp.sem_inc(carrier, 1)
                load_tab(T + 2, s)

            loads(0, 0)
            rope_loads(0, 0)

            def body(g, last, first=False):
                for k in range(SUP):
                    T = g * SUP + 1 + k
                    n, s = load_n(g, k)
                    more = not (last and k >= SUP - 2)
                    if more:
                        loads(T, s)
                    if k == 1:
                        store(g, T - 2, first)
                        load_cols(g + 1)
                    if more:
                        rope_loads(T, s)

            body(0, False, first=True)
            with sp.Fori(1, SUPERS - 1) as g:
                body(g, False)
            body(SUPERS - 1, True)
            store(SUPERS, LAST)
            sp.wait_ge(stored_t, 16 * (META_T + STORES_T * SUPERS))
            sp.wait_ge(stored_m, 16 * (META_M + STORES_M * SUPERS))

        @block.scalar
        def _(act):
            def x_stats(T, n, s):
                act.drain()
                act.wait_ge(x_loaded[s], 16 * n + 16)
                nc.scalar.activation(junk[:, 0:D], x[:, s, :], ACT.Square, accum_out=ssq[:, s:s + 1])
                act.drain()
                nc.scalar.activation(std[:, s:s + 1], ssq[:, s:s + 1], ACT.Sqrt, scale=1.0 / D,
                                     bias=eps[:, 0:1]).then_inc(std_ready, 1)

            def z_out(T, s, first=False):
                act.wait_ge(z_psum, T + 1)
                act.wait_ge(rstd_ready, T + 1)
                if not first:
                    act.wait_ge(rope_ready, T)
                nc.scalar.activation(z[:, :], psZ[:, 0:D_IN], ACT.Copy, scale=rstd[:, s:s + 1]).then_inc(z_ready, 1)
                act.drain()
                nc.scalar.activation(sq[:, 0:ZKR], z[:, 0:ZKR], ACT.Square).then_inc(sq_ready, 1)

            def head_std(T):
                act.wait_ge(hs_ready, T + 1)
                nc.scalar.activation(hstd[:, :], hsn[:, :], ACT.Sqrt, bias=eps[:, 0:1]).then_inc(hstd_ready, 1)

            def tr_out(U, k):
                act.wait_ge(tr_psum, U + 1)
                cols = slice(k * P, k * P + P)
                nc.scalar.activation(qk_hi[:, :, cols], psR[:, 0:640].rearrange("p (a n) -> p a n", a=5),
                                     ACT.Copy)
                nc.scalar.activation(kr_hi[0:RD, cols], psR[0:RD, 1024:1152], ACT.Copy).then_inc(tr_hi, 1)

            def mla_out(S):
                for u, (kind, j) in enumerate(UNITS[:UA]):
                    act.wait_ge(mla_psum, S * UN + u + 1)
                    b = psX[:, u % 2, :]
                    if kind == "n":
                        nc.scalar.activation(qn_hi[:, j, :], b, ACT.Copy, scale=MSCALE).then_inc(mla_a, 1)
                    elif kind == "k":
                        nc.scalar.activation(mk_hi[:, j, :], b, ACT.Copy).then_inc(mla_a, 1)
                    else:
                        nc.scalar.activation(vst[:, j, PAIRS:, 0:VD],
                                             b.rearrange("p (h c) -> p h c", c=VD), ACT.Copy).then_inc(mla_a, 1)

            act.wait_ge(consts, 1)
            x_stats(0, 0, 0)
            z_out(0, 0, first=True)
            x_stats(1, 0, 1)
            head_std(0)

            def body(g, last):
                for k in range(SUP):
                    T = g * SUP + 1 + k
                    n, s = load_n(g, k)
                    z_out(T, s)
                    if not (last and k == SUP - 1):
                        n1, s1 = load_n(g, k + 1)
                        x_stats(T + 1, n1, s1)
                    if k == 1:
                        head_std(T)
                        mla_out(g)
                        act.wait_ge(stored_t, 16 * META_T + 16 * STORES_T * g)
                    tr_out(T - 1, (k - 1) % SUP)
                    if k != 1:
                        head_std(T)
                    if k == SUP - 1:
                        act.wait_ge(stored_m, 16 * META_M + 16 * STORES_M * g)

            with act.Fori(0, SUPERS - 1) as g:
                body(g, False)
            body(SUPERS - 1, True)
            tr_out(LAST, SUP - 1)
            mla_out(SUPERS)

        @block.vector
        def _(dve):
            def xt_out(T):
                dve.wait_ge(xt_psum, T + 1)
                nc.vector.tensor_tensor(xT[:, :, :], psX[:, :, :].rearrange("p b (c n) -> p (b c) n", n=P),
                                        g_mix[:, :].unsqueeze(2).broadcast_to([P, KC, P]),
                                        ALU.mult).then_inc(xt_ready, 1)

            def x_rstd(T, s):
                dve.wait_ge(std_ready, T + 1)
                nc.vector.reciprocal(rstd[:, s:s + 1], std[:, s:s + 1]).then_inc(rstd_ready, 1)

            def tr_out(U, k, s):
                dve.wait_ge(tr_psum, U + 1)
                dve.wait_ge(tr_hi, U + 1)
                cols = slice(k * P, k * P + P)
                nc.vector.tensor_tensor(cqT[:, :, cols], psR[:, 640:896].rearrange("p (a n) -> p a n", a=2),
                                        g_cq[:, :].unsqueeze(2).broadcast_to([P, 2, P]), ALU.mult)
                nc.vector.tensor_scalar(ckvT[:, cols], psR[:, 896:1024], g_ckv[:, 0:1], None, ALU.mult)
                for copy in range(2):
                    nc.vector.tensor_copy(vst[:, k, copy:PAIRS:2, 0:VD],
                                          trin[:, s, 1056:1184].rearrange("p (h c) -> p h c", c=VD))
                nc.vector.tensor_tensor(kr_lo[:, cols], psR[0:RD, 1024:1152], kr_hi[0:RD, cols].bitcast(F32),
                                        ALU.subtract)
                nc.vector.tensor_tensor(qk_lo[:, :, cols], psR[:, 0:640].rearrange("p (a n) -> p a n", a=5),
                                        qk_hi[:, :, cols].bitcast(F32), ALU.subtract).then_inc(tr_free, 2)

            def reduce(T, n, s):
                dve.drain()
                dve.wait_ge(sq_ready, T + 1)
                nc.vector.tensor_reduce(hss[:, 0:10], sq[:, 0:640].rearrange("p (h c) -> p h c", c=GD), AX.X, ALU.add)
                nc.vector.tensor_reduce(hss[:, 10:11], sq[:, ZCQ:ZCKV], AX.X, ALU.add)
                nc.vector.tensor_reduce(hss[:, 11:12], sq[:, ZCKV:ZKR], AX.X, ALU.add)
                dve.drain()
                nc.vector.tensor_tensor(hsn[:, :], hss[:, :], inv_n[:, :], ALU.mult).then_inc(hs_ready, 1)
                dve.wait_ge(tab_loaded[s], 16 * n + 16)
                for j in range(4):
                    nc.vector.scalar_tensor_tensor(tA[:, j, :], tab[:, s, (j % 2) * GD:(j % 2) * GD + GD],
                                                   GSCALE if j < 2 else 1.0, g_rows[:, j, :], ALU.mult, ALU.mult)

            def rope(T, s):
                dve.wait_ge(hstd_ready, T + 1)
                nc.vector.reciprocal(hr[:, :], hstd[:, :])
                dve.drain()
                heads = z[:, 0:640].rearrange("p (h c) -> p h c", c=GD)
                nc.vector.tensor_tensor(qn[:, :].rearrange("p (h c) -> p h c", c=GD), heads,
                                        hr[:, 0:10].unsqueeze(2).broadcast_to([P, 10, GD]), ALU.mult)
                nc.vector.tensor_scalar(trin[:, s, 640:896], z[:, ZCQ:ZCKV], hr[:, 10:11], None, ALU.mult)
                nc.vector.tensor_scalar(trin[:, s, 896:1024], z[:, ZCKV:ZKR], hr[:, 11:12], None, ALU.mult)
                nc.vector.tensor_copy(trin[:, s, 1056:1184], z[:, ZV:ZCQ])
                dve.drain()
                for lo, n, j in ((0, GH, 0), (512, GKV, 2)):
                    q3 = qn[:, lo:lo + n * GD].rearrange("p (h c) -> p h c", c=GD)
                    q4 = qn[:, lo:lo + n * GD].rearrange("p (h i two) -> p h i two", h=n, two=2)
                    s4 = qs[:, lo:lo + n * GD].rearrange("p (h i two) -> p h i two", h=n, two=2)
                    tb = tA[:, j + 1, :].rearrange("p (i two) -> p i two", two=2)
                    for e in range(2):
                        nc.vector.tensor_tensor(s4[:, :, :, e], q4[:, :, :, 1 - e],
                                                tb[:, :, e].unsqueeze(1).broadcast_to([P, n, GD // 2]), ALU.mult)
                    dst = trin[:, s, lo:lo + n * GD].rearrange("p (h c) -> p h c", c=GD)
                    nc.vector.tensor_tensor(dst, q3, tA[:, j, :].unsqueeze(1).broadcast_to([P, n, GD]), ALU.mult)
                kr = z[:, ZKR:D_IN].rearrange("p (i two) -> p i two", two=2)
                ks = kr_tmp[:, 0:RD].rearrange("p (i two) -> p i two", two=2)
                sn = tab[:, s, 160:192].rearrange("p (i two) -> p i two", two=2)
                for e in range(2):
                    nc.vector.tensor_tensor(ks[:, :, e], kr[:, :, 1 - e], sn[:, :, e], ALU.mult)
                nc.vector.tensor_tensor(kr_tmp[:, RD:2 * RD], z[:, ZKR:D_IN], tab[:, s, 128:160], ALU.mult)
                dve.drain()
                nc.vector.tensor_tensor(trin[:, s, 1024:1056], kr_tmp[:, 0:RD], kr_tmp[:, RD:2 * RD], ALU.add)
                nc.vector.tensor_tensor(trin[:, s, 0:640], trin[:, s, 0:640], qs[:, :], ALU.add).then_inc(rope_ready, 1)

            def mla_out(S):
                dve.wait_ge(col_loaded, 16 * S + 16)
                for u, (kind, j) in enumerate(UNITS):
                    if kind == "v":
                        continue
                    dve.wait_ge(mla_psum, S * UN + u + 1)
                    if u < UA:
                        dve.wait_ge(mla_a, S * UA + u + 1)
                    b = psX[:, u % 2, :]
                    if kind == "k":
                        i = nc.vector.tensor_tensor(mk_lo[:, j, :], b, mk_hi[:, j, :].bitcast(F32), ALU.subtract)
                    elif kind == "n":
                        i = nc.vector.scalar_tensor_tensor(qn_lo[:, j, :], b, MSCALE, qn_hi[:, j, :].bitcast(F32),
                                                           ALU.mult, ALU.subtract)
                    elif kind == "r":
                        i = nc.vector.tensor_tensor(rope_c[:, j, :], b, colc[:, 0, :], ALU.mult)
                    else:
                        i = nc.vector.tensor_tensor(rope_s[:, j, :], b, colc[:, 1, :], ALU.mult)
                    i.then_inc(mla_d, 1)

            def mla_rope_out():
                dve.drain()
                nc.vector.tensor_tensor(rope_c[:, :, :], rope_c[:, :, :], rope_s[:, :, :], ALU.add)
                dve.drain()
                nc.vector.tensor_copy(qr_hi[:, :, :], rope_c[:, :, :])
                dve.drain()
                nc.vector.tensor_tensor(qr_lo[:, :, :], rope_c[:, :, :], qr_hi[:, :, :].bitcast(F32),
                                        ALU.subtract).then_inc(mla_rope, 1)

            nc.vector.memset(eps[:, :], EPS)
            nc.vector.memset(ones_row[:, :].bitcast(F32), 1.0)
            nc.vector.memset(kr_hi[RD:RD + 1, :].bitcast(F32), 1.0)
            nc.vector.memset(vst[:, :, :, :], 1.0)
            nc.vector.memset(cqT[:, :, :], 0.0)
            nc.vector.memset(ckvT[:, :], 0.0).then_inc(consts, 1)
            dve.drain()
            dve.wait_ge(setup, 16 * 6)
            xt_out(0)
            x_rstd(0, 0)
            xt_out(1)
            x_rstd(1, 1)
            reduce(0, 0, 0)
            rope(0, 0)

            def body(g, last):
                for k in range(SUP):
                    T = g * SUP + 1 + k
                    n, s = load_n(g, k)
                    more = not (last and k == SUP - 1)
                    if k == 1:
                        reduce(T, n, s)
                        mla_out(g)
                        xt_out(T + 1)
                        x_rstd(T + 1, 1 - s)
                        mla_rope_out()
                        dve.wait_ge(stored_t, 16 * META_T + 16 * STORES_T * g)
                        tr_out(T - 1, k - 1, 1 - s)
                    else:
                        if more:
                            xt_out(T + 1)
                            x_rstd(T + 1, 1 - s)
                        tr_out(T - 1, (k - 1) % SUP, 1 - s)
                        reduce(T, n, s)
                    rope(T, s)
                    if k == SUP - 1:
                        dve.wait_ge(stored_m, 16 * META_M + 16 * STORES_M * g)

            with dve.Fori(0, SUPERS - 1) as g:
                body(g, False)
            body(SUPERS - 1, True)
            tr_out(LAST, SUP - 1, LAST % 2)
            mla_out(SUPERS)
            mla_rope_out()

        @block.tensor
        def _(pe):
            def xt(T, n, s, first=False):
                pe.wait_ge(x_loaded[s], 16 * n + 16)
                if not first:
                    pe.wait_ge(xt_ready, T)
                xv = x[:, s, :].rearrange("p (m c) -> p c m", c=KC)
                for c in range(KC):
                    i = nc.tensor.transpose(psX[:, c // 4, (c % 4) * P:(c % 4) * P + P], xv[:, c, :], ident[:, :])
                i.then_inc(xt_psum, 1)

            def zz(T, first=False):
                pe.wait_ge(xt_ready, T + 1)
                if not first:
                    pe.wait_ge(z_ready, T)
                for lo, hi in ((0, 512), (512, 1024), (1024, D_IN)):
                    for c in range(KC):
                        i = nc.tensor.matmul(psZ[:, lo:hi], xT[:, c, :], w_in[:, c, lo:hi],
                                             start=c == 0, stop=c == KC - 1)
                i.then_inc(z_psum, 1)

            def tr(U, s):
                pe.wait_ge(rope_ready, U + 1)
                pe.wait_ge(tr_free, 2 * U + 2)
                for j in range(9):
                    w = P if j < 8 else RD
                    i = nc.tensor.transpose(psR[0:w, j * P:j * P + P], trin[:, s, j * P:j * P + w], ident[:, :])
                i.then_inc(tr_psum, 1)

            def mla(S, U):
                pe.wait_ge(tr_free, 2 * U + 4)
                for u, (kind, j) in enumerate(UNITS):
                    if u >= 2:
                        if u - 2 < UV:
                            pe.wait_ge(mla_a, S * UA + u - 1)
                        else:
                            pe.wait_ge(mla_d, S * UD + u - 1 - UV)
                    b = psX[:, u % 2, :]
                    if kind == "v":
                        i = nc.tensor.matmul(b, ckvT[:, j * P:j * P + P], w_vup[:, :], start=True, stop=True)
                    elif kind == "k":
                        i = nc.tensor.matmul(b, w_kup[:, j * P:j * P + P], ckvT[:, :], start=True, stop=True)
                    else:
                        q = j + {"n": 0, "r": 4, "s": 6}[kind]
                        for c in range(2):
                            i = nc.tensor.matmul(b, w_qup[:, c, q * P:q * P + P], cqT[:, c, :],
                                                 start=c == 0, stop=c == 1)
                    i.then_inc(mla_psum, 1)

            pe.sem_inc(tr_free, 2)
            pe.wait_ge(setup, 16 * 6)
            xt(0, 0, 0, first=True)
            pe.wait_ge(w_loaded, 16 * 2)
            zz(0, first=True)
            xt(1, 0, 1)
            pe.wait_ge(up_loaded, 16 * 3)

            def body(g, last):
                for k in range(SUP):
                    T = g * SUP + 1 + k
                    n, s = load_n(g, k)
                    zz(T)
                    if k == 1:
                        mla(g, T - 2)
                        pe.wait_ge(mla_d, (g + 1) * UD)
                    if not (last and k == SUP - 1):
                        n1, s1 = load_n(g, k + 1)
                        xt(T + 1, n1, s1)
                    tr(T - 1, 1 - s)

            with pe.Fori(0, SUPERS - 1) as g:
                body(g, False)
            body(SUPERS - 1, True)
            tr(LAST, LAST % 2)
            mla(SUPERS, LAST)


def stage_attend(nc, t):
    with ExitStack() as ctx:
        def sb(name, shape, dt=F32):
            return ctx.enter_context(nc.sbuf_tensor("b_" + name, shape, dt))

        def ps(name, shape):
            return ctx.enter_context(nc.psum_tensor("b_" + name, shape, F32))

        def sem(name):
            return ctx.enter_context(nc.semaphore("b_" + name))

        q0 = [sb(f"q0_{s}", [P, TOK], F32R) for s in range(2)]
        q1 = [sb(f"q1_{s}", [P, TOK], F32R) for s in range(2)]
        k0 = [sb(f"k0_{s}", [P, KEYS], F32R) for s in range(2)]
        k1 = [sb(f"k1_{s}", [P, KEYS], F32R) for s in range(2)]
        v = [sb(f"v_{s}", [P, TILES + 1, VC]) for s in range(2)]
        v_hi = [sb(f"v_hi_{s}", [P, TILES, VC], F32R) for s in range(2)]
        v_lo = [sb(f"v_lo_{s}", [P, TILES, VC], F32R) for s in range(2)]
        v_meta = [sb(f"v_meta_{s}", [P, VC], F32R) for s in range(2)]
        M_HI, M_LO, M_HI2 = [slice(k, k + META) for k in (0, 32, 64)]
        ident = sb("ident", [P, P])
        zeros = sb("zeros", [P, 256])
        NP = 4
        POOL_EVERY = 8
        prob = sb("prob", [P, NP, W])
        p_hi = sb("p_hi", [P, NP, W], F32R)
        p_lo = sb("p_lo", [P, NP, W], F32R)
        oT = sb("oT", [VC, 2, W])
        rden = sb("rden", [P, SUP])
        ost = sb("ost", [P, 2, SUP, VD])
        mx_s = sb("mx_s", [P, DEC_SEQ // P, 4])
        mx_p = sb("mx_p", [P, SEQ // P, 2])
        nmx = sb("nmx", [P, TILES])
        nmx_m = sb("nmx_m", [P, TILES])
        nmxT = sb("nmxT", [TILES, P], F32R)

        psS = ps("psS", [P, 2, W])
        psM = ps("psM", [P, 2, 512])
        psK = ps("psK", [P, TILES * META])
        psO = ps("psO", [P, 2, W])
        psT = ps("psT", [P, 512])

        ident_loaded = sem("ident_loaded")
        cleared = sem("cleared")
        y_cleared = sem("y_cleared")
        ld_s = [sem("sample_loaded0"), sem("sample_loaded1")]
        ld_p = [sem("prompt_loaded0"), sem("prompt_loaded1")]
        s_psum = sem("s_psum")
        p_ready = sem("p_ready")
        lo_ready = sem("lo_ready")
        lo_ready_pool = sem("lo_ready_pool")
        v_ready = sem("v_ready")
        pv_done = sem("pv_done")
        ot_ready = sem("ot_ready")
        t_psum = sem("t_psum")
        t_free = sem("t_free")
        o_ready = sem("o_ready")
        o_stored = [sem("o_stored0"), sem("o_stored1")]
        m_psum = sem("m_psum")
        m_free = sem("m_free")
        k_psum = sem("k_psum")
        nmx_ready = sem("nmx_ready")
        row_made = sem("row_made")
        row_kept = sem("row_kept")
        row_loaded = sem("row_loaded")
        pool_carrier = sem("pool_carrier")
        carrier = sem("carrier")

        ITEMS = []
        BLOCKS_END = []
        for base, n in ((SEQ, DEC_SEQ), (0, SEQ)):
            for qc in range(base, base + n, W):
                ch = [(META + base + c * P, P, (base + c * P) // P) for c in range(n // P)] + [(0, META, TILES)]
                for c, (kc, kn, vc) in enumerate(ch):
                    ITEMS.append((qc, kc, kn, vc, c == 0, c == len(ch) - 1))
                BLOCKS_END.append((len(ITEMS) - 1, qc))
        NI = len(ITEMS)
        NB = len(BLOCKS_END)
        END_OF = {j: b for b, (j, _) in enumerate(BLOCKS_END)}
        SAMPLE_LAST = BLOCKS_END[DEC_SEQ // W - 1][0]
        UNITS = [(SEQ // P + i, META + SEQ + u * 512, u) for i in range(DEC_SEQ // P) for u in range(4)]
        UNITS += [(i, META + u * 512, u) for i in range(SEQ // P) for u in range(2)]
        NU = len(UNITS)
        R = 4
        SPAN = 72
        UNIT_AT = {}
        for u in range(NU):
            UNIT_AT.setdefault(R + u * SPAN // NU, []).append(u)
        META_AT, ROW_AT = R + SPAN, R + SPAN + 3
        ON_POOL = [j for j in range(24, NI - 3) if j % POOL_EVERY == 0 and ITEMS[j][2] == P]
        NUSE = NB + 1
        ROW_USE = sum(j + 5 < ROW_AT for j, _ in BLOCKS_END)
        HEADS = GH + MH

        def loads_seen(i, gqa, part):
            v_loads = 1 if part == "s" else 2
            if gqa:
                return 16 * (6 + v_loads) * (i + 1)
            return 16 * (8 + v_loads) * (i + 1) - 16 * 2 * (GH // 2)

        def use(h, b, last):
            return h * NUSE + 1 + b + (1 if b >= ROW_USE and not last else 0)

        block = ctx.enter_context(nc.Block())

        def o_store(engine, h, b):
            engine.wait_ge(o_ready, h * NB + b + 1)
            if engine is not nc.scalar:
                engine.sem_inc(carrier, 1)
            qc = BLOCKS_END[b][1]
            engine.dma_start(t["O"].rearrange("(j p) c -> p j c", p=P)[:, qc // P:qc // P + SUP, bass.ds(h * VD, VD)],
                             ost[:, b % 2, :, :]).then_inc(o_stored[b % 2], 16)

        def over_heads(engine, head):
            def pair(i, lasts):
                for s in range(2):
                    gqa, nxt, last = lasts[s]
                    head(2 * i + s, i, s, gqa, nxt, last)
            with engine.Fori(0, GH // 2 - 1) as i:
                pair(i, [(True, True, False)] * 2)
            pair(GH // 2 - 1, [(True, True, False), (True, False, False)])
            with engine.Fori(GH // 2, HEADS // 2 - 1) as i:
                pair(i, [(False, False, False)] * 2)
            pair(HEADS // 2 - 1, [(False, False, False), (False, None, True)])

        @block.sync
        def _(sp):
            def load(h, i, s, gqa, part):
                if part == "s":
                    q, k, sm = slice(SEQ, TOK), slice(META + SEQ, KEYS), ld_s[s]
                else:
                    q, k, sm = slice(0, SEQ), slice(0, META + SEQ), ld_p[s]

                def dma(dst, src):
                    sp.dma_start(dst.bitcast(F32), src).then_inc(sm, 16)

                if gqa:
                    rq, rk = bass.ds(h * GD, GD), bass.ds(i * GD, GD)
                    dma(q0[s][0:GD, q], t["QGH"][rq, q])
                    dma(q0[s][GD:P, q], t["QGL"][rq, q])
                    dma(q1[s][0:GD, q], t["QGH"][rq, q])
                    dma(k0[s][0:GD, k], t["KGH"][rk, k])
                    dma(k0[s][GD:P, k], t["KGH"][rk, k])
                    dma(k1[s][0:GD + 1, k], t["KGL"].rearrange("g r n -> (g r) n")[bass.ds(i * (GD + 1), GD + 1), k])
                    vh = i
                else:
                    m = h - GH
                    rk, rr = bass.ds(m * ND, ND), bass.ds(m * RD, RD)
                    dma(q0[s][0:ND, q], t["QNH"][rk, q])
                    dma(q0[s][ND:QKD, q], t["QRH"][rr, q])
                    dma(q1[s][0:ND, q], t["QNL"][rk, q])
                    dma(q1[s][ND:QKD, q], t["QRL"][rr, q])
                    dma(k0[s][0:ND, k], t["KMH"][rk, k])
                    dma(k0[s][ND:QKD + 1, k], t["KRH"][:, k])
                    dma(k1[s][0:ND, k], t["KML"][rk, k])
                    dma(k1[s][ND:QKD, k], t["KRL"][:, k])
                    vh = m + PAIRS
                vcol = bass.ds(vh * VC, VC)
                if part == "s":
                    sp.dma_start(v[s][:, SEQ // P:TILES, :],
                                 t["V"][META + SEQ:KEYS, vcol].rearrange("(c p) d -> p c d", p=P)).then_inc(sm, 16)
                else:
                    sp.dma_start(v[s][:, 0:SEQ // P, :],
                                 t["V"][META:META + SEQ, vcol].rearrange("(c p) d -> p c d", p=P)).then_inc(sm, 16)
                    sp.dma_start(v[s][0:META, TILES, :], t["V"][0:META, vcol]).then_inc(sm, 16)

            def row(n, s, gqa):
                sp.wait_ge(row_made, n + 1)
                sp.dma_start(t["MX"].rearrange("(a b) -> a b", b=P), nmxT[:, :].bitcast(F32)).then_inc(row_kept, 16)
                sp.wait_ge(row_kept, 16 * n + 32)
                dst = q1[s][GD:GD + 1, :] if gqa else q0[s][QKD:QKD + 1, :]
                sp.dma_start(dst.bitcast(F32), t["MX"].rearrange("(a b) -> a b", a=1)).then_inc(row_loaded, 16)
                sp.wait_ge(row_loaded, 16 * n + 16)
                sp.sem_inc(carrier, 1)

            sp.dma_start(ident[:, :], t["ident"]).then_inc(ident_loaded, 16)
            sp.wait_ge(cleared, 1)
            for s in range(2):
                load(s, 0, s, True, "s")
                load(s, 0, s, True, "p")
            row(0, 0, True)

            def head(h, i, s, gqa, nxt, last):
                if last:
                    return
                more = not isinstance(h, int) or h + 2 < HEADS
                kind = gqa if not isinstance(h, int) else h + 2 < GH
                if more:
                    sp.wait_ge(pv_done, h * NI + SAMPLE_LAST + 1 + NP)
                    load(h + 2, i + 1, s, kind, "s")
                row(h + 1, 1 - s, nxt)
                if more:
                    sp.wait_ge(pv_done, h * NI + NI + NP)
                    sp.sem_inc(carrier, 1)
                    load(h + 2, i + 1, s, kind, "p")
                o_store(sp, h, NB - 1)

            over_heads(sp, head)

        @block.gpsimd
        def _(pool):
            def split(n, i, s, gqa):
                for sm, part, chunks in ((ld_s[s], "s", [slice(SEQ // P, TILES)]),
                                         (ld_p[s], "p", [slice(0, SEQ // P)])):
                    pool.drain()
                    pool.wait_ge(sm, loads_seen(i, gqa, part))
                    pool.sem_inc(pool_carrier, 1)
                    for c in chunks:
                        nc.gpsimd.tensor_copy(v_hi[s][:, c, :], v[s][:, c, :])
                    if part == "p":
                        for rows in (M_HI, M_HI2):
                            pool.drain()
                            nc.gpsimd.tensor_copy(v_meta[s][rows, :], v[s][0:META, TILES, :])
                    pool.drain()
                    if part == "p":
                        nc.gpsimd.tensor_tensor(v_meta[s][M_LO, :], v[s][0:META, TILES, :],
                                                v_meta[s][M_HI, :].bitcast(F32), ALU.subtract)
                        pool.drain()
                    for c in chunks:
                        m = nc.gpsimd.tensor_tensor(v_lo[s][:, c, :], v[s][:, c, :], v_hi[s][:, c, :].bitcast(F32),
                                                    ALU.subtract)
                    m.then_inc(v_ready, 1)

            pool.wait_ge(cleared, 1)
            split(0, 0, 0, True)

            def head(h, i, s, gqa, nxt, last):
                if not last:
                    split(h + 1, i + s, 1 - s, nxt)
                for j in ON_POOL:
                    kn, slot = ITEMS[j][2], (s * NI + j) % NP
                    pool.wait_ge(p_ready, h * NI + j + 3)
                    nc.gpsimd.tensor_tensor(p_lo[:, slot, :], prob[0:kn, slot, :], p_hi[0:kn, slot, :].bitcast(F32),
                                            ALU.subtract).then_inc(lo_ready_pool, 1)

            over_heads(pool, head)

        @block.scalar
        def _(act):
            def exp(h, s, j):
                _, _, kn, _, _, _ = ITEMS[j]
                act.wait_ge(s_psum, h * NI + j + 1)
                act.wait_ge(pv_done, h * NI + j + 1)
                nc.scalar.activation(p_hi[0:kn, (s * NI + j) % NP, :], psS[0:kn, j % 2, :], ACT.Exp)
                if kn == META:
                    nc.scalar.activation(p_hi[M_LO, (s * NI + j) % NP, :], psS[0:kn, j % 2, :], ACT.Exp)
                nc.scalar.activation(prob[0:kn, (s * NI + j) % NP, :], psS[0:kn, j % 2, :], ACT.Exp).then_inc(p_ready, 1)

            def o_out(h, b):
                act.wait_ge(pv_done, h * NI + BLOCKS_END[b][0] + 1 + NP)
                nc.scalar.activation(oT[:, b % 2, :], psO[0:VC, b % 2, :], ACT.Copy).then_inc(ot_ready, 1)

            act.sem_inc(pv_done, NP)
            act.wait_ge(cleared, 1)
            for j in range(R):
                exp(0, 0, j)
            for c in range(D // 256):
                act.dma_start(t["Y"].rearrange("(b p) d -> p b d", p=P)[:, BLOCKS_SURE:, c * 256:c * 256 + 256],
                              zeros[:, :].unsqueeze(1).broadcast_to([P, BLOCKS - BLOCKS_SURE, 256])).then_inc(y_cleared, 16)

            def head(h, i, s, gqa, nxt, last):
                for j in range(R, NI):
                    exp(h, s, j)
                    if j - 3 in END_OF:
                        o_out(h, END_OF[j - 3])
                    if j - 8 in END_OF:
                        o_store(act, h, END_OF[j - 8])
                if not last:
                    for j in range(R - 1):
                        exp(h + 1, 1 - s, j)
                o_out(h, NB - 1)
                if not last:
                    exp(h + 1, 1 - s, R - 1)

            over_heads(act, head)
            o_store(act, HEADS - 1, NB - 1)
            for b in range(2):
                act.wait_ge(o_stored[b], 16 * (HEADS * NB // 2 + 1))
            act.wait_ge(y_cleared, 16 * (D // 256))

        @block.vector
        def _(dve):
            def remainder(h, s, j):
                if j in ON_POOL:
                    return
                kn, slot = ITEMS[j][2], (s * NI + j) % NP
                dve.wait_ge(p_ready, h * NI + j + 3)
                out = p_hi[M_HI2, slot, :] if kn == META else p_lo[:, slot, :]
                nc.vector.tensor_tensor(out, prob[0:kn, slot, :], p_hi[0:kn, slot, :].bitcast(F32),
                                        ALU.subtract).then_inc(lo_ready, 1)

            def unit(n, u):
                q, _, g = UNITS[u]
                dve.wait_ge(m_psum, n * NU + u + 1)
                dst = mx_s[:, q - SEQ // P, g:g + 1] if q >= SEQ // P else mx_p[:, q, g:g + 1]
                nc.vector.tensor_reduce(dst, psM[:, u % 2, :], AX.X, ALU.max).then_inc(m_free, 1)

            def finish(n):
                dve.drain()
                dve.wait_ge(k_psum, n + 1)
                nc.vector.tensor_reduce(nmx_m[:, :], psK[:, :].rearrange("p (a b) -> p a b", b=META), AX.X, ALU.max,
                                        negate=True)
                nc.vector.tensor_reduce(nmx[:, SEQ // P:], mx_s[:, :, :], AX.X, ALU.max, negate=True)
                nc.vector.tensor_reduce(nmx[:, 0:SEQ // P], mx_p[:, :, :], AX.X, ALU.max, negate=True)
                dve.drain()
                nc.vector.tensor_tensor(nmx[:, :], nmx[:, :], nmx_m[:, :], ALU.min).then_inc(nmx_ready, 1)

            def row(n, u):
                dve.wait_ge(t_psum, u + 1)
                dve.wait_ge(row_kept, 16 * n + 16)
                nc.vector.tensor_copy(nmxT[:, :], psT[0:TILES, 260:388])
                dve.drain().then_inc(row_made, 1)
                dve.drain().then_inc(t_free, 1)

            def normalise(h, b, u):
                dve.drain()
                dve.wait_ge(t_psum, u + 1)
                tv = psT[:, 0:SUP * VC].rearrange("p (j c) -> p j c", c=VC)
                nc.vector.reciprocal(rden[:, :].unsqueeze(2), tv[:, :, VD:VC])
                dve.drain()
                dve.wait_ge(o_stored[b % 2], 16 * (h * (NB // 2) + b // 2 + 1))
                nc.vector.tensor_tensor(ost[:, b % 2, :, :], tv[:, :, 0:VD],
                                        rden[:, :].unsqueeze(2).broadcast_to([P, SUP, VD]), ALU.mult).then_inc(o_ready, 1)
                dve.drain().then_inc(t_free, 1)

            for b in range(2):
                dve.sem_inc(o_stored[b], 16)
            dve.sem_inc(row_kept, 16)
            nc.vector.memset(zeros[:, :], 0.0)
            nc.vector.memset(p_hi[:, :, :].bitcast(F32), 0.0)
            nc.vector.memset(p_lo[:, :, :].bitcast(F32), 0.0)
            for s in range(2):
                nc.vector.memset(v_meta[s][:, :].bitcast(F32), 0.0)
            dve.drain().then_inc(cleared, 1)
            for u in range(NU):
                unit(0, u)
            finish(0)
            row(0, 0)
            for j in range(R - 1):
                remainder(0, 0, j)

            def head(h, i, s, gqa, nxt, last):
                for j in range(R, NI):
                    remainder(h, s, j - 1)
                    if not last:
                        for u in UNIT_AT.get(j, ()):
                            unit(h + 1, u)
                        if j == META_AT:
                            finish(h + 1)
                        if j == ROW_AT:
                            row(h + 1, h * NUSE + 1 + ROW_USE)
                    if j - 6 in END_OF:
                        normalise(h, END_OF[j - 6], use(h, END_OF[j - 6], last))
                remainder(h, s, NI - 1)
                if not last:
                    for j in range(R - 1):
                        remainder(h + 1, 1 - s, j)
                normalise(h, NB - 1, use(h, NB - 1, last))

            over_heads(dve, head)

        @block.tensor
        def _(pe):
            def qk(h, s, gqa, j):
                qc, kc, kn, _, _, _ = ITEMS[j]
                pe.wait_ge(p_ready, h * NI + j + 1)
                q, k = slice(qc, qc + W), slice(kc, kc + kn)
                passes = ([(k0, q0, P), (k1, q1, GD + 1)] if gqa else
                          [(k0, q0, QKD + 1), (k0, q1, QKD), (k1, q0, QKD)])
                for n, (kk, qq, r) in enumerate(passes):
                    m = nc.tensor.matmul(psS[0:kn, j % 2, :], kk[s][0:r, k], qq[s][0:r, q],
                                         start=n == 0, stop=n == len(passes) - 1)
                m.then_inc(s_psum, 1)

            def pv(h, s, j, b):
                _, _, _, vc, first, last = ITEMS[j]
                if j == 0:
                    pe.wait_ge(v_ready, 2 * h + 1)
                if j == BLOCKS_END[0][0]:
                    pe.wait_ge(v_ready, 2 * h + 2)
                before = sum(k < j for k in ON_POOL)
                if j in ON_POOL:
                    pe.wait_ge(lo_ready_pool, h * len(ON_POOL) + before + 1)
                else:
                    pe.wait_ge(lo_ready, h * (NI - len(ON_POOL)) + j - before + 1)
                if first:
                    pe.wait_ge(ot_ready, h * NB + b + 1)
                slot = (s * NI + j) % NP
                if ITEMS[j][2] == META:
                    nc.tensor.matmul(psO[0:VC, b % 2, :], v_meta[s][:, :], p_hi[:, slot, :],
                                     start=first, stop=last).then_inc(pv_done, 1)
                    return
                for n, (vv, pp) in enumerate(((v_hi, p_hi), (v_lo, p_hi), (v_hi, p_lo))):
                    m = nc.tensor.matmul(psO[0:VC, b % 2, :], vv[s][:, vc, :], pp[:, slot, :],
                                         start=first and n == 0, stop=last and n == 2)
                m.then_inc(pv_done, 1)

            def unit(n, s, gqa, u):
                q, kc, _ = UNITS[u]
                pe.wait_ge(m_free, n * NU + u + 1)
                r = P if gqa else QKD
                nc.tensor.matmul(psM[:, u % 2, :], q0[s][0:r, q * P:q * P + P], k0[s][0:r, kc:kc + 512],
                                 start=True, stop=True).then_inc(m_psum, 1)

            def meta(n, s, gqa):
                r = P if gqa else QKD
                for q in range(TILES):
                    m = nc.tensor.matmul(psK[:, q * META:q * META + META], q0[s][0:r, q * P:q * P + P],
                                         k0[s][0:r, 0:META], start=True, stop=True)
                m.then_inc(k_psum, 1)

            def row(n, u):
                pe.wait_ge(nmx_ready, n + 1)
                pe.wait_ge(t_free, u + 1)
                nc.tensor.transpose(psT[0:TILES, 260:388], nmx[:, :], ident[:, :]).then_inc(t_psum, 1)

            def o_turn(h, b, u):
                pe.wait_ge(ot_ready, h * NB + b + 3)
                pe.wait_ge(t_free, u + 1)
                for c in range(SUP):
                    m = nc.tensor.transpose(psT[:, c * VC:c * VC + VC], oT[:, b % 2, c * P:c * P + P], ident[0:VC, 0:VC])
                m.then_inc(t_psum, 1)

            pe.sem_inc(p_ready, 2)
            pe.sem_inc(ot_ready, 2)
            pe.sem_inc(m_free, 2)
            pe.sem_inc(t_free, 1)
            pe.wait_ge(ident_loaded, 16)
            pe.wait_ge(ld_s[0], loads_seen(0, True, "s"))
            for u in range(NU):
                if UNITS[u][0] == 0 and UNITS[u][2] == 0:
                    pe.wait_ge(ld_p[0], loads_seen(0, True, "p"))
                unit(0, 0, True, u)
            meta(0, 0, True)
            row(0, 0)
            pe.wait_ge(row_loaded, 16)
            for j in range(R):
                qk(0, 0, True, j)
                if j >= 2:
                    pv(0, 0, j - 2, 0)

            def head(h, i, s, gqa, nxt, last):
                block_of = [sum(e < j for e, _ in BLOCKS_END) for j in range(NI)]
                i1 = i + s
                for j in range(R, NI):
                    qk(h, s, gqa, j)
                    if not last:
                        for u in UNIT_AT.get(j, ()):
                            if u == 0:
                                pe.wait_ge(ld_s[1 - s], loads_seen(i1, nxt, "s"))
                            if UNITS[u][0] == 0 and UNITS[u][2] == 0:
                                pe.wait_ge(ld_p[1 - s], loads_seen(i1, nxt, "p"))
                            unit(h + 1, 1 - s, nxt, u)
                        if j == META_AT:
                            meta(h + 1, 1 - s, nxt)
                        if j == ROW_AT:
                            row(h + 1, h * NUSE + 1 + ROW_USE)
                    pv(h, s, j - 2, block_of[j - 2])
                    if j - 5 in END_OF:
                        o_turn(h, END_OF[j - 5], use(h, END_OF[j - 5], last))
                if not last:
                    pe.wait_ge(row_loaded, 16 * h + 32)
                for j in range(R):
                    if not last:
                        qk(h + 1, 1 - s, nxt, j)
                    if j < 2:
                        pv(h, s, NI - 2 + j, NB - 1)
                    elif not last:
                        pv(h + 1, 1 - s, j - 2, 0)
                o_turn(h, NB - 1, use(h, NB - 1, last))

            over_heads(pe, head)


def stage_mix_out(nc, t, logits):
    with ExitStack() as ctx:
        def sb(name, shape, dt=F32):
            return ctx.enter_context(nc.sbuf_tensor("c_" + name, shape, dt))

        def ps(name, shape):
            return ctx.enter_context(nc.psum_tensor("c_" + name, shape, F32))

        def sem(name):
            return ctx.enter_context(nc.semaphore("c_" + name))

        NR = G + E
        H = D // 2
        w_raw = sb("w_raw", [P, KC, D])
        w_hi = sb("w_hi", [P, KC, D], F32R)
        w_lo = sb("w_lo", [P, KC, D], F32R)
        w_r = sb("w_r", [P, KC, NR])
        b_r = sb("b_r", [NR, 1])
        g_out = sb("g_out", [P, KC])
        g_ffn = sb("g_ffn", [P, D])
        ident = sb("ident", [P, P])
        eps = sb("eps", [P, 1])
        o = sb("o", [P, 2, D])
        x = sb("x", [P, 2, D])
        junk = sb("junk", [P, D])
        oss = sb("oss", [P, 2, 2])
        ostd = sb("ostd", [P, 2, 2])
        orr = sb("orr", [P, 2, 2])
        os_ = sb("os", [P, 2, D])
        oT = sb("oT", [P, KC, P])
        oT_hi = sb("oT_hi", [P, 2, KC, P], F32R)
        oT_lo = sb("oT_lo", [P, 2, KC, P], F32R)
        h2 = sb("h2", [P, 2, D])
        hss = sb("hss", [P, 2])
        hstd = sb("hstd", [P, 2])
        hr = sb("hr", [P, 2])
        u2 = sb("u2", [P, 2, D])
        uT = sb("uT", [P, KC, P])
        lg = sb("lg", [P, P])

        psA = ps("psA", [P, 2, 512])
        psY = ps("psY", [P, 2, 512])
        psU = ps("psU", [P, 2, 512])
        psR = ps("psR", [NR, 512])
        psL = ps("psL", [P, 512])

        w_loaded, small_loaded = [sem("w_loaded0"), sem("w_loaded1")], sem("small_loaded")
        w_hi_ready, w_lo_ready = sem("w_hi_ready"), sem("w_lo_ready")
        eps_ready = sem("eps_ready")
        o_loaded = [sem("o_loaded0"), sem("o_loaded1")]
        x_loaded = [sem("x_loaded0"), sem("x_loaded1")]
        ostd_ready, orr_ready, os_ready = sem("ostd_ready"), sem("orr_ready"), sem("os_ready")
        oT_psum, oT_ready, hi_ready, lo_ready = sem("oT_psum"), sem("oT_ready"), sem("hi_ready"), sem("lo_ready")
        y_psum, h2_ready, hstd_ready = sem("y_psum"), sem("h2_ready"), sem("hstd_ready")
        u2_ready, uT_psum, uT_ready = sem("u2_ready"), sem("uT_psum"), sem("uT_ready")
        r_psum, lg_ready, l_psum, l_ready = sem("r_psum"), sem("lg_ready"), sem("l_psum"), sem("l_ready")
        h_stored = [sem("h_stored0"), sem("h_stored1")]

        N = TILES
        block = ctx.enter_context(nc.Block())

        def over_tiles(engine, body):
            for j in range(2):
                for s in range(2):
                    body(2 * j + s, j, s)
            with engine.Fori(2, N // 2 - 2) as j:
                for s in range(2):
                    body(2 * j + s, j, s)
            for j in (N // 2 - 2, N // 2 - 1):
                for s in range(2):
                    body(2 * j + s, j, s)

        def at_least(T, n):
            return not isinstance(T, int) or T >= n

        def below(T, n):
            return not isinstance(T, int) or T < n

        @block.sync
        def _(sp):
            def load_o(T, s):
                sp.dma_start(o[:, s, :], t["O"][bass.ds(T * P, P), :]).then_inc(o_loaded[s], 16)

            def load_x(T, s):
                sp.dma_start(x[:, s, :], t["xall"][bass.ds(T * P + P, P), :]).then_inc(x_loaded[s], 16)

            sp.dma_start(ident[:, :], t["ident"]).then_inc(small_loaded, 16)
            sp.dma_start(g_out[:, :], t["g_out"]).then_inc(small_loaded, 16)
            sp.dma_start(w_r[:, :, :], t["w_r"].rearrange("(p c) n -> p c n", c=KC)).then_inc(small_loaded, 16)
            sp.dma_start(b_r[:, :], t["b_r"]).then_inc(small_loaded, 16)
            sp.dma_start(g_ffn[:, :], t["g_ffn"]).then_inc(small_loaded, 16)
            load_o(0, 0)
            load_o(1, 1)
            for part in range(2):
                c = slice(part * KC // 2, (part + 1) * KC // 2)
                sp.dma_start(w_raw[:, c, :], t["w_out"].rearrange("(p c) n -> p c n", c=KC)[:, c, :]).then_inc(w_loaded[part], 16)
            load_x(0, 0)
            load_x(1, 1)
            sp.wait_ge(os_ready, 1)
            load_o(2, 0)

            def store(T, j, s):
                sp.wait_ge(u2_ready, T + 1)
                sp.dma_start(t["H2"][bass.ds(T * P, P), :], h2[:, s, :]).then_inc(h_stored[s], 16)
                sp.dma_start(t["U2"][bass.ds(T * P, P), :], u2[:, s, :]).then_inc(h_stored[s], 16)

            def body(T, j, s):
                if at_least(T, 1):
                    if below(T, N - 1):
                        sp.wait_ge(h2_ready, T)
                        load_x(T + 1, 1 - s)
                    store(T - 1, j, 1 - s)
                if below(T, N - 3):
                    sp.wait_ge(os_ready, T + 2)
                    load_o(T + 3, 1 - s)

            over_tiles(sp, body)
            store(N - 1, 0, 1)
            for s in range(2):
                sp.wait_ge(h_stored[s], 32 * (N // 2))

        @block.scalar
        def _(act):
            def o_scaled(T, j, s, again=True):
                act.drain()
                if again:
                    act.wait_ge(oT_psum, T - 1)
                act.wait_ge(o_loaded[s], 16 * j + 16)
                for k in range(2):
                    nc.scalar.activation(junk[:, k * H:k * H + H], o[:, s, k * H:k * H + H], ACT.Square,
                                         accum_out=oss[:, s, k:k + 1])
                act.drain()
                nc.scalar.activation(ostd[:, s, :], oss[:, s, :], ACT.Sqrt, scale=1.0 / H,
                                     bias=eps[:, 0:1]).then_inc(ostd_ready, 1)
                act.wait_ge(orr_ready, T + 1)
                for k in range(2):
                    i = nc.scalar.activation(os_[:, s, k * H:k * H + H], o[:, s, k * H:k * H + H], ACT.Copy,
                                             scale=orr[:, s, k:k + 1])
                i.then_inc(os_ready, 1)

            def oT_rounded(T, s):
                act.wait_ge(oT_ready, T + 1)
                nc.scalar.activation(oT_hi[:, s, :, :], oT[:, :, :], ACT.Copy).then_inc(hi_ready, 1)

            def h_stats(T, s):
                act.drain()
                act.wait_ge(h2_ready, T + 1)
                nc.scalar.activation(junk[:, :], h2[:, s, :], ACT.Square, accum_out=hss[:, s:s + 1])
                act.drain()
                nc.scalar.activation(hstd[:, s:s + 1], hss[:, s:s + 1], ACT.Sqrt, scale=1.0 / D,
                                     bias=eps[:, 0:1]).then_inc(hstd_ready, 1)

            act.wait_ge(eps_ready, 1)
            o_scaled(0, 0, 0, again=False)
            o_scaled(1, 0, 1, again=False)
            for part in range(2):
                c = slice(part * KC // 2, (part + 1) * KC // 2)
                act.wait_ge(w_loaded[part], 16)
                nc.scalar.activation(w_hi[:, c, :], w_raw[:, c, :], ACT.Copy).then_inc(w_hi_ready, 1)
            oT_rounded(0, 0)

            def body(T, j, s):
                if at_least(T, 1):
                    h_stats(T - 1, 1 - s)
                if below(T, N - 1):
                    oT_rounded(T + 1, 1 - s)
                if below(T, N - 2):
                    o_scaled(T + 2, j + 1, s)

            over_tiles(act, body)
            h_stats(N - 1, 1)

        @block.vector
        def _(dve):
            def o_recip(T, s):
                dve.wait_ge(ostd_ready, T + 1)
                nc.vector.reciprocal(orr[:, s, :], ostd[:, s, :]).then_inc(orr_ready, 1)

            def oT_out(T):
                dve.drain()
                dve.wait_ge(oT_psum, T + 1)
                nc.vector.tensor_tensor(oT[:, :, :], psA[:, :, :].rearrange("p b (c n) -> p (b c) n", n=P),
                                        g_out[:, :].unsqueeze(2).broadcast_to([P, KC, P]), ALU.mult).then_inc(oT_ready, 1)

            def oT_rest(T, s):
                dve.wait_ge(hi_ready, T + 1)
                nc.vector.tensor_tensor(oT_lo[:, s, :, :], oT[:, :, :], oT_hi[:, s, :, :].bitcast(F32),
                                        ALU.subtract).then_inc(lo_ready, 1)

            def h_out(T, j, s):
                dve.wait_ge(y_psum, T + 1)
                dve.wait_ge(x_loaded[s], 16 * j + 16)
                if at_least(T, 2):
                    dve.wait_ge(h_stored[s], 32 * j)
                nc.vector.tensor_tensor(h2[:, s, :], psY[:, :, :].rearrange("p b n -> p (b n)"), x[:, s, :],
                                        ALU.add).then_inc(h2_ready, 1)

            def u_out(T, s):
                dve.wait_ge(hstd_ready, T + 1)
                nc.vector.reciprocal(hr[:, s:s + 1], hstd[:, s:s + 1])
                dve.drain()
                nc.vector.scalar_tensor_tensor(u2[:, s, :], h2[:, s, :], hr[:, s:s + 1], g_ffn[:, :],
                                               ALU.mult, ALU.mult).then_inc(u2_ready, 1)

            def uT_out(T):
                dve.wait_ge(uT_psum, T + 1)
                nc.vector.tensor_copy(uT[:, :, :], psU[:, :, :].rearrange("p b (c n) -> p (b c) n", n=P)).then_inc(uT_ready, 1)

            def lg_out(T):
                dve.wait_ge(r_psum, T + 1)
                nc.vector.tensor_scalar(lg[0:NR, :], psR[:, 0:P], b_r[:, 0:1], None, ALU.add).then_inc(lg_ready, 1)

            def l_out(T):
                dve.wait_ge(l_psum, T + 1)
                nc.vector.tensor_copy(logits[:, bass.ds(T * NR, NR)], psL[:, 0:NR]).then_inc(l_ready, 1)

            nc.vector.memset(lg[:, :], 0.0)
            nc.vector.memset(eps[:, :], EPS).then_inc(eps_ready, 1)
            dve.drain()
            dve.wait_ge(small_loaded, 16 * 5)
            o_recip(0, 0)
            o_recip(1, 1)
            for part in range(2):
                c = slice(part * KC // 2, (part + 1) * KC // 2)
                dve.wait_ge(w_hi_ready, part + 1)
                nc.vector.tensor_tensor(w_lo[:, c, :], w_raw[:, c, :], w_hi[:, c, :].bitcast(F32),
                                        ALU.subtract).then_inc(w_lo_ready, 1)
            oT_out(0)
            oT_rest(0, 0)

            def body(T, j, s):
                if at_least(T, 1):
                    h_out(T - 1, j - 1 if s == 0 else j, 1 - s)
                if at_least(T, 2):
                    uT_out(T - 2)
                if below(T, N - 1):
                    oT_out(T + 1)
                if at_least(T, 1):
                    u_out(T - 1, 1 - s)
                if below(T, N - 1):
                    oT_rest(T + 1, 1 - s)
                if below(T, N - 2):
                    o_recip(T + 2, s)
                if at_least(T, 3):
                    l_out(T - 3)
                if at_least(T, 2):
                    lg_out(T - 2)

            over_tiles(dve, body)
            h_out(N - 1, N // 2 - 1, 1)
            uT_out(N - 2)
            u_out(N - 1, 1)
            l_out(N - 3)
            lg_out(N - 2)
            uT_out(N - 1)
            l_out(N - 2)
            lg_out(N - 1)
            l_out(N - 1)

        @block.tensor
        def _(pe):
            def o_turn(T, s, first=False):
                pe.wait_ge(os_ready, T + 1)
                if not first:
                    pe.wait_ge(oT_ready, T)
                ov = os_[:, s, :].rearrange("p (m c) -> p c m", c=KC)
                for c in range(KC):
                    i = nc.tensor.transpose(psA[:, c // 4, (c % 4) * P:(c % 4) * P + P], ov[:, c, :], ident[:, :])
                i.then_inc(oT_psum, 1)

            def y_of(T, s):
                pe.wait_ge(lo_ready, T + 1)
                if at_least(T, 1):
                    pe.wait_ge(h2_ready, T)
                for b in range(2):
                    n = 0
                    for c in range(KC):
                        for a, w in ((oT_hi, w_hi), (oT_lo, w_hi), (oT_hi, w_lo)):
                            i = nc.tensor.matmul(psY[:, b, :], a[:, s, c, :], w[:, c, b * 512:b * 512 + 512],
                                                 start=n == 0, stop=n == 3 * KC - 1)
                            n += 1
                i.then_inc(y_psum, 1)

            def u_turn(T, s):
                pe.wait_ge(u2_ready, T + 1)
                if at_least(T, 1):
                    pe.wait_ge(uT_ready, T)
                uv = u2[:, s, :].rearrange("p (m c) -> p c m", c=KC)
                for c in range(KC):
                    i = nc.tensor.transpose(psU[:, c // 4, (c % 4) * P:(c % 4) * P + P], uv[:, c, :], ident[:, :])
                i.then_inc(uT_psum, 1)

            def route(T):
                pe.wait_ge(uT_ready, T + 1)
                if at_least(T, 1):
                    pe.wait_ge(lg_ready, T)
                for c in range(KC):
                    i = nc.tensor.matmul(psR[:, 0:P], w_r[:, c, :], uT[:, c, :], start=c == 0, stop=c == KC - 1)
                i.then_inc(r_psum, 1)

            def l_turn(T):
                pe.wait_ge(lg_ready, T + 1)
                if at_least(T, 1):
                    pe.wait_ge(l_ready, T)
                nc.tensor.transpose(psL[:, 0:P], lg[:, :], ident[:, :]).then_inc(l_psum, 1)

            pe.wait_ge(small_loaded, 16 * 5)
            o_turn(0, 0, first=True)
            o_turn(1, 1)
            pe.wait_ge(w_lo_ready, 2)

            def body(T, j, s):
                if at_least(T, 3):
                    l_turn(T - 3)
                y_of(T, s)
                if at_least(T, 1):
                    u_turn(T - 1, 1 - s)
                if below(T, N - 2):
                    o_turn(T + 2, s)
                if at_least(T, 1):
                    route(T - 1)

            over_tiles(pe, body)
            l_turn(N - 3)
            u_turn(N - 1, 1)
            l_turn(N - 2)
            route(N - 1)
            l_turn(N - 1)


EXPERT_AT, NEW_AT, TARGET_AT, SLOT_AT, PAIRS_AT, STORED_AT = [k * BLOCKS for k in range(5)] + [4 * BLOCKS + 1]
WS = 4


def stage_route(nc, t, logits, picks, eb, idx):
    with ExitStack() as ctx:
        def sb(name, shape, dt=F32):
            return ctx.enter_context(nc.sbuf_tensor("r_" + name, shape, dt))

        def sem(name):
            return ctx.enter_context(nc.semaphore("r_" + name))

        NR = G + E
        N = TILES
        HN = N // 2
        prio = sb("prio", [P, EPG])
        tri = sb("tri", [P, P])
        ones = sb("ones", [P, P])
        tok = sb("tok", [P, N])
        cols = sb("cols", [P, P])
        first_slot = sb("first_slot", [1, BLOCKS])
        gm = sb("gm", [P, N])
        gd = sb("gd", [P, N, G])
        ge = sb("ge", [P, N, G])
        gsum = sb("gsum", [P, N])
        pg = sb("pg", [P, N])
        eqg = sb("eqg", [P, N, G])
        top = sb("top", [P, N])
        ohg = sb("ohg", [P, N, G])
        wide = sb("wide", [P, N, G, EPG])
        le = sb("le", [P, N, EPG])
        le2 = sb("le2", [P, N, EPG])
        m1 = sb("m1", [P, N])
        m2 = sb("m2", [P, N])
        eq = sb("eq", [P, N, EPG])
        oh1 = sb("oh1", [P, N, EPG])
        oh2 = sb("oh2", [P, N, EPG])
        md = sb("md", [P, N])
        e2 = sb("e2", [P, N])
        den = sb("den", [P, N])
        pick1 = sb("pick1", [P, N, G, EPG])
        pick2 = sb("pick2", [P, N, G, EPG])
        both = sb("both", [P, N * E])
        total = sb("total", [P, N * E])
        before = sb("before", [P, N + 1, E])
        cnt_i = sb("cnt_i", [P, E], I32)
        padded = sb("padded", [P, E])
        ends = sb("ends", [P, E])
        starts = sb("starts", [P, E])
        base = sb("base", [P, N * E])
        slot_f = sb("slot_f", [P, 2, N])
        slot_i = sb("slot_i", [P, 2, N], I32)
        blk_i = sb("blk_i", [P, 2, N], I32)
        blk_f = sb("blk_f", [P, 2, N])
        row_f = sb("row_f", [P, 2, N])
        in_row = sb("in_row", [P, 2, N, P])
        in_blk = sb("in_blk", [P, 2, N, BLOCKS])
        cmp = sb("cmp", [1, BLOCKS, E])
        eb_f = sb("eb_f", [1, BLOCKS])
        new_f = sb("new_f", [1, BLOCKS])
        cnt_f = sb("cnt_f", [1, BLOCKS])
        ones_b = sb("ones_b", [1, BLOCKS])
        ord_i = sb("ord_i", [1, BLOCKS], I32)
        live_i = sb("live_i", [1, 1], I32)

        psR = ctx.enter_context(nc.psum_tensor("r_psR", [P, 2, 512], F32))
        psT = ctx.enter_context(nc.psum_tensor("r_psT", [P, 2, 512], F32))
        psI = ctx.enter_context(nc.psum_tensor("r_psI", [P, 512], F32))

        loaded = sem("loaded")
        gd_ready, ge_ready, md_ready, e2_ready = sem("gd_ready"), sem("ge_ready"), sem("md_ready"), sem("e2_ready")
        both_ready, ranks, places_ready, idx_psum = sem("both_ready"), sem("ranks"), sem("places_ready"), sem("idx_psum")

        block = ctx.enter_context(nc.Block())

        @block.sync
        def _(sp):
            for dst, src in ((prio, "prio"), (tri, "tri"), (tok, "tok"), (cols, "cols"), (first_slot, "first_slot")):
                sp.dma_start(dst[:, :], t[src]).then_inc(loaded, 16)

        @block.scalar
        def _(act):
            act.wait_ge(gd_ready, 1)
            nc.scalar.activation(ge[:, :, :], gd[:, :, :], ACT.Exp).then_inc(ge_ready, 1)
            act.wait_ge(md_ready, 1)
            nc.scalar.activation(e2[:, :], md[:, :], ACT.Exp).then_inc(e2_ready, 1)

        @block.tensor
        def _(pe):
            pe.wait_ge(both_ready, 1)
            pe.wait_ge(loaded, 16 * 5)
            for h in range(2):
                part = slice(h * HN * E, (h + 1) * HN * E)
                nc.tensor.matmul(psR[:, h, 0:HN * E], tri[:, :], both[:, part], start=True, stop=True)
                i = nc.tensor.matmul(psT[:, h, 0:HN * E], ones[:, :], both[:, part], start=True, stop=True)
            i.then_inc(ranks, 1)
            for k in range(2):
                for h in range(2):
                    pe.wait_ge(places_ready, 2 * k + h + 1)
                    for n in range(h * HN, (h + 1) * HN):
                        i = nc.tensor.matmul(psI[:, 0:BLOCKS], in_row[:, k, n, :], in_blk[:, k, n, :],
                                             start=k == 0 and n == 0, stop=k == 1 and n == N - 1)
            i.then_inc(idx_psum, 1)

        @block.vector
        def _(dve):
            def over(ap, n):
                return ap.unsqueeze(2).broadcast_to([P, N, n])

            def tt(out, a, b, op):
                i = nc.vector.tensor_tensor(out, a, b, op)
                dve.drain()
                return i

            def red(out, a, op):
                nc.vector.tensor_reduce(out, a, AX.X, op)
                dve.drain()

            L3 = logits[:, :].rearrange("p (n r) -> p n r", r=NR)
            lg = L3[:, :, 0:G]
            nc.vector.memset(ones[:, :], 1.0)
            nc.vector.memset(ones_b[:, :], 1.0)
            nc.vector.memset(before[:, 0, :], 0.0)
            dve.drain()
            dve.wait_ge(loaded, 16 * 5)

            def first_max(onehot, hits, val, m, n):
                tt(hits, val, over(m, n), ALU.is_equal)
                tt(hits, hits, prio[:, EPG - n:EPG].unsqueeze(1).broadcast_to([P, N, n]), ALU.mult)
                red(top[:, :], hits, ALU.max)
                tt(onehot, hits, over(top[:, :], n), ALU.is_equal)

            red(gm[:, :], lg, ALU.max)
            nc.vector.tensor_tensor(gd[:, :, :], lg, over(gm[:, :], G), ALU.subtract).then_inc(gd_ready, 1)
            first_max(ohg[:, :, :], eqg[:, :, :], lg, gm[:, :], G)
            dve.wait_ge(ge_ready, 1)
            red(gsum[:, :], ge[:, :, :], ALU.add)
            nc.vector.reciprocal(pg[:, :], gsum[:, :])

            for g in range(G):
                tt(wide[:, :, g, :], L3[:, :, G + g * EPG:G + (g + 1) * EPG],
                   ohg[:, :, g:g + 1].broadcast_to([P, N, EPG]), ALU.mult)
            tt(le[:, :, :], wide[:, :, 0, :], wide[:, :, 1, :], ALU.add)
            tt(le2[:, :, :], wide[:, :, 2, :], wide[:, :, 3, :], ALU.add)
            tt(le[:, :, :], le[:, :, :], le2[:, :, :], ALU.add)
            red(m1[:, :], le[:, :, :], ALU.max)
            first_max(oh1[:, :, :], eq[:, :, :], le[:, :, :], m1[:, :], EPG)
            nc.vector.scalar_tensor_tensor(le2[:, :, :], oh1[:, :, :], -3.0e38, le[:, :, :], ALU.mult, ALU.add)
            dve.drain()
            red(m2[:, :], le2[:, :, :], ALU.max)
            first_max(oh2[:, :, :], eq[:, :, :], le2[:, :, :], m2[:, :], EPG)

            tt(md[:, :], m2[:, :], m1[:, :], ALU.subtract)
            dve.drain().then_inc(md_ready, 1)
            dve.wait_ge(e2_ready, 1)
            nc.vector.tensor_scalar(den[:, :], e2[:, :], 1.0, None, ALU.add)
            dve.drain()
            nc.vector.reciprocal(den[:, :], den[:, :])
            dve.drain()
            gate = picks[:, :].rearrange("p (n k) -> p n k", k=4)
            tt(gate[:, :, 2], pg[:, :], den[:, :], ALU.mult)
            tt(gate[:, :, 3], gate[:, :, 2], e2[:, :], ALU.mult)

            for g in range(G):
                og = ohg[:, :, g:g + 1].broadcast_to([P, N, EPG])
                nc.vector.tensor_tensor(pick1[:, :, g, :], oh1[:, :, :], og, ALU.mult)
                nc.vector.tensor_tensor(pick2[:, :, g, :], oh2[:, :, :], og, ALU.mult)
            dve.drain()
            flat = "p n g e -> p (n g e)"
            tt(both[:, :], pick1[:, :, :, :].rearrange(flat), pick2[:, :, :, :].rearrange(flat), ALU.add)
            dve.drain().then_inc(both_ready, 1)

            dve.wait_ge(ranks, 1)
            for h in range(2):
                nc.vector.tensor_copy(total[:, h * HN * E:(h + 1) * HN * E], psT[:, h, 0:HN * E])
            dve.drain()
            for n in range(N):
                tt(before[:, n + 1, :], before[:, n, :], total[:, n * E:(n + 1) * E], ALU.add)

            nc.vector.tensor_scalar(cnt_i[:, :], before[:, N, :], float(P - 1), None, ALU.add)
            dve.drain()
            nc.vector.tensor_scalar(cnt_i[:, :], cnt_i[:, :], 7, 7, ALU.arith_shift_right, ALU.logical_shift_left)
            dve.drain()
            nc.vector.tensor_copy(padded[:, :], cnt_i[:, :])
            dve.drain()
            nc.vector.tensor_tensor_scan(ends[:, :], ones[:, 0:E], padded[:, :], 0.0, ALU.mult, ALU.add)
            dve.drain()
            tt(starts[:, :], ends[:, :], padded[:, :], ALU.subtract)

            for h in range(2):
                part = slice(h * HN * E, (h + 1) * HN * E)
                nc.vector.tensor_tensor(base[:, part], psR[:, h, 0:HN * E],
                                        before[:, h * HN:(h + 1) * HN, :].rearrange("p n e -> p (n e)"), ALU.add)
            dve.drain()
            b3 = base[:, :].rearrange("p (n e) -> p n e", e=E)
            tt(b3, b3, starts[:, :].unsqueeze(1).broadcast_to([P, N, E]), ALU.add)
            for k, pick in enumerate((pick1, pick2)):
                tt(both[:, :], pick[:, :, :, :].rearrange(flat), base[:, :], ALU.mult)
                red(slot_f[:, k, :], both[:, :].rearrange("p (n e) -> p n e", e=E), ALU.add)
                nc.vector.tensor_copy(gate[:, :, k].bitcast(U32), slot_f[:, k, :])
            nc.vector.tensor_copy(slot_i[:, :, :], slot_f[:, :, :])
            dve.drain()
            nc.vector.tensor_scalar(blk_i[:, :, :], slot_i[:, :, :], 7, None, ALU.arith_shift_right)
            dve.drain()
            nc.vector.tensor_copy(blk_f[:, :, :], blk_i[:, :, :])
            dve.drain()
            nc.vector.scalar_tensor_tensor(row_f[:, :, :], blk_f[:, :, :], -float(P), slot_f[:, :, :], ALU.mult, ALU.add)
            dve.drain()
            for k in range(2):
                for h in range(2):
                    part = slice(h * HN, (h + 1) * HN)
                    nc.vector.tensor_tensor(in_blk[:, k, part, :], cols[:, 0:BLOCKS].unsqueeze(1).broadcast_to([P, HN, BLOCKS]),
                                            blk_f[:, k, part].unsqueeze(2).broadcast_to([P, HN, BLOCKS]), ALU.is_equal)
                    nc.vector.tensor_tensor(in_row[:, k, part, :], cols[:, :].unsqueeze(1).broadcast_to([P, HN, P]),
                                            row_f[:, k, part].unsqueeze(2).broadcast_to([P, HN, P]), ALU.is_equal)
                    dve.drain()
                    nc.vector.tensor_tensor(in_blk[:, k, part, :], in_blk[:, k, part, :],
                                            tok[:, part].unsqueeze(2).broadcast_to([P, HN, BLOCKS]),
                                            ALU.mult).then_inc(places_ready, 1)

            tt(cmp[:, :, :], ends[0:1, :].unsqueeze(1).broadcast_to([1, BLOCKS, E]),
               first_slot[0:1, :].unsqueeze(2).broadcast_to([1, BLOCKS, E]), ALU.is_le)
            red(eb_f[:, :], cmp[:, :, :], ALU.add)
            nc.vector.tensor_scalar(eb_f[:, :], eb_f[:, :], float(E - 1), None, ALU.min)
            dve.drain()
            nc.vector.tensor_copy(eb[:, EXPERT_AT:EXPERT_AT + BLOCKS], eb_f[:, :])
            nc.vector.memset(new_f[:, 0:1], 1.0)
            tt(new_f[:, 1:], eb_f[:, 1:], eb_f[:, :BLOCKS - 1], ALU.not_equal)
            nc.vector.tensor_copy(eb[:, NEW_AT:NEW_AT + BLOCKS], new_f[:, :])
            nc.vector.tensor_tensor_scan(cnt_f[:, :], ones_b[:, :], new_f[:, :], 0.0, ALU.mult, ALU.add)
            dve.drain()
            nc.vector.tensor_scalar(eb[:, TARGET_AT:TARGET_AT + BLOCKS], cnt_f[:, :], 48.0, None, ALU.mult)
            nc.vector.tensor_copy(ord_i[:, :], cnt_f[:, :])
            dve.drain()
            nc.vector.tensor_scalar(eb[:, SLOT_AT:SLOT_AT + BLOCKS], ord_i[:, :], WS - 1, None, ALU.bitwise_and)
            nc.vector.tensor_scalar(live_i[:, :], ends[0:1, E - 1:E], float(2 * P - 1), None, ALU.add)
            dve.drain()
            nc.vector.tensor_scalar(live_i[:, :], live_i[:, :], 8, None, ALU.arith_shift_right)
            dve.drain()
            nc.vector.tensor_copy(eb[:, PAIRS_AT:PAIRS_AT + 1], live_i[:, :])
            nc.vector.tensor_scalar(eb[:, STORED_AT:STORED_AT + 1], live_i[:, :], 16.0, 16.0, ALU.mult, ALU.add)
            dve.wait_ge(idx_psum, 1)
            nc.vector.tensor_copy(idx[:, :], psI[:, 0:BLOCKS])
            dve.drain()


def stage_experts(nc, t, eb, idx):
    with ExitStack() as ctx:
        def sb(name, shape, dt=F32):
            return ctx.enter_context(nc.sbuf_tensor("e_" + name, shape, dt))

        def ps(name, shape):
            return ctx.enter_context(nc.psum_tensor("e_" + name, shape, F32))

        def sem(name):
            return ctx.enter_context(nc.semaphore("e_" + name))

        HC = DE // P
        HK = KC // 2
        ident = sb("ident", [P, P])
        w_gu = sb("w_gu", [P, WS * KC, 2 * DE])
        w_dn = sb("w_dn", [P, WS * HC, D])
        cur = sb("cur", [P, 2], U32)
        x = [sb(f"x{s}", [P, D]) for s in range(2)]
        xT = sb("xT", [P, KC - HK, P])
        xT_hi, xT_lo = sb("xT_hi", [P, HK, P], F32R), sb("xT_lo", [P, HK, P], F32R)
        wg_hi, wg_lo = sb("wg_hi", [P, HK, 2 * DE], F32R), sb("wg_lo", [P, HK, 2 * DE], F32R)
        act_g = sb("act_g", [P, DE])
        hid = sb("hid", [P, 2, DE])
        hT_hi, hT_lo = sb("hT_hi", [P, HC, P], F32R), sb("hT_lo", [P, HC, P], F32R)
        wd_hi, wd_lo = sb("wd_hi", [P, 2 * HC, D], F32R), sb("wd_lo", [P, 2 * HC, D], F32R)
        y = sb("y", [P, 2, D])

        psX = ps("psX", [P, 2, 512])
        psG = ps("psG", [P, 2, 512])
        psH = ps("psH", [P, 512])
        psY = ps("psY", [P, 2, 512])

        ident_loaded = sem("ident_loaded")
        w_loaded, w_ready = sem("w_loaded"), sem("w_ready")
        x_loaded = [sem("x_loaded0"), sem("x_loaded1")]
        cur_ready = sem("cur_ready")
        xT_psum, xT_ready = sem("xT_psum"), sem("xT_ready")
        g_psum, silu_ready, hid_ready = sem("g_psum"), sem("silu_ready"), sem("hid_ready")
        hT_psum, hT_rounded, hT_ready = sem("hT_psum"), sem("hT_rounded"), sem("hT_ready")
        wd_rounded, wd_ready = sem("wd_rounded"), sem("wd_ready")
        wg_rounded, wg_ready = sem("wg_rounded"), sem("wg_ready")
        xT_rounded, xT_rest_ready = sem("xT_rounded"), sem("xT_rest_ready")
        y_psum, y_ready = sem("y_psum"), sem("y_ready")
        y_stored = [sem("y_stored0"), sem("y_stored1")]
        carrier = sem("carrier")

        block = ctx.enter_context(nc.Block())

        def over_blocks(engine, body):
            pairs = engine.value_load(eb[0:1, PAIRS_AT:PAIRS_AT + 1], min_val=1, max_val=BLOCKS // 2)
            for s in range(2):
                body(s, 0, s)
            with engine.Fori(1, BLOCKS // 2 - 1) as j:
                with engine.If(j < pairs):
                    for s in range(2):
                        body(2 * j + s, j, s)
            with engine.If(pairs > BLOCKS // 2 - 1):
                for s in range(2):
                    body(BLOCKS - 2 + s, BLOCKS // 2 - 1, s)
            return pairs

        def is_last(b):
            return isinstance(b, int) and b == BLOCKS - 1

        @block.sync
        def _(sp):
            sp.dma_start(ident[:, :], t["ident"]).then_inc(ident_loaded, 16)
            sp.sem_inc(y_psum, WS)

            def body(b, j, s):
                new = sp.value_load(eb[0:1, bass.ds(b + NEW_AT, 1)], min_val=0, max_val=1)
                with sp.If(new > 0):
                    e = sp.value_load(eb[0:1, bass.ds(b + EXPERT_AT, 1)], min_val=0, max_val=E - 1)
                    w = sp.value_load(eb[0:1, bass.ds(b + SLOT_AT, 1)], min_val=0, max_val=WS - 1)
                    target = sp.value_load(eb[0:1, bass.ds(b + TARGET_AT, 1)], min_val=48, max_val=48 * E)
                    sp.wait_ge(y_psum, b + 1)
                    for k, name in enumerate(("w_gate", "w_up")):
                        sp.dma_start(w_gu[:, bass.ds(w * KC, KC), k * DE:(k + 1) * DE],
                                     t[name][bass.ds(e * D, D), :].rearrange("(p c) n -> p c n", c=KC)).then_inc(w_loaded, 16)
                    sp.dma_start(w_dn[:, bass.ds(w * HC, HC), :],
                                 t["w_down"][bass.ds(e * DE, DE), :].rearrange("(p c) n -> p c n", c=HC)).then_inc(w_loaded, 16)
                    sp.wait_ge(w_loaded, target)
                    sp.sem_inc(carrier, 1)
                sp.sem_inc(w_ready, 1)

            over_blocks(sp, body)
            final = sp.value_load(eb[0:1, STORED_AT:STORED_AT + 1], min_val=32, max_val=16 * (BLOCKS // 2) + 16)
            for s in range(2):
                sp.wait_ge(y_stored[s], final)
                sp.sem_inc(carrier, 1)

        @block.gpsimd
        def _(pool):
            pool.sem_inc(xT_psum, 2)

            def body(b, j, s):
                pool.wait_ge(xT_psum, b + 1)
                nc.gpsimd.tensor_copy(cur[:, s:s + 1], idx[:, bass.ds(b, 1)]).then_inc(cur_ready, 1)
                pool.wait_ge(ident_loaded, 16)
                pool.wait_ge(cur_ready, b + 1)
                pool.indirect_dma_start(x[s][:, :], None, t["U2"],
                                        bass.IndirectOffsetOnAxis(cur[:, s:s + 1], 0)).then_inc(x_loaded[s], 16)
                pool.wait_ge(x_loaded[s], 16 * j + 16)

            pairs = pool.value_load(eb[0:1, PAIRS_AT:PAIRS_AT + 1], min_val=1, max_val=BLOCKS // 2)
            with pool.Fori(0, BLOCKS // 2) as j:
                with pool.If(j < pairs + 1):
                    body(2 * j, j, 0)
                with pool.If(j < pairs):
                    body(2 * j + 1, j, 1)

        @block.scalar
        def _(act):
            for s in range(2):
                act.sem_inc(y_stored[s], 16)

            def wg_round(b):
                w = act.value_load(eb[0:1, bass.ds(b + SLOT_AT, 1)], min_val=0, max_val=WS - 1)
                act.wait_ge(w_ready, b + 1)
                nc.scalar.activation(wg_hi[:, :, :], w_gu[:, bass.ds(w * KC, HK), :], ACT.Copy).then_inc(wg_rounded, 1)

            def xT_round(b):
                act.wait_ge(xT_psum, b + 3)
                nc.scalar.activation(xT_hi[:, :, :], psX[:, 0, :].rearrange("p (c n) -> p c n", n=P), ACT.Copy).then_inc(xT_rounded, 1)

            def hT_round(b):
                act.wait_ge(hT_psum, b + 1)
                nc.scalar.activation(hT_hi[:, :, :], psH[:, 0:DE].rearrange("p (c n) -> p c n", n=P), ACT.Copy).then_inc(hT_rounded, 1)

            def wd_round(b, s):
                w = act.value_load(eb[0:1, bass.ds(b + SLOT_AT, 1)], min_val=0, max_val=WS - 1)
                act.wait_ge(w_ready, b + 1)
                nc.scalar.activation(wd_hi[:, s * HC:(s + 1) * HC, :], w_dn[:, bass.ds(w * HC, HC), :], ACT.Copy).then_inc(wd_rounded, 1)

            def y_out(b, j, s):
                act.wait_ge(y_psum, b + 1 + WS)
                act.wait_ge(y_stored[s], 16 * j + 16)
                nc.scalar.activation(y[:, s, :], psY[:, :, :].rearrange("p b n -> p (b n)"), ACT.Copy).then_inc(y_ready, 1)
                act.wait_ge(y_ready, b + 2)
                act.dma_start(t["Y"][bass.ds(b * P, P), :], y[:, s, :]).then_inc(y_stored[s], 16)

            def body(b, j, s):
                wg_round(b)
                xT_round(b)
                if not isinstance(b, int) or b > 1:
                    y_out(b - 2, j - 1, s)
                wd_round(b, s)
                if not isinstance(b, int) or b > 0:
                    hT_round(b - 1)
                act.wait_ge(g_psum, b + 1)
                act.wait_ge(hid_ready, b + 1)
                nc.scalar.activation(act_g[:, :], psG[:, s, 0:DE], ACT.Silu).then_inc(silu_ready, 1)

            act.sem_inc(hid_ready, 1)
            pairs = over_blocks(act, body)
            y_out(2 * pairs - 2, pairs - 1, 0)
            hT_round(2 * pairs - 1)
            y_out(2 * pairs - 1, pairs - 1, 1)

        @block.vector
        def _(dve):
            def xT_out(b):
                dve.wait_ge(xT_psum, b + 3)
                nc.vector.tensor_copy(xT[:, :, :], psX[:, 1, :].rearrange("p (c n) -> p c n", n=P)).then_inc(xT_ready, 1)
                dve.wait_ge(xT_rounded, b + 1)
                nc.vector.tensor_tensor(xT_lo[:, :, :], psX[:, 0, :].rearrange("p (c n) -> p c n", n=P),
                                        xT_hi[:, :, :].bitcast(F32), ALU.subtract).then_inc(xT_rest_ready, 1)

            def wg_rest(b):
                w = dve.value_load(eb[0:1, bass.ds(b + SLOT_AT, 1)], min_val=0, max_val=WS - 1)
                dve.wait_ge(wg_rounded, b + 1)
                nc.vector.tensor_tensor(wg_lo[:, :, :], w_gu[:, bass.ds(w * KC, HK), :], wg_hi[:, :, :].bitcast(F32),
                                        ALU.subtract).then_inc(wg_ready, 1)

            def hT_out(b):
                dve.wait_ge(hT_rounded, b + 1)
                nc.vector.tensor_tensor(hT_lo[:, :, :], psH[:, 0:DE].rearrange("p (c n) -> p c n", n=P),
                                        hT_hi[:, :, :].bitcast(F32), ALU.subtract).then_inc(hT_ready, 1)

            def wd_rest(b, s):
                w = dve.value_load(eb[0:1, bass.ds(b + SLOT_AT, 1)], min_val=0, max_val=WS - 1)
                dve.wait_ge(wd_rounded, b + 1)
                c = slice(s * HC, (s + 1) * HC)
                nc.vector.tensor_tensor(wd_lo[:, c, :], w_dn[:, bass.ds(w * HC, HC), :], wd_hi[:, c, :].bitcast(F32),
                                        ALU.subtract).then_inc(wd_ready, 1)

            def body(b, j, s):
                xT_out(b)
                wg_rest(b)
                wd_rest(b, s)
                if not isinstance(b, int) or b > 0:
                    hT_out(b - 1)
                dve.wait_ge(silu_ready, b + 1)
                nc.vector.tensor_tensor(hid[:, s, :], act_g[:, :], psG[:, s, DE:2 * DE], ALU.mult).then_inc(hid_ready, 1)

            pairs = over_blocks(dve, body)
            hT_out(2 * pairs - 1)

        @block.tensor
        def _(pe):
            def x_turn(b, n, s):
                pe.wait_ge(x_loaded[s], 16 * n + 16)
                pe.wait_ge(xT_ready, b + 1)
                xv = x[s][:, :].rearrange("p (m c) -> p c m", c=KC)
                for c in range(KC):
                    i = nc.tensor.transpose(psX[:, c // 4, (c % 4) * P:(c % 4) * P + P], xv[:, c, :], ident[:, :])
                i.then_inc(xT_psum, 1)

            def hid_turn(b, s):
                pe.wait_ge(hid_ready, b + 2)
                hv = hid[:, s, :].rearrange("p (m c) -> p c m", c=HC)
                for c in range(HC):
                    i = nc.tensor.transpose(psH[:, c * P:(c + 1) * P], hv[:, c, :], ident[:, :])
                i.then_inc(hT_psum, 1)

            def down(b, s):
                pe.wait_ge(wd_ready, b + 1)
                pe.wait_ge(hT_ready, b + 1)
                pe.wait_ge(y_ready, b + 1)
                for h in range(2):
                    n = 0
                    for c in range(HC):
                        for a, w in ((hT_hi, wd_hi), (hT_hi, wd_lo), (hT_lo, wd_hi)):
                            i = nc.tensor.matmul(psY[:, h, :], a[:, c, :], w[:, s * HC + c, h * 512:(h + 1) * 512],
                                                 start=n == 0, stop=n == 3 * HC - 1)
                            n += 1
                i.then_inc(y_psum, 1)

            def body(b, j, s):
                w = pe.value_load(eb[0:1, bass.ds(b + SLOT_AT, 1)], min_val=0, max_val=WS - 1)
                pe.wait_ge(w_ready, b + 1)
                pe.wait_ge(xT_ready, b + 2)
                for c in range(HK, KC):
                    nc.tensor.matmul(psG[:, s, :], xT[:, c - HK, :], w_gu[:, bass.ds(w * KC + c, 1), :].rearrange("p o n -> p (o n)"), start=c == HK, stop=False)
                pe.wait_ge(xT_rest_ready, b + 1)
                pe.wait_ge(wg_ready, b + 1)
                for c in range(HK):
                    for a, ww in ((xT_hi, wg_hi), (xT_hi, wg_lo), (xT_lo, wg_hi)):
                        i = nc.tensor.matmul(psG[:, s, :], a[:, c, :], ww[:, c, :], start=False,
                                             stop=c == HK - 1 and ww is wg_hi and a is xT_lo)
                i.then_inc(g_psum, 1)
                some_before = not isinstance(b, int) or b > 0
                if some_before:
                    hid_turn(b - 1, 1 - s)
                if not is_last(b):
                    x_turn(b + 1, j + s, 1 - s)
                if some_before:
                    down(b - 1, 1 - s)

            pe.sem_inc(xT_ready, 1)
            pe.sem_inc(y_ready, 1)
            pe.wait_ge(ident_loaded, 16)
            x_turn(0, 0, 0)
            pairs = over_blocks(pe, body)
            hid_turn(2 * pairs - 1, 1)
            down(2 * pairs - 1, 1)


def stage_combine(nc, t, picks):
    with ExitStack() as ctx:
        def sb(name, shape, dt=F32):
            return ctx.enter_context(nc.sbuf_tensor("f_" + name, shape, dt))

        def sem(name):
            return ctx.enter_context(nc.semaphore("f_" + name))

        N = TILES
        g_fin = sb("g_fin", [P, D])
        eps = sb("eps", [P, 1])
        cur = sb("cur", [P, 2, 4])
        ya = [sb(f"ya{s}", [P, D]) for s in range(2)]
        yb = [sb(f"yb{s}", [P, D]) for s in range(2)]
        h = sb("h", [P, 2, D])
        acc = sb("acc", [P, 2, D])
        junk = sb("junk", [P, D])
        ss, std, rs = sb("ss", [P, 2]), sb("std", [P, 2]), sb("rs", [P, 2])
        res = sb("res", [P, 2, D])

        g_loaded, eps_ready, cur_ready = sem("g_loaded"), sem("eps_ready"), sem("cur_ready")
        y_loaded = [sem("y_loaded0"), sem("y_loaded1")]
        h_loaded = [sem("h_loaded0"), sem("h_loaded1")]
        sum_ready, std_ready, res_ready = sem("sum_ready"), sem("std_ready"), sem("res_ready")
        res_stored = [sem("res_stored0"), sem("res_stored1")]

        block = ctx.enter_context(nc.Block())

        def over_tiles(engine, body):
            with engine.Fori(0, N // 2 - 1) as j:
                for s in range(2):
                    body(2 * j + s, j, s)
            for s in range(2):
                body(N - 2 + s, N // 2 - 1, s)

        def is_last(T):
            return isinstance(T, int) and T == N - 1

        @block.sync
        def _(sp):
            sp.dma_start(g_fin[:, :], t["g_fin"]).then_inc(g_loaded, 16)
            sp.sem_inc(sum_ready, 2)

            def body(T, j, s):
                sp.wait_ge(sum_ready, T + 1)
                sp.dma_start(h[:, s, :], t["H2"][bass.ds(T * P, P), :]).then_inc(h_loaded[s], 16)

            over_tiles(sp, body)

        @block.gpsimd
        def _(pool):
            def body(T, j, s):
                pool.wait_ge(sum_ready, T + 1)
                nc.gpsimd.tensor_copy(cur[:, s, :].bitcast(U32),
                                      picks[:, bass.ds(T * 4, 4)].bitcast(U32)).then_inc(cur_ready, 1)
                pool.wait_ge(g_loaded, 16)
                pool.wait_ge(cur_ready, T + 1)
                for k, y in enumerate((ya, yb)):
                    pool.indirect_dma_start(y[s][:, :], None, t["Y"],
                                            bass.IndirectOffsetOnAxis(cur[:, s, k:k + 1].bitcast(U32), 0)).then_inc(y_loaded[s], 16)

            over_tiles(pool, body)

        @block.vector
        def _(dve):
            def sum_of(T, j, s):
                dve.drain()
                dve.wait_ge(y_loaded[s], 32 * j + 32)
                dve.wait_ge(h_loaded[s], 16 * j + 16)
                dve.wait_ge(cur_ready, T + 1)
                nc.vector.scalar_tensor_tensor(acc[:, s, :], ya[s][:, :], cur[:, s, 2:3], h[:, s, :], ALU.mult, ALU.add)
                dve.drain()
                nc.vector.scalar_tensor_tensor(acc[:, s, :], yb[s][:, :], cur[:, s, 3:4], acc[:, s, :],
                                               ALU.mult, ALU.add).then_inc(sum_ready, 1)

            nc.vector.memset(eps[:, :], EPS).then_inc(eps_ready, 1)
            dve.wait_ge(g_loaded, 16)
            for s in range(2):
                dve.sem_inc(res_stored[s], 16)
            sum_of(0, 0, 0)

            def body(T, j, s):
                if not is_last(T):
                    sum_of(T + 1, j + s, 1 - s)
                dve.wait_ge(std_ready, T + 1)
                nc.vector.reciprocal(rs[:, s:s + 1], std[:, s:s + 1])
                dve.drain()
                dve.wait_ge(res_stored[s], 16 * j + 16)
                nc.vector.scalar_tensor_tensor(res[:, s, :], acc[:, s, :], rs[:, s:s + 1], g_fin[:, :],
                                               ALU.mult, ALU.mult).then_inc(res_ready, 1)

            over_tiles(dve, body)

        @block.scalar
        def _(act):
            def stats(T, s):
                act.drain()
                act.wait_ge(sum_ready, T + 3)
                nc.scalar.activation(junk[:, :], acc[:, s, :], ACT.Square, accum_out=ss[:, s:s + 1])
                act.drain()
                nc.scalar.activation(std[:, s:s + 1], ss[:, s:s + 1], ACT.Sqrt, scale=1.0 / D,
                                     bias=eps[:, 0:1]).then_inc(std_ready, 1)

            act.wait_ge(eps_ready, 1)
            stats(0, 0)

            def body(T, j, s):
                if not is_last(T):
                    stats(T + 1, 1 - s)
                act.wait_ge(res_ready, T + 1)
                act.dma_start(t["out"][bass.ds(T * P, P), :], res[:, s, :]).then_inc(res_stored[s], 16)

            over_tiles(act, body)
            for s in range(2):
                act.wait_ge(res_stored[s], 16 * (N // 2) + 16)


def hymba_trunk(nc, t):
    for name, (shape, dt) in SCRATCH.items():
        t[name] = nc.dram_tensor(name, shape, dt).ap()
    stage_project(nc, t)
    stage_attend(nc, t)
    with ExitStack() as ctx:
        logits = ctx.enter_context(nc.sbuf_tensor("logits", [P, TILES * (G + E)], F32))
        picks = ctx.enter_context(nc.sbuf_tensor("picks", [P, TILES * 4], F32))
        eb = ctx.enter_context(nc.sbuf_tensor("eb", [1, 4 * BLOCKS + 2], I32))
        idx = ctx.enter_context(nc.sbuf_tensor("idx", [P, BLOCKS], I32))
        stage_mix_out(nc, t, logits)
        stage_route(nc, t, logits, picks, eb, idx)
        stage_experts(nc, t, eb, idx)
        stage_combine(nc, t, picks)


def layouts(i):
    f = np.float32
    c = np.ascontiguousarray
    sw = np.arange(GD).reshape(-1, 2)[:, ::-1].ravel()
    rows = lambda a: np.broadcast_to(a, (P,) + a.shape)
    meta = np.zeros((P, D), f)
    meta[:META] = i["meta_tokens"]
    xall = np.concatenate([meta, i["x_prompt"][0], i["x_sample"][0]])
    gq, gk = i["gqa_q_norm_g"][0], i["gqa_k_norm_g"][0]
    g_rows = rows(np.stack([gq, gq[sw], gk, gk[sw]]))
    qup = i["w_mla_q_up"][0].reshape(QR, MH, QKD)
    qup = np.concatenate([qup[:, :, :ND].reshape(QR, -1), qup[:, :, ND:].reshape(QR, -1),
                          qup[:, :, ND:][:, :, sw[:RD]].reshape(QR, -1)], axis=1)
    kv = i["w_mla_kv_up"][0].reshape(KVR, MH, ND + VD)

    def angles(pr, pc, rot):
        half = rot // 2
        inv = (f(10000.0) ** (-np.arange(0, half, 2, dtype=f) / f(half))).astype(f)
        a = np.concatenate([pr[:, None] * inv, pc[:, None] * inv], axis=-1)
        co, si = np.cos(a).astype(f), np.sin(a).astype(f)
        return np.repeat(co, 2, axis=1), np.stack([-si, si], axis=2).reshape(len(pr), rot)

    n = np.arange(DEC_SEQ)
    pr = np.concatenate([np.full(P, -1), n[:SEQ] // 64, n // 64]).astype(f)
    pc = np.concatenate([np.arange(P), n[:SEQ] % 64, n % 64]).astype(f)
    cg, sg = angles(pr, pc, GD)
    cm, sm = angles(pr, pc, RD)
    rope_rows = np.concatenate([cg, sg, cm, sm], axis=1)
    pad = np.zeros((P, W - P), f)
    rope_cols = np.stack([np.concatenate([pad, np.tile(a.T * f(MSCALE), (P // RD, 1))], axis=1) for a in (cm, sm)])
    inv_n = np.broadcast_to(np.array([1 / GD] * 10 + [1 / QR, 1 / KVR], f), (P, 12))
    a = {
        "xall": xall, "rope_rows": rope_rows, "rope_cols": rope_cols, "ident": np.eye(P, dtype=f),
        "g_mix": i["norm_mix_g"][0].reshape(P, KC), "g_cq": i["mla_q_norm_g"][0].reshape(2, P).T,
        "g_ckv": i["mla_kv_norm_g"][0].reshape(P, 1), "g_rows": g_rows, "inv_n": inv_n,
        "w_in": i["w_in"][0], "w_qup": qup, "w_kup": kv[:, :, :ND].reshape(KVR, MH * ND),
        "w_vup": kv[:, :, ND:].reshape(KVR, MH * VD),
        "w_out": i["w_out"][0],
        "g_out": np.concatenate([i["gqa_out_norm_g"][0], i["mla_out_norm_g"][0]]).reshape(P, KC),
        "g_ffn": rows(i["norm_ffn_g"][0]),
        "g_fin": rows(i["norm_final_g"]),
        "w_gate": i["w_expert_gate"][0].reshape(E * D, DE), "w_up": i["w_expert_up"][0].reshape(E * D, DE),
        "w_down": i["w_expert_down"][0].reshape(E * DE, D),
        "prio": rows(np.arange(EPG, 0, -1).astype(f)), "tri": np.triu(np.ones((P, P), f), 1),
        "tok": (np.arange(TILES)[None, :] * P + np.arange(P)[:, None]).astype(f), "cols": rows(np.arange(P).astype(f)),
        "first_slot": (np.arange(BLOCKS) * P).astype(f).reshape(1, BLOCKS),
        "w_r": np.concatenate([i["w_router_group"][0], i["w_router_expert"][0]], axis=1),
        "b_r": np.concatenate([i["b_router_group"][0], i["b_router_expert"][0]]).reshape(G + E, 1),
    }
    return {k: c(np.asarray(v)) for k, v in a.items()}


SCRATCH = {
    "QGH": ([GH * GD, TOK], F32), "QGL": ([GH * GD, TOK], F32),
    "QNH": ([MH * ND, TOK], F32), "QNL": ([MH * ND, TOK], F32),
    "QRH": ([MH * RD, TOK], F32), "QRL": ([MH * RD, TOK], F32),
    "KGH": ([PAIRS * GD, KEYS], F32), "KGL": ([PAIRS, GD + 1, KEYS], F32),
    "KMH": ([MH * ND, KEYS], F32), "KML": ([MH * ND, KEYS], F32),
    "KRH": ([RD + 1, KEYS], F32), "KRL": ([RD, KEYS], F32),
    "V": ([KEYS, NV * VC], F32),
    "MX": ([TOK], F32), "O": ([TOK, D], F32),
    "H2": ([TOK, D], F32), "U2": ([TOK, D], F32),
    "Y": ([P * BLOCKS, D], F32),
}


def kernel(**inputs):
    import concourse.bacc as bacc
    from concourse.bass_utils import run_bass_kernel_spmd

    nc = bacc.Bacc("TRN2", target_bir_lowering=False, num_devices=1)
    arrays = layouts({k: np.asarray(v) for k, v in inputs.items()})
    t = {n: nc.dram_tensor(n, a.shape, mybir.dt.from_np(a.dtype), kind="ExternalInput").ap()
         for n, a in arrays.items()}
    t["out"] = nc.dram_tensor("out", (TOK, D), F32, kind="ExternalOutput").ap()
    hymba_trunk(nc, t)
    out = run_bass_kernel_spmd(nc, [arrays], core_ids=[0]).results[0]["out"]
    return out[None, :SEQ], out[None, SEQ:]
```
